# Optimizing a Trainium2 kernel written in Bass

```python
import math
import jax, jax.numpy as jnp
from jax import lax
import numpy as np

D_MODEL = 1024
BATCH = 1
SEQ = 512
DEPTH = 1

CHUNK = 64
Q_BLOCK = 128
SB_HEADS = 8
SB_HEAD_DIM = 64
SB_WIDTH = SB_HEADS * SB_HEAD_DIM
SSM_WIDTH = D_MODEL // 2
SSM_GROUP = 16
SSM_GROUPS = SSM_WIDTH // SSM_GROUP
SSM_STATE = 64
DT_MIN = 1e-3
DT_MAX = 1e-1
FFN_HIDDEN = ((8 * D_MODEL // 3 + 255) // 256) * 256
IN_SPLITS = (SB_WIDTH, 2 * SB_WIDTH, 3 * SB_WIDTH, 3 * SB_WIDTH + SSM_WIDTH,
             3 * SB_WIDTH + SSM_WIDTH + D_MODEL)
IN_COLS = 3 * SB_WIDTH + SSM_WIDTH + 2 * D_MODEL
N_MOD = 6
DEEPNORM_ALPHA = (2 * DEPTH) ** 0.25
DEEPNORM_BETA = (8 * DEPTH) ** -0.25
LN_EPS = 1e-5


def _normalize(x):
    xf = x.astype(jnp.float32)
    mu = jnp.mean(xf, axis=-1, keepdims=True)
    var = jnp.mean(jnp.square(xf - mu), axis=-1, keepdims=True)
    return ((xf - mu) * lax.rsqrt(var + LN_EPS)).astype(x.dtype)

def _layer_norm(x, g, b):
    return _normalize(x) * g + b

def stick_breaking_attention(q, k, v):
    b, s, h, dh = q.shape
    nb = s // Q_BLOCK
    f32 = jnp.float32
    qb = q.astype(f32).reshape(b, nb, Q_BLOCK, h, dh).transpose(1, 0, 3, 2, 4)
    kt = k.astype(f32).transpose(0, 2, 1, 3)
    vt = v.astype(f32).transpose(0, 2, 1, 3)
    key_pos = jnp.arange(s, dtype=jnp.int32)
    scale = 1.0 / math.sqrt(dh)

    def one_block(args):
        q_blk, blk = args
        q_pos = blk * Q_BLOCK + jnp.arange(Q_BLOCK, dtype=jnp.int32)
        z = jnp.einsum('bhqd,bhkd->bhqk', q_blk, kt) * scale
        causal = key_pos[None, :] < q_pos[:, None]
        log_beta = jax.nn.log_sigmoid(z)
        log_one_minus = jnp.where(causal, log_beta - z, 0.0)
        after = lax.cumsum(log_one_minus, axis=3, reverse=True) - log_one_minus
        w = jnp.where(causal, jnp.exp(log_beta + after), 0.0)
        return jnp.einsum('bhqk,bhkd->bhqd', w, vt)

    out = lax.map(one_block, (qb, jnp.arange(nb, dtype=jnp.int32)))
    return out.transpose(1, 0, 3, 2, 4).reshape(b, s, h * dh).astype(v.dtype)

def s5_branch(u, a_re, a_im, log_dt, b_re, b_im, c_re, c_im, d_skip, w_glu, b_glu):
    f32 = jnp.float32
    c64 = jnp.complex64
    bsz, s, _ = u.shape
    n_chunks = s // CHUNK
    uf = u.astype(f32)
    lam = lax.complex(a_re.astype(f32), a_im.astype(f32))
    dt = jnp.exp(log_dt.astype(f32))[:, None]
    lam_dt = lam * dt
    lam_bar = jnp.exp(lam_dt)
    b_mat = lax.complex(b_re.astype(f32), b_im.astype(f32))
    b_bar = ((lam_bar - 1.0) / lam)[..., None] * b_mat
    c_mat = lax.complex(c_re.astype(f32), c_im.astype(f32))
    steps = jnp.arange(1, CHUNK + 1, dtype=f32)
    powers = jnp.exp(lam_dt[None] * steps[:, None, None].astype(c64))
    a_seq = jnp.broadcast_to(lam_bar[None, None], (CHUNK, bsz, SSM_GROUPS, SSM_STATE))

    u_chunks = uf.reshape(bsz, n_chunks, CHUNK, SSM_GROUPS, SSM_GROUP).transpose(1, 2, 0, 3, 4)

    def combine(left, right):
        a_l, b_l = left
        a_r, b_r = right
        return a_r * a_l, a_r * b_l + b_r

    def step(state, u_c):
        bu = jnp.einsum('gpc,lbgc->lbgp', b_bar, u_c.astype(c64))
        _, h_loc = lax.associative_scan(combine, (a_seq, bu), axis=0)
        h = h_loc + powers[:, None] * state[None]
        y = jnp.einsum('gcp,lbgp->lbgc', c_mat, h).real
        return h[-1], y

    state0 = jnp.zeros((bsz, SSM_GROUPS, SSM_STATE), c64)
    _, ys = lax.scan(step, state0, u_chunks)
    y = ys.transpose(2, 0, 1, 3, 4).reshape(bsz, s, SSM_WIDTH)
    y = y + d_skip.astype(f32) * uf
    y = jax.nn.gelu(y)
    y = y * jax.nn.sigmoid(y @ w_glu.astype(f32) + b_glu.astype(f32))
    return y.astype(u.dtype)

def token_mixer(h, w_in, w_sb_up, a_re, a_im, log_dt, b_re, b_im, c_re, c_im,
                d_skip, w_glu, b_glu, w_ssm_up, w_out):
    bsz, s, _ = h.shape
    proj = h @ w_in
    q, k, v, u, g_sb, g_ssm = jnp.split(proj, IN_SPLITS, axis=-1)
    shp = (bsz, s, SB_HEADS, SB_HEAD_DIM)
    y_sb = stick_breaking_attention(q.reshape(shp), k.reshape(shp), v.reshape(shp)) @ w_sb_up
    y_ssm = s5_branch(u, a_re, a_im, log_dt, b_re, b_im, c_re, c_im,
                      d_skip, w_glu, b_glu) @ w_ssm_up
    merged = jax.nn.sigmoid(g_sb) * y_sb + jax.nn.sigmoid(g_ssm) * y_ssm
    return merged @ w_out

def swiglu_ffn(h, w_ffn_in, w_ffn_out):
    gate, up = jnp.split(h @ w_ffn_in, 2, axis=-1)
    return (jax.nn.silu(gate) * up) @ w_ffn_out

def first_inputs(seed: int = 0) -> dict:
    key = jax.random.key(seed)
    ks = jax.random.split(key, 32)
    f32 = jnp.float32

    def nrm(k, shape, scale):
        return jax.random.normal(k, shape, f32) * scale

    G, P, Cg = SSM_GROUPS, SSM_STATE, SSM_GROUP
    n = jnp.arange(P, dtype=f32)
    return {
        "x": nrm(ks[0], (BATCH, SEQ, D_MODEL), 1.0),
        "c": nrm(ks[1], (BATCH, D_MODEL), 1.0),
        "w_ada": nrm(ks[2], (DEPTH, D_MODEL, N_MOD * D_MODEL), 0.5 * D_MODEL ** -0.5),
        "b_ada": nrm(ks[3], (DEPTH, N_MOD * D_MODEL), 0.02),
        "w_in": nrm(ks[4], (DEPTH, D_MODEL, IN_COLS), D_MODEL ** -0.5),
        "w_sb_up": nrm(ks[5], (DEPTH, SB_WIDTH, D_MODEL), SB_WIDTH ** -0.5),
        "ssm_a_re": -0.5 + nrm(ks[6], (DEPTH, G, P), 0.01),
        "ssm_a_im": math.pi * n + nrm(ks[7], (DEPTH, G, P), 0.01),
        "ssm_log_dt": jax.random.uniform(ks[8], (DEPTH, G), f32,
                                         math.log(DT_MIN), math.log(DT_MAX)),
        "ssm_b_re": nrm(ks[9], (DEPTH, G, P, Cg), (2 * Cg) ** -0.5),
        "ssm_b_im": nrm(ks[10], (DEPTH, G, P, Cg), (2 * Cg) ** -0.5),
        "ssm_c_re": nrm(ks[11], (DEPTH, G, Cg, P), P ** -0.5),
        "ssm_c_im": nrm(ks[12], (DEPTH, G, Cg, P), P ** -0.5),
        "ssm_d": 1.0 + nrm(ks[13], (DEPTH, SSM_WIDTH), 0.1),
        "w_glu": nrm(ks[14], (DEPTH, SSM_WIDTH, SSM_WIDTH), SSM_WIDTH ** -0.5),
        "b_glu": nrm(ks[15], (DEPTH, SSM_WIDTH), 0.02),
        "w_ssm_up": nrm(ks[16], (DEPTH, SSM_WIDTH, D_MODEL), SSM_WIDTH ** -0.5),
        "w_out": nrm(ks[17], (DEPTH, D_MODEL, D_MODEL), D_MODEL ** -0.5 * DEEPNORM_BETA),
        "ln1_g": 1.0 + nrm(ks[18], (DEPTH, D_MODEL), 0.02),
        "ln1_b": nrm(ks[19], (DEPTH, D_MODEL), 0.02),
        "w_ffn_in": nrm(ks[20], (DEPTH, D_MODEL, 2 * FFN_HIDDEN), D_MODEL ** -0.5),
        "w_ffn_out": nrm(ks[21], (DEPTH, FFN_HIDDEN, D_MODEL), FFN_HIDDEN ** -0.5 * DEEPNORM_BETA),
        "ln2_g": 1.0 + nrm(ks[22], (DEPTH, D_MODEL), 0.02),
        "ln2_b": nrm(ks[23], (DEPTH, D_MODEL), 0.02),
    }

def first_block(x, c, w_ada, b_ada, w_in, w_sb_up, ssm_a_re, ssm_a_im, ssm_log_dt,
              ssm_b_re, ssm_b_im, ssm_c_re, ssm_c_im, ssm_d, w_glu, b_glu,
              w_ssm_up, w_out, ln1_g, ln1_b, w_ffn_in, w_ffn_out, ln2_g, ln2_b):
    c_act = jax.nn.silu(c)
    for l in range(DEPTH):
        mod = c_act @ w_ada[l] + b_ada[l]
        sh_m, sc_m, g_m, sh_f, sc_f, g_f = [m[:, None, :] for m in jnp.split(mod, N_MOD, axis=-1)]
        h = _normalize(x) * (1.0 + sc_m) + sh_m
        y = token_mixer(h, w_in[l], w_sb_up[l], ssm_a_re[l], ssm_a_im[l], ssm_log_dt[l],
                        ssm_b_re[l], ssm_b_im[l], ssm_c_re[l], ssm_c_im[l], ssm_d[l],
                        w_glu[l], b_glu[l], w_ssm_up[l], w_out[l])
        x = _layer_norm(DEEPNORM_ALPHA * x + (1.0 + g_m) * y, ln1_g[l], ln1_b[l])
        h = _normalize(x) * (1.0 + sc_f) + sh_f
        y = swiglu_ffn(h, w_ffn_in[l], w_ffn_out[l])
        x = _layer_norm(DEEPNORM_ALPHA * x + (1.0 + g_f) * y, ln2_g[l], ln2_b[l])
    return x


_first_inputs = first_inputs


def first_inputs(seed=0):
    import zlib

    import numpy as np

    out = dict(_first_inputs(seed))
    spreads = {}
    factors = {'b_ada': 3.236,
     'ssm_a_re': 64.0,
     'ssm_a_im': 43.608,
     'ssm_log_dt': 47.528,
     'ssm_b_re': 61.256,
     'ssm_b_im': 61.48,
     'ssm_c_re': 58.856,
     'ssm_c_im': 58.608,
     'ssm_d': 4.351,
     'b_glu': 24.702,
     'ln1_g': 8.007,
     'ln1_b': 7.846,
     'ln2_g': 7.895,
     'ln2_b': 8.189}
    for name, (base, spread) in spreads.items():
        noise = np.random.default_rng([zlib.crc32(name.encode()), seed]).standard_normal(out[name].shape)
        drawn = base * np.exp(spread * noise) if base else spread * noise
        out[name] = __import__('jax').numpy.asarray(drawn.astype(out[name].dtype))
    for name, factor in factors.items():
        out[name] = (out[name] * factor).astype(out[name].dtype)
    return out


_narrow_inputs = first_inputs


def first_inputs(seed=0):

    out = dict(_narrow_inputs(seed))
    wider = {'ln1_g': 3.26, 'ln1_b': 3.26, 'ln2_g': 3.16, 'ln2_b': 3.16}
    for name, times in wider.items():
        mean = out[name].mean()
        out[name] = (mean + times * (out[name] - mean)).astype(out[name].dtype)
    return out


DEPTH_2 = 2

GLA_HEADS = 4
GLA_DK = 64
GLA_DV = 128
GLA_GATE_RANK = 16
GLA_GATE_TAU = 16.0
GLA_CHUNK = 64
DSA_HEADS = 8
DSA_HD = 64
IDX_HEADS = 4
IDX_HD = 64
TOPK_MAX = 256
ROPE_THETA = 500000.0
ROPE_FRAC_DIV = 4
SGU_CHUNK = 128
SGU_GROUPS = 8
SGU_WIDTH = D_MODEL
D_FF = 2816
CONV_W = 3
EPS = 1e-6

A_WIDTH = GLA_HEADS * GLA_DV
B_WIDTH = DSA_HEADS * DSA_HD
IN_WIDTHS = (
    GLA_HEADS * GLA_DK,
    GLA_HEADS * GLA_DK,
    GLA_HEADS * GLA_DV,
    A_WIDTH,
    GLA_GATE_RANK,
    DSA_HEADS * DSA_HD,
    DSA_HD,
    DSA_HD,
    IDX_HEADS * IDX_HD,
    IDX_HD,
    IDX_HEADS,
)
IN_WIDTH = sum(IN_WIDTHS)
N_EVEN = (DEPTH_2 + 1) // 2
N_ODD = DEPTH_2 // 2


def rmsnorm(x, g):
    xf = x.astype(jnp.float32)
    y = xf * lax.rsqrt(jnp.mean(xf * xf, axis=-1, keepdims=True) + EPS)
    return (y * g.astype(jnp.float32)).astype(x.dtype)

def layernorm(x, g, b):
    xf = x.astype(jnp.float32)
    mu = jnp.mean(xf, axis=-1, keepdims=True)
    xc = xf - mu
    y = xc * lax.rsqrt(jnp.mean(xc * xc, axis=-1, keepdims=True) + LN_EPS)
    return (y * g.astype(jnp.float32) + b.astype(jnp.float32)).astype(x.dtype)

def split_cols(a, widths):
    out, start = [], 0
    for w in widths:
        out.append(a[..., start:start + w])
        start += w
    return out

def rope_partial(x, pos):
    d = x.shape[-1]
    rd = d // ROPE_FRAC_DIV
    half = rd // 2
    inv = jnp.power(ROPE_THETA, -(jnp.arange(half, dtype=jnp.float32) * 2.0 / rd))
    ang = pos[:, None] * inv[None, :]
    cos = jnp.cos(ang)[:, None, :].astype(x.dtype)
    sin = jnp.sin(ang)[:, None, :].astype(x.dtype)
    x1, x2, rest = x[..., :half], x[..., half:rd], x[..., rd:]
    return jnp.concatenate([x1 * cos - x2 * sin, x2 * cos + x1 * sin, rest], axis=-1)

def gla_chunked(q, k, v, log_a):
    Bn, T, H, dk = q.shape
    dv = v.shape[-1]
    C = GLA_CHUNK
    N = T // C

    def chunks(a):
        return a.astype(jnp.float32).reshape(Bn, N, C, H, a.shape[-1]).transpose(0, 3, 1, 2, 4)

    qf = chunks(q) * (dk ** -0.5)
    kf, vf, la = chunks(k), chunks(v), chunks(log_a)
    b = jnp.cumsum(la, axis=3)
    b_last = b[:, :, :, -1:]
    b_mid = b[:, :, :, C // 2:C // 2 + 1]
    att = jnp.einsum('bhnid,bhnjd->bhnij', qf * jnp.exp(b - b_mid), kf * jnp.exp(b_mid - b))
    att = att * jnp.tril(jnp.ones((C, C), jnp.float32))
    o_intra = jnp.einsum('bhnij,bhnjd->bhnid', att, vf)
    dS = jnp.einsum('bhncd,bhnce->bhnde', kf * jnp.exp(b_last - b), vf)
    decay = jnp.exp(b_last[:, :, :, 0])

    def step(S, inp):
        dec, ds = inp
        return dec[..., None] * S + ds, S

    S0 = jnp.zeros((Bn, H, dk, dv), jnp.float32)
    _, S_prev = lax.scan(step, S0, (jnp.moveaxis(decay, 2, 0), jnp.moveaxis(dS, 2, 0)))
    S_prev = jnp.moveaxis(S_prev, 0, 2)
    o_inter = jnp.einsum('bhncd,bhnde->bhnce', qf * jnp.exp(b), S_prev)
    o = o_intra + o_inter
    return o.transpose(0, 2, 3, 1, 4).reshape(Bn, T, H, dv)

def dsa_attention(q, k, v, iq, ik, iw, topk):
    Bn, T, Hq, d = q.shape
    di = ik.shape[-1]
    NB = T // Q_BLOCK
    key_pos = jnp.arange(T, dtype=jnp.int32)
    ikf = ik.astype(jnp.float32)

    def to_blocks(a):
        return jnp.moveaxis(a.reshape((Bn, NB, Q_BLOCK) + a.shape[2:]), 1, 0)

    q_pos = key_pos.reshape(NB, Q_BLOCK)

    def one_block(args):
        qb, iqb, iwb, qp = args
        s_idx = jnp.einsum('bqhd,bsd->bqhs', iqb.astype(jnp.float32), ikf) * (di ** -0.5)
        score = jnp.einsum('bqh,bqhs->bqs', iwb.astype(jnp.float32), jax.nn.relu(s_idx))
        causal = key_pos[None, :] <= qp[:, None]
        score = jnp.where(causal[None], score, -jnp.inf)
        _, idx = lax.top_k(score, topk)
        kg = jax.vmap(lambda kb, ib: kb[ib])(k, idx)
        vg = jax.vmap(lambda vb, ib: vb[ib])(v, idx)
        valid = idx <= qp[None, :, None]
        s = jnp.einsum('bqhd,bqkd->bqhk', qb.astype(jnp.float32), kg.astype(jnp.float32)) * (d ** -0.5)
        s = jnp.where(valid[:, :, None, :], s, -jnp.inf)
        p = jax.nn.softmax(s, axis=-1)
        o = jnp.einsum('bqhk,bqkd->bqhd', p, vg.astype(jnp.float32))
        return o.astype(q.dtype)

    ob = lax.map(one_block, (to_blocks(q), to_blocks(iq), to_blocks(iw), q_pos))
    return jnp.moveaxis(ob, 0, 1).reshape(Bn, T, Hq * d)

def hybrid_attn_layer(x, g, w_in, w_a2, b_a, head_g, w_o, topk):
    Bn, T, _ = x.shape
    pos = jnp.arange(T, dtype=jnp.float32)
    h = rmsnorm(x, g)
    proj = h @ w_in
    aq, ak, av, ar, alr, bq, bk, bv, iq, ik, iw = split_cols(proj, IN_WIDTHS)
    log_a = jax.nn.log_sigmoid((alr @ w_a2 + b_a).astype(jnp.float32)) / GLA_GATE_TAU
    oa = gla_chunked(aq.reshape(Bn, T, GLA_HEADS, GLA_DK),
                     ak.reshape(Bn, T, GLA_HEADS, GLA_DK),
                     av.reshape(Bn, T, GLA_HEADS, GLA_DV),
                     log_a.reshape(Bn, T, GLA_HEADS, GLA_DK))
    oa = rmsnorm(oa, head_g).reshape(Bn, T, A_WIDTH).astype(x.dtype) * jax.nn.silu(ar)
    bq = rope_partial(bq.reshape(Bn, T, DSA_HEADS, DSA_HD), pos)
    bk = rope_partial(bk[:, :, None, :], pos)[:, :, 0, :]
    iq = rope_partial(iq.reshape(Bn, T, IDX_HEADS, IDX_HD), pos)
    ik = rope_partial(ik[:, :, None, :], pos)[:, :, 0, :]
    iw = iw * (IDX_HEADS ** -0.5)
    ob = dsa_attention(bq, bk, bv, iq, ik, iw, topk)
    return x + jnp.concatenate([oa, ob], axis=-1) @ w_o

def sgu_layer(x, g, w_uv, ln_g, ln_b, w_s, b_s, w_out):
    Bn, T, _ = x.shape
    NC = T // SGU_CHUNK
    gw = SGU_WIDTH // SGU_GROUPS
    h = rmsnorm(x, g)
    z = jax.nn.gelu(h @ w_uv)
    u, v = z[..., :SGU_WIDTH], z[..., SGU_WIDTH:]
    v = layernorm(v, ln_g, ln_b)
    vc = v.reshape(Bn, NC, SGU_CHUNK, SGU_GROUPS, gw)
    ws = w_s * jnp.tril(jnp.ones((SGU_CHUNK, SGU_CHUNK), w_s.dtype))
    mixed = jnp.einsum('gts,bnsgc->bntgc', ws, vc) + b_s.T[None, None, :, :, None]
    return x + (u * mixed.reshape(Bn, T, SGU_WIDTH)) @ w_out

def conv_ffn(x, g, w_up, conv_w, conv_b, w_down):
    T = x.shape[1]
    h = rmsnorm(x, g)
    a = h @ w_up
    ap = jnp.pad(a, ((0, 0), (CONV_W - 1, 0), (0, 0)))
    c = conv_b + sum(conv_w[j] * ap[:, j:j + T] for j in range(CONV_W))
    gate, up = c[..., :D_FF], c[..., D_FF:]
    return x + (jax.nn.silu(gate) * up) @ w_down

def second_inputs(seed: int = 0) -> dict:
    key = jax.random.key(seed)
    ks = jax.random.split(key, 24)

    def nrm(k, shape, scale):
        return jax.random.normal(k, shape, jnp.float32) * scale

    D = D_MODEL
    return {
        "x": nrm(ks[0], (BATCH, SEQ, D), 1.0),
        "attn_norm": 1.0 + nrm(ks[1], (N_EVEN, D), 0.02),
        "attn_w_in": nrm(ks[2], (N_EVEN, D, IN_WIDTH), D ** -0.5),
        "gla_w_a2": nrm(ks[3], (N_EVEN, GLA_GATE_RANK, GLA_HEADS * GLA_DK), GLA_GATE_RANK ** -0.5),
        "gla_b_a": nrm(ks[4], (N_EVEN, GLA_HEADS * GLA_DK), 0.1),
        "gla_head_g": 1.0 + nrm(ks[5], (N_EVEN, GLA_DV), 0.02),
        "attn_w_o": nrm(ks[6], (N_EVEN, A_WIDTH + B_WIDTH, D), (A_WIDTH + B_WIDTH) ** -0.5),
        "sgu_norm": 1.0 + nrm(ks[7], (N_ODD, D), 0.02),
        "sgu_w_uv": nrm(ks[8], (N_ODD, D, 2 * SGU_WIDTH), D ** -0.5),
        "sgu_ln_g": 1.0 + nrm(ks[9], (N_ODD, SGU_WIDTH), 0.02),
        "sgu_ln_b": nrm(ks[10], (N_ODD, SGU_WIDTH), 0.02),
        "sgu_w_s": nrm(ks[11], (N_ODD, SGU_GROUPS, SGU_CHUNK, SGU_CHUNK), 0.5 * SGU_CHUNK ** -0.5),
        "sgu_b_s": 1.0 + nrm(ks[12], (N_ODD, SGU_GROUPS, SGU_CHUNK), 0.02),
        "sgu_w_out": nrm(ks[13], (N_ODD, SGU_WIDTH, D), SGU_WIDTH ** -0.5),
        "ffn_norm": 1.0 + nrm(ks[14], (DEPTH_2, D), 0.02),
        "ffn_w_up": nrm(ks[15], (DEPTH_2, D, 2 * D_FF), D ** -0.5),
        "ffn_conv_w": nrm(ks[16], (DEPTH_2, CONV_W, 2 * D_FF), CONV_W ** -0.5),
        "ffn_conv_b": nrm(ks[17], (DEPTH_2, 2 * D_FF), 0.02),
        "ffn_w_down": nrm(ks[18], (DEPTH_2, D_FF, D), D_FF ** -0.5),
        "final_norm": 1.0 + nrm(ks[19], (D,), 0.02),
    }

def second_block(x, attn_norm, attn_w_in, gla_w_a2, gla_b_a, gla_head_g, attn_w_o,
              sgu_norm, sgu_w_uv, sgu_ln_g, sgu_ln_b, sgu_w_s, sgu_b_s, sgu_w_out,
              ffn_norm, ffn_w_up, ffn_conv_w, ffn_conv_b, ffn_w_down, final_norm):
    T = x.shape[1]
    topk = min(TOPK_MAX, T // 4)
    for i in range(DEPTH_2):
        j = i // 2
        if i % 2 == 0:
            x = hybrid_attn_layer(x, attn_norm[j], attn_w_in[j], gla_w_a2[j], gla_b_a[j],
                                  gla_head_g[j], attn_w_o[j], topk)
        else:
            x = sgu_layer(x, sgu_norm[j], sgu_w_uv[j], sgu_ln_g[j], sgu_ln_b[j],
                          sgu_w_s[j], sgu_b_s[j], sgu_w_out[j])
        x = conv_ffn(x, ffn_norm[i], ffn_w_up[i], ffn_conv_w[i], ffn_conv_b[i], ffn_w_down[i])
    return rmsnorm(x, final_norm)


_first_inputs_2 = second_inputs


def second_inputs(seed=0):
    import zlib

    import numpy as np

    out = dict(_first_inputs_2(seed))
    spreads = {}
    factors = {'gla_b_a': 2.747,
     'gla_head_g': 5.005,
     'sgu_norm': 4.976,
     'sgu_ln_g': 8.0,
     'sgu_ln_b': 8.0,
     'sgu_b_s': 5.988,
     'ffn_norm': 2.937,
     'ffn_conv_b': 3.072,
     'final_norm': 2.831}
    for name, (base, spread) in spreads.items():
        noise = np.random.default_rng([zlib.crc32(name.encode()), seed]).standard_normal(out[name].shape)
        drawn = base * np.exp(spread * noise) if base else spread * noise
        out[name] = __import__('jax').numpy.asarray(drawn.astype(out[name].dtype))
    for name, factor in factors.items():
        out[name] = (out[name] * factor).astype(out[name].dtype)
    return out


_narrow_inputs_2 = second_inputs


def second_inputs(seed=0):

    out = dict(_narrow_inputs_2(seed))
    wider = {'sgu_ln_g': 7.82, 'sgu_ln_b': 8.25, 'sgu_b_s': 3.82, 'final_norm': 3.2}
    for name, times in wider.items():
        mean = out[name].mean()
        out[name] = (mean + times * (out[name] - mean)).astype(out[name].dtype)
    return out


CONV_DIM = 512
CONV_KERNEL = 31
HGRN_DIM = 1024
HGRN_HEADS = 8
HGRN_HEAD_DIM = HGRN_DIM // HGRN_HEADS
HGRN_CHUNK = 64
N_BRANCHES = 2
FFN_KERNEL = 3
RMS_EPS = 1e-6
ALPHA = (2.0 * DEPTH) ** 0.25
BETA = (8.0 * DEPTH) ** -0.25

IN_SPLITS_3 = [CONV_DIM, CONV_DIM, HGRN_DIM, HGRN_DIM, HGRN_DIM, HGRN_DIM, N_BRANCHES * D_MODEL]
IN_COLS_3 = sum(IN_SPLITS_3)
IN_OFFSETS = list(np.cumsum(IN_SPLITS_3)[:-1])


def layer_norm(x, g, b):
    xf = x.astype(jnp.float32)
    mu = jnp.mean(xf, axis=-1, keepdims=True)
    var = jnp.mean(jnp.square(xf - mu), axis=-1, keepdims=True)
    y = (xf - mu) * lax.rsqrt(var + LN_EPS) * g.astype(jnp.float32) + b.astype(jnp.float32)
    return y.astype(x.dtype)

def causal_dwconv(x, w, b):
    k_w = w.shape[0]
    c = x.shape[-1]
    y = lax.conv_general_dilated(
        x, w[:, None, :].astype(x.dtype), window_strides=(1,), padding=[(k_w - 1, 0)],
        dimension_numbers=("NWC", "WIO", "NWC"), feature_group_count=c)
    return y + b.astype(x.dtype)

def hgrn2_chunked(q, k, v, logf):
    bsz, seq, nh, dk = q.shape
    dv = v.shape[-1]
    nc = seq // HGRN_CHUNK

    def to_chunks(t):
        return t.reshape(bsz, nc, HGRN_CHUNK, nh, t.shape[-1]).transpose(1, 0, 3, 2, 4)

    qc, kc, vc, lfc = to_chunks(q), to_chunks(k), to_chunks(v), to_chunks(logf)
    bc = jnp.cumsum(lfc, axis=3)
    mask = jnp.tril(jnp.ones((HGRN_CHUNK, HGRN_CHUNK), dtype=bool))[:, :, None]

    def step(state, inp):
        q_c, k_c, v_c, b_c = inp
        diff = b_c[:, :, :, None, :] - b_c[:, :, None, :, :]
        decay = jnp.exp(jnp.where(mask, diff, -jnp.inf))
        scores = jnp.einsum("bhtk,bhsk,bhtsk->bhts", q_c, k_c, decay)
        o_intra = jnp.einsum("bhts,bhsv->bhtv", scores, v_c)
        o_inter = jnp.einsum("bhtk,bhkv->bhtv", q_c * jnp.exp(b_c), state)
        b_last = b_c[:, :, -1, :]
        k_tail = k_c * jnp.exp(b_last[:, :, None, :] - b_c)
        new_state = jnp.exp(b_last)[..., None] * state + jnp.einsum("bhsk,bhsv->bhkv", k_tail, v_c)
        return new_state, o_intra + o_inter

    s0 = jnp.zeros((bsz, nh, dk, dv), jnp.float32)
    _, oc = lax.scan(step, s0, (qc, kc, vc, bc))
    return oc.transpose(1, 0, 3, 2, 4).reshape(bsz, seq, nh, dv)

def third_inputs(seed: int = 0) -> dict:
    key = jax.random.key(seed)
    ks = jax.random.split(key, 20)

    def nrm(k, shape, scale):
        return jax.random.normal(k, shape, jnp.float32) * scale

    col_scale = jnp.concatenate([
        jnp.ones((2 * CONV_DIM + 2 * HGRN_DIM,), jnp.float32),
        jnp.full((HGRN_DIM,), BETA, jnp.float32),
        jnp.ones((HGRN_DIM + N_BRANCHES * D_MODEL,), jnp.float32)])
    ffn_scale = jnp.concatenate([jnp.full((D_FF,), BETA, jnp.float32), jnp.ones((D_FF,), jnp.float32)])
    return {
        "x": nrm(ks[0], (BATCH, SEQ, D_MODEL), 1.0),
        "w_in": nrm(ks[1], (DEPTH, D_MODEL, IN_COLS_3), D_MODEL ** -0.5) * col_scale,
        "w_conv_dw": nrm(ks[2], (DEPTH, CONV_KERNEL, CONV_DIM), CONV_KERNEL ** -0.5),
        "b_conv_dw": nrm(ks[3], (DEPTH, CONV_DIM), 0.02),
        "conv_ln_g": 1.0 + nrm(ks[4], (DEPTH, CONV_DIM), 0.02),
        "conv_ln_b": nrm(ks[5], (DEPTH, CONV_DIM), 0.02),
        "w_conv_out": nrm(ks[6], (DEPTH, CONV_DIM, D_MODEL), BETA * CONV_DIM ** -0.5),
        "hgrn_lb_logits": nrm(ks[7], (DEPTH + 1, HGRN_DIM), 0.5),
        "hgrn_norm_g": 1.0 + nrm(ks[8], (DEPTH, HGRN_DIM), 0.02),
        "w_hgrn_out": nrm(ks[9], (DEPTH, HGRN_DIM, D_MODEL), BETA * HGRN_DIM ** -0.5),
        "w_out": nrm(ks[10], (DEPTH, D_MODEL, D_MODEL), BETA * D_MODEL ** -0.5),
        "ln1_g": 1.0 + nrm(ks[11], (DEPTH, D_MODEL), 0.02),
        "ln1_b": nrm(ks[12], (DEPTH, D_MODEL), 0.02),
        "w_ffn_in": nrm(ks[13], (DEPTH, D_MODEL, 2 * D_FF), D_MODEL ** -0.5) * ffn_scale,
        "w_ffn_dw": nrm(ks[14], (DEPTH, FFN_KERNEL, D_FF), FFN_KERNEL ** -0.5),
        "b_ffn_dw": nrm(ks[15], (DEPTH, D_FF), 0.02),
        "w_ffn_out": nrm(ks[16], (DEPTH, D_FF, D_MODEL), BETA * D_FF ** -0.5),
        "ln2_g": 1.0 + nrm(ks[17], (DEPTH, D_MODEL), 0.02),
        "ln2_b": nrm(ks[18], (DEPTH, D_MODEL), 0.02),
    }

def third_block(x, w_in, w_conv_dw, b_conv_dw, conv_ln_g, conv_ln_b, w_conv_out,
              hgrn_lb_logits, hgrn_norm_g, w_hgrn_out, w_out, ln1_g, ln1_b,
              w_ffn_in, w_ffn_dw, b_ffn_dw, w_ffn_out, ln2_g, ln2_b):
    bsz, seq, _ = x.shape
    lb_all = jnp.cumsum(jax.nn.softmax(hgrn_lb_logits.astype(jnp.float32), axis=0), axis=0)
    for l in range(DEPTH):
        h = x
        proj = h @ w_in[l]
        c_val, c_gate, q_z, f_z, i_v, g_z, m_z = jnp.split(proj, IN_OFFSETS, axis=-1)

        c = c_val * jax.nn.sigmoid(c_gate)
        c = causal_dwconv(c, w_conv_dw[l], b_conv_dw[l])
        c = jax.nn.silu(layer_norm(c, conv_ln_g[l], conv_ln_b[l]))
        y_conv = c @ w_conv_out[l]

        lb = lb_all[l]
        zf = f_z.astype(jnp.float32)
        logf = jnp.log(lb + (1.0 - lb) * jax.nn.sigmoid(zf))
        k_in = (1.0 - lb) * jax.nn.sigmoid(-zf)
        qf = jax.nn.silu(q_z.astype(jnp.float32))
        heads = lambda t: t.reshape(bsz, seq, HGRN_HEADS, HGRN_HEAD_DIM)
        o = hgrn2_chunked(heads(qf), heads(k_in), heads(i_v.astype(jnp.float32)), heads(logf))
        o = o * lax.rsqrt(jnp.mean(jnp.square(o), axis=-1, keepdims=True) + RMS_EPS)
        o = o.reshape(bsz, seq, HGRN_DIM) * hgrn_norm_g[l].astype(jnp.float32)
        o = o.astype(x.dtype) * jax.nn.silu(g_z)
        y_hgrn = o @ w_hgrn_out[l]

        gates = jax.nn.sigmoid(m_z).reshape(bsz, seq, N_BRANCHES, D_MODEL)
        mixed = gates[:, :, 0, :] * y_conv + gates[:, :, 1, :] * y_hgrn
        mix = mixed @ w_out[l]
        x = layer_norm(ALPHA * x + mix, ln1_g[l], ln1_b[l])

        z = x @ w_ffn_in[l]
        u, gv = jnp.split(z, [D_FF], axis=-1)
        u = causal_dwconv(u, w_ffn_dw[l], b_ffn_dw[l])
        y_ffn = (jax.nn.gelu(u) * gv) @ w_ffn_out[l]
        x = layer_norm(ALPHA * x + y_ffn, ln2_g[l], ln2_b[l])
    return x


_first_inputs_3 = third_inputs


def third_inputs(seed=0):
    import zlib

    import numpy as np

    out = dict(_first_inputs_3(seed))
    spreads = {}
    factors = {'b_conv_dw': 8.0,
     'conv_ln_g': 8.0,
     'conv_ln_b': 8.0,
     'hgrn_lb_logits': 8.0,
     'hgrn_norm_g': 8.0,
     'ln1_g': 2.781,
     'ln1_b': 2.844,
     'b_ffn_dw': 8.0,
     'ln2_g': 2.874,
     'ln2_b': 2.903}
    for name, (base, spread) in spreads.items():
        noise = np.random.default_rng([zlib.crc32(name.encode()), seed]).standard_normal(out[name].shape)
        drawn = base * np.exp(spread * noise) if base else spread * noise
        out[name] = __import__('jax').numpy.asarray(drawn.astype(out[name].dtype))
    for name, factor in factors.items():
        out[name] = (out[name] * factor).astype(out[name].dtype)
    return out


_narrow_inputs_3 = third_inputs


def third_inputs(seed=0):

    out = dict(_narrow_inputs_3(seed))
    wider = {'conv_ln_g': 5.11, 'conv_ln_b': 4.72, 'hgrn_norm_g': 6.16, 'ln2_g': 3.24, 'ln2_b': 3.23}
    for name, times in wider.items():
        mean = out[name].mean()
        out[name] = (mean + times * (out[name] - mean)).astype(out[name].dtype)
    return out


def setup_inputs(seed=0):
    out = dict(first_inputs(seed))
    for name, value in second_inputs(seed + 1).items():
        if name != "x":
            out[name + "_2"] = value
    for name, value in third_inputs(seed + 2).items():
        if name != "x":
            out[name + "_3"] = value
    return out


def reference(
    x, c, w_ada, b_ada, w_in, w_sb_up, ssm_a_re, ssm_a_im, ssm_log_dt, ssm_b_re, ssm_b_im,
    ssm_c_re, ssm_c_im, ssm_d, w_glu, b_glu, w_ssm_up, w_out, ln1_g, ln1_b, w_ffn_in, w_ffn_out,
    ln2_g, ln2_b, attn_norm_2, attn_w_in_2, gla_w_a2_2, gla_b_a_2, gla_head_g_2, attn_w_o_2,
    sgu_norm_2, sgu_w_uv_2, sgu_ln_g_2, sgu_ln_b_2, sgu_w_s_2, sgu_b_s_2, sgu_w_out_2,
    ffn_norm_2, ffn_w_up_2, ffn_conv_w_2, ffn_conv_b_2, ffn_w_down_2, final_norm_2, w_in_3,
    w_conv_dw_3, b_conv_dw_3, conv_ln_g_3, conv_ln_b_3, w_conv_out_3, hgrn_lb_logits_3,
    hgrn_norm_g_3, w_hgrn_out_3, w_out_3, ln1_g_3, ln1_b_3, w_ffn_in_3, w_ffn_dw_3, b_ffn_dw_3,
    w_ffn_out_3, ln2_g_3, ln2_b_3,
):
    x = first_block(
        x, c, w_ada, b_ada, w_in, w_sb_up, ssm_a_re, ssm_a_im, ssm_log_dt, ssm_b_re, ssm_b_im,
        ssm_c_re, ssm_c_im, ssm_d, w_glu, b_glu, w_ssm_up, w_out, ln1_g, ln1_b, w_ffn_in,
        w_ffn_out, ln2_g, ln2_b,
    )
    x = second_block(
        x, attn_norm_2, attn_w_in_2, gla_w_a2_2, gla_b_a_2, gla_head_g_2, attn_w_o_2,
        sgu_norm_2, sgu_w_uv_2, sgu_ln_g_2, sgu_ln_b_2, sgu_w_s_2, sgu_b_s_2, sgu_w_out_2,
        ffn_norm_2, ffn_w_up_2, ffn_conv_w_2, ffn_conv_b_2, ffn_w_down_2, final_norm_2,
    )
    return third_block(
        x, w_in_3, w_conv_dw_3, b_conv_dw_3, conv_ln_g_3, conv_ln_b_3, w_conv_out_3,
        hgrn_lb_logits_3, hgrn_norm_g_3, w_hgrn_out_3, w_out_3, ln1_g_3, ln1_b_3, w_ffn_in_3,
        w_ffn_dw_3, b_ffn_dw_3, w_ffn_out_3, ln2_g_3, ln2_b_3,
    )


_drawn_inputs = setup_inputs


def setup_inputs(seed=0):
    import zlib

    import numpy as np

    out = dict(_drawn_inputs(seed))
    spreads = {}
    factors = {'attn_norm_2': 2.774,
     'gla_head_g_2': 5.246,
     'sgu_norm_2': 14.853,
     'ffn_norm_2': 6.357,
     'ffn_conv_b_2': 5.734}
    for name, (base, spread) in spreads.items():
        noise = np.random.default_rng([zlib.crc32(name.encode()), seed]).standard_normal(out[name].shape)
        drawn = base * np.exp(spread * noise) if base else spread * noise
        out[name] = __import__('jax').numpy.asarray(drawn.astype(out[name].dtype))
    for name, factor in factors.items():
        out[name] = (out[name] * factor).astype(out[name].dtype)
    return out
```

```python
import math
from contextlib import ExitStack

import numpy as np
import concourse.bass as bass
from concourse import mybir

F32 = mybir.dt.float32
I32 = mybir.dt.int32
ALU = mybir.AluOpType
ACT = mybir.ActivationFunctionType
AXX = mybir.AxisListType.X

P = 128
T = 512
D = 1024
KT = D // P
TT = T // P
HID = 2816
HT = HID // P
SLOTS = 4
SLOT = 2048
BANKS = 4
LN_EPS, RMS_EPS = 1e-5, 1e-6
ALPHA = 2.0 ** 0.25
NEG = -3.0e38
TOPK = min(256, T // 4)

VECTORS = [
    ("b_ada", 48), ("ssm_a_re", 16), ("ssm_a_im", 16), ("ssm_d", 4), ("b_glu", 4), ("c", 8),
    ("ln1_g", 8), ("ln1_b", 8), ("ln2_g", 8), ("ln2_b", 8), ("attn_norm_2", 8),
    ("gla_b_a_2", 2), ("gla_head_g_2", 1), ("sgu_norm_2", 8), ("ffn_norm_2", 16),
    ("ffn_conv_w_2", 264), ("ffn_conv_b_2", 88), ("final_norm_2", 8),
    ("w_conv_dw_3", 124), ("b_conv_dw_3", 4), ("conv_ln_g_3", 4), ("conv_ln_b_3", 4),
    ("hgrn_lb_logits_3", 16), ("hgrn_norm_g_3", 8), ("ln1_g_3", 8), ("ln1_b_3", 8),
    ("w_ffn_dw_3", 66), ("b_ffn_dw_3", 22), ("ln2_g_3", 8), ("ln2_b_3", 8),
]
COLUMN, _at = {}, 0
for _name, _rows in VECTORS:
    COLUMN[_name] = _at
    _at += _rows
VROWS = _at
VTILES = -(-VROWS // P)

CONST_AT = {}


def constants():
    r, c = np.arange(P)[:, None], np.arange(P)[None, :]
    parts, at = [], 0

    def put(name, a):
        nonlocal at
        CONST_AT[name] = at
        a = np.broadcast_to(np.asarray(a, np.float32), (P, a.shape[-1]))
        parts.append(a)
        at += a.shape[1]

    put("ident", (r == c).astype(np.float32))
    put("ones", np.ones((P, P)))
    put("later", (r > c).astype(np.float32))
    put("before", (r < c).astype(np.float32))
    put("upto", (r <= c).astype(np.float32))
    put("chunk64", ((r <= c) & (r // 64 == c // 64)).astype(np.float32))
    put("notyet", np.where(c <= r, 0.0, NEG))
    perm = np.zeros((P, P))
    for h in range(2):
        for i in range(8):
            perm[64 * h + 8 + i, 64 * h + i] = -1.0
            perm[64 * h + i, 64 * h + 8 + i] = 1.0
    put("turn", perm)
    for lv in range(7):
        h = 64 >> lv
        put(f"level{lv}", ((r // (2 * h) == c // (2 * h)) & (r % (2 * h) < h) & (c % (2 * h) >= h)).astype(np.float32))
    put("group0", ((r // 16) % 2 == 0).astype(np.float32))
    put("group1", ((r // 16) % 2 == 1).astype(np.float32))
    inv = np.power(np.float32(500000.0), -(np.arange(8, dtype=np.float32) * 2.0 / 16)).astype(np.float32)
    ang = (np.arange(T, dtype=np.float32)[None, :] * inv[:, None]).astype(np.float32)
    cos, sin = np.ones((P, T)), np.zeros((P, T))
    for h in range(2):
        for k in range(2):
            cos[64 * h + 8 * k:64 * h + 8 * k + 8] = np.cos(ang)
            sin[64 * h + 8 * k:64 * h + 8 * k + 8] = np.sin(ang)
    put("cos", cos)
    put("sin", sin)
    put("keep64", (np.arange(T)[None, :] % 64 != 0).astype(np.float32))
    put("keep128", (np.arange(T)[None, :] % 128 != 0).astype(np.float32))
    return np.ascontiguousarray(np.concatenate(parts, axis=1), np.float32)


class Signal:

    def __init__(self, handle):
        self.handle, self.base, self.total = handle, 0, 0

    def up(self):
        self.total += 1
        return self.handle, 1

    def at(self, k):
        return self.handle, self.base + k


class Gemm:

    def __init__(self, name, n, panels, tiles, kt, evac, ppt=1):
        self.name, self.n, self.panels, self.tiles, self.kt = name, n, panels, tiles, kt
        self.evac, self.ppt = evac, ppt
        self.ppu = len(panels)


def build_program(nc, a, out, debug=None, blocks=(1, 2, 3)):
    ctx = ExitStack()
    with ctx:
        def sbuf(name, shape, dt=F32):
            return ctx.enter_context(nc.sbuf_tensor(name, shape, dt))

        signals = {}

        def sig(name):
            if name not in signals:
                signals[name] = Signal(ctx.enter_context(nc.semaphore(name)))
            return signals[name]

        arena = sbuf("arena", [P, 9, KT, T])
        weights = sbuf("weights", [P, SLOTS, SLOT])
        ncst = a["constants"].shape[1]
        cst = sbuf("cst", [P, ncst])
        cols = sbuf("cols", [P, VTILES * P])
        mod = sbuf("mod", [P, 48])
        small = sbuf("small", [P, 512])
        ps = ctx.enter_context(nc.psum_tensor("ps", [P, 8, 512], F32))

        def big(i):
            return arena[:, i, :, :]

        def const(name, n=P):
            return cst[:, CONST_AT[name]:CONST_AT[name] + n]

        def col(name, i=0):
            at = COLUMN[name] + i
            return cols[:, at:at + 1] if isinstance(i, int) else cols[:, bass.ds(at, 1)]

        X, H = big(0), big(1)
        ident = const("ident")

        def kview(w):
            return w.rearrange("(k p) n -> p k n", p=P)

        def slot_view(s, kt, n):
            return weights[:, s, 0:kt * n].rearrange("p (k n) -> p k n", k=kt)

        def cols_panel(w, kt, c0, width):
            def dmas(u, s):
                return [(slot_view(s, kt, width), kview(w)[:, :, bass.ds(c0 + u * width, width)])]
            return dmas

        def pair_panel(w):
            v = kview(w).rearrange("p k (h n) -> p k h n", h=2)

            def mk(h):
                def one(u, s):
                    dst = slot_view(s, KT, 256).rearrange("p k (h n) -> p k h n", h=2)
                    return dst[:, :, h, :], v[:, :, h, bass.ds(u * P, P)]
                return one
            return lambda u, s: [mk(0)(u, s), mk(1)(u, s)]

        def half_panel(w, half):
            v = w.rearrange("(h k p) n -> p h k n", p=P, h=2)[:, half]
            return lambda u, s: [(slot_view(s, HT // 2, P), v[:, :, bass.ds(u * P, P)])]

        plan, order = {}, []

        def gemm(name, *args, **kw):
            plan[name] = Gemm(name, *args, **kw)
            order.append(plan[name])

        def feat(name, w, kt, n, evac, c0=0):
            width = 256 if kt == 8 else 512
            tiles = [("w", i * P, P, 0) for i in range(width // P)]
            gemm(name, n, [cols_panel(w, kt, c0, width)], tiles, kt, evac)

        def tok(name, w, kt, n, evac, c0=0):
            gemm(name, n, [cols_panel(w, kt, c0, 256)], [("x", 0, 256, i) for i in range(TT)], kt, evac)

        def ffn(tag, w_in, w_out, evac):
            gemm(tag + "_in", HT, [pair_panel(w_in)], [("w", 0, P, 0), ("w", P, P, 0)], KT, evac)
            gemm(tag + "_out", KT, [half_panel(w_out, 0), half_panel(w_out, 1)], [("w", 0, P, 0)], HT, "dve")

        if 1 in blocks:
            w = a["w_in"][0]
            gemm("ada", 24, [cols_panel(a["w_ada"][0], KT, 0, 256)], [("w", 0, P, 0), ("w", P, P, 0)], KT, None)
            feat("qk", w, KT, 4, "act")
            tok("v", w, KT, 2, "act", c0=1024)
            feat("u", w, KT, 2, "act", c0=1536)
            feat("gates", w, KT, 8, "act", c0=2048)
            feat("sb_up", a["w_sb_up"][0], 4, 2, "dve")
            feat("glu", a["w_glu"][0], 4, 1, "act")
            feat("ssm_up", a["w_ssm_up"][0], 4, 2, "dve")
            feat("out1", a["w_out"][0], KT, 4, "dve")
            ffn("ffn1", a["w_ffn_in"][0], a["w_ffn_out"][0], "swiglu")
        if 2 in blocks:
            w = a["attn_w_in_2"][0]
            feat("aqk", w, KT, 2, "act")
            tok("av", w, KT, 2, "act", c0=512)
            feat("ar", w, KT, 2, "act", c0=1024)
            feat("bq", w, KT, 2, "act", c0=1552)
            feat("iq", w, KT, 1, "act", c0=2192)
            wk = kview(w)
            gemm("shared", 1, [lambda u, s: [
                (slot_view(s, KT, 256)[:, :, 64 * i:64 * i + 64], wk[:, :, c0:c0 + 64])
                for i, c0 in enumerate((2064, 2064, 2448, 2448))]],
                [("w", 0, P, 0), ("w", P, P, 0)], KT, "act")
            gemm("narrow", 1, [lambda u, s: [
                (slot_view(s, KT, 256)[:, :, o:o + n], wk[:, :, c0:c0 + n])
                for o, n, c0 in ((0, 16, 1536), (16, 64, 2128), (80, 4, 2512))]],
                [("w", 0, 16, 0)] + [("x", 16, 68, i) for i in range(TT)], KT, "act")
            feat("w_o", a["attn_w_o_2"][0], KT, 4, "dve")
            ffn("ffn2", a["ffn_w_up_2"][0], a["ffn_w_down_2"][0], "conv")
            feat("sgu_u", a["sgu_w_uv_2"][0], KT, 4, "act")
            tok("sgu_v", a["sgu_w_uv_2"][0], KT, 4, "act", c0=1024)
            feat("sgu_out", a["sgu_w_out_2"][0], KT, 4, "dve")
            ffn("ffn3", a["ffn_w_up_2"][1], a["ffn_w_down_2"][1], "conv")
        if 3 in blocks:
            w = a["w_in_3"][0]
            feat("cval", w, KT, 2, "act")
            feat("cgate", w, KT, 2, "act", c0=512)
            feat("qz", w, KT, 4, "act", c0=1024)
            feat("fz", w, KT, 4, "act", c0=2048)
            tok("iv", w, KT, 4, "act", c0=3072)
            feat("gz", w, KT, 4, "act", c0=4096)
            feat("mz", w, KT, 8, "act", c0=5120)
            feat("conv_out", a["w_conv_out_3"][0], 4, 2, "dve")
            feat("hgrn_out", a["w_hgrn_out_3"][0], KT, 4, "dve")
            feat("out3", a["w_out_3"][0], KT, 4, "dve")
            ffn("ffn4", a["w_ffn_in_3"][0], a["w_ffn_out_3"][0], "convgelu")

        RATES = {None: {}, "act": {"tile_act": "t"}, "dve": {"tile_dve": "t"},
                 "swiglu": {"tile_act": 1, "tile_dve": 1},
                 "conv": {"tap_act": 2, "tap_step": 2, "tile_dve": 2, "gate_act": 1, "hidden_done": 1},
                 "convgelu": {"tap_act": 1, "tap_step": 1, "tile_dve": 2, "gate_act": 1}}
        running = dict.fromkeys(["tiles", "tile_act", "tile_dve", "tap_act", "tap_step", "gate_act"], 0)
        running["hidden_done"] = 2
        panel_list, slot_count = [], [0] * SLOTS
        for g in order:
            g.base, g.first_panel = dict(running), len(panel_list)
            for u in range(g.n):
                for j, dmas in enumerate(g.panels):
                    s = len(panel_list) % SLOTS
                    k = len(dmas(0, s))
                    slot_count[s] += 16 * k
                    panel_list.append(dict(g=g, u=u, j=j, slot=s, filled=slot_count[s],
                                           freed=running["tiles"] + (u + 1) * len(g.tiles)))
            running["tiles"] += g.n * len(g.tiles)
            for k, v in RATES[g.evac].items():
                running[k] += g.n * (len(g.tiles) if v == "t" else v)
            g.end = dict(running)
        tiles_done = sig("tiles_done")
        panel_in = [sig(f"panel_in{s}") for s in range(SLOTS)]
        fed = [0]

        def one_panel(sp, p, u, freed):
            info = panel_list[p]
            if freed is not None:
                sp.wait_ge(tiles_done.handle, freed)
            for dst, src in info["g"].panels[info["j"]](u, info["slot"]):
                sp.dma_start(dst, src).then_inc(panel_in[info["slot"]].handle, 16)

        def feed(sp, last):
            g = plan[last] if last else None
            end = min((g.first_panel + g.n * g.ppu if g else 0) + SLOTS, len(panel_list))
            while fed[0] < end:
                p = fed[0]
                g, ppu = panel_list[p]["g"], panel_list[p]["g"].ppu
                per = SLOTS // ppu
                stop = min(end, g.first_panel + g.n * ppu)
                turns = (stop - p) // SLOTS
                inner = p - g.first_panel >= SLOTS and (p - g.first_panel) % ppu == 0
                if inner and turns >= 2:
                    u0, step = panel_list[p]["u"], per * len(g.tiles)
                    with sp.Fori(0, turns) as i:
                        for j in range(SLOTS):
                            one_panel(sp, p + j, i * per + (u0 + j // ppu),
                                      i * step + panel_list[p + j - SLOTS]["freed"])
                    fed[0] += turns * SLOTS
                else:
                    one_panel(sp, p, panel_list[p]["u"], panel_list[p - SLOTS]["freed"] if p >= SLOTS else None)
                    fed[0] += 1

        def units(eng, g, emit):
            turns = g.n // 4
            done = 0
            if turns >= 2:
                with eng.Fori(0, turns) as i:
                    for j in range(4):
                        emit(i * 4 + j, j)
                done = turns * 4
            for u in range(done, g.n):
                emit(u, u)

        def bank_of(g, j, t):
            return (g.base["tiles"] + j * len(g.tiles) + t) % BANKS

        def mm_gemm(pe, name, x):
            g = plan[name]
            nt = len(g.tiles)
            if g.evac is not None:
                for k in ("tile_act", "tile_dve"):
                    if g.base[k]:
                        pe.wait_ge(sig(k).handle, g.base[k])
            r = {k: (nt if v == "t" else v) for k, v in RATES[g.evac].items()}

            def emit(u, j):
                infos = [panel_list[g.first_panel + j * g.ppu + i] for i in range(g.ppu)]
                per = SLOTS // g.ppu
                for t, (kind, c0, width, tt) in enumerate(g.tiles):
                    bank = bank_of(g, j, t)
                    back = j * nt + t - BANKS
                    if g.evac is not None and (j * nt + t >= BANKS or not isinstance(u, int)):
                        bu, bt = back // nt, back % nt
                        if g.evac in ("swiglu", "convgelu", "conv"):
                            k, idx, rate = {"swiglu": [("tile_act", 0, 1), ("tile_dve", 0, 1)],
                                            "conv": [("tile_dve", 0, 2), ("tile_dve", 1, 2)],
                                            "convgelu": [("tile_dve", 0, 2), ("tile_dve", 1, 2)]}[g.evac][bt]
                        else:
                            (k,), idx, rate = tuple(r), bt, nt
                        value = g.base[k] + idx + 1 + (u + (bu - j)) * rate
                        if isinstance(value, int) or g.base[k] >= BANKS:
                            pe.wait_ge(sig(k).handle, value)
                        else:
                            raise ValueError("wait might fall below zero")
                    kk = 0
                    for i in range(g.ppu):
                        info = infos[i]
                        if t == 0:
                            gap = panel_list[info_index(g, j, i) + SLOTS]["filled"] - info["filled"] \
                                if not isinstance(u, int) else 0
                            first = info["filled"]
                            value = first if isinstance(u, int) else turn_value(u, j, per, gap, first)
                            pe.wait_ge(panel_in[info["slot"]].handle, value)
                        kt = g.kt // g.ppu
                        total = sum(width_of(d) for d in [g])
                        wv = slot_view(info["slot"], kt, total)
                        for k in range(kt):
                            if kind == "w":
                                lhs, rhs = wv[:, k, c0:c0 + width], x(kk)
                                o = ps[0:width, bank, :]
                                if g.name == "ada":
                                    rhs = x(kk)
                                    o = ps[:, 4, bass.ds(u * 2 + t, 1)]
                            else:
                                lhs, rhs = x(kk)[:, tt * P:tt * P + P], wv[:, k, c0:c0 + width]
                                o = ps[:, bank, 0:width]
                            last = nc.tensor.matmul(o, lhs, rhs, start=kk == 0, stop=kk == g.kt - 1)
                            kk += 1
                    last.then_inc(tiles_done.handle, 1)

            def info_index(g, j, i):
                return g.first_panel + j * g.ppu + i

            def turn_value(u, j, per, gap, first):
                return (u - j) * (gap // per) + first

            units(pe, g, emit)

        def width_of(g):
            if g.kt == HT:
                return P
            return 256 if g.kt == KT else 512

        def take(eng, name, signal, tiles, fn):
            g = plan[name]
            nt = len(g.tiles)

            def emit(u, j):
                for t in tiles:
                    eng.wait_ge(tiles_done.handle, g.base["tiles"] + u * nt + (t + 1))
                    fn(u, t, bank_of(g, j, t)).then_inc(sig(signal).handle, 1)
            units(eng, g, emit)

        def at_tile(view, i):
            if isinstance(i, int):
                return view[:, i, :]
            return view[:, bass.ds(i, 1), :].rearrange("p a t -> p (a t)")

        def phase(last=None):
            for s in signals.values():
                s.base = s.total
            block = nc.Block()
            return block

        def stepper(eng, name):
            s = sig(name)

            def step(ins):
                ins.then_inc(*s.up())
                eng.wait_ge(s.handle, s.total)
                return ins
            return step

        def bc(row, n):
            return row.rearrange("p (a t) -> p a t", a=1).broadcast_to([row.shape[0], n, row.shape[1]])

        def bl(c, n):
            return c.rearrange("p (a b) -> p a b", b=1).broadcast_to([c.shape[0], c.shape[1], n])

        def normalize(src, dst, kt, center, eps, gain=None, bias=None, func=ACT.Identity, rescale=None, tmp=8):
            n = kt * P
            sq = arena[:, tmp, 0:kt, :]
            part, mean, var = (small_row(i) for i in range(3))
            std = rstd = var
            with phase() as block:
                @block.vector
                def _(dve):
                    step = stepper(dve, "norm_step")
                    cur = src
                    if center:
                        nc.vector.tensor_reduce(part, src.rearrange("p k t -> p t k"), AXX, ALU.add)\
                          .then_inc(*sig("part_sum").up())
                        dve.wait_ge(*sig("summed").at(1))
                        step(nc.vector.tensor_scalar(mean, ps[:, 0, :], 1.0 / n, None, ALU.mult))
                        nc.vector.tensor_tensor(dst, src, bc(mean, kt), ALU.subtract)\
                          .then_inc(*sig("centered").up())
                        cur = dst
                    dve.wait_ge(*sig("squared").at(1))
                    nc.vector.tensor_reduce(part2, sq.rearrange("p k t -> p t k"), AXX, ALU.add)\
                      .then_inc(*sig("part_sum").up())
                    dve.wait_ge(*sig("summed").at(1 + center))
                    nc.vector.tensor_scalar(var, ps[:, 1, :], 1.0 / n, eps, ALU.mult, ALU.add)\
                      .then_inc(*sig("variance").up())
                    dve.wait_ge(*sig("deviation").at(1))
                    step(nc.vector.reciprocal(rstd, std))
                    nc.vector.tensor_tensor(dst, cur, bc(rstd, kt), ALU.mult)\
                      .then_inc(*sig("normed").up())

                @block.tensor
                def _(pe):
                    if center:
                        pe.wait_ge(*sig("part_sum").at(1))
                        nc.tensor.matmul(ps[:, 0, :], const("ones"), part, start=True, stop=True)\
                          .then_inc(*sig("summed").up())
                    pe.wait_ge(*sig("part_sum").at(1 + center))
                    nc.tensor.matmul(ps[:, 1, :], const("ones"), part2, start=True, stop=True)\
                      .then_inc(*sig("summed").up())

                @block.scalar
                def _(act):
                    if center:
                        act.wait_ge(*sig("centered").at(1))
                    nc.scalar.activation(sq, dst if center else src, ACT.Square).then_inc(*sig("squared").up())
                    act.wait_ge(*sig("variance").at(1))
                    nc.scalar.activation(std, var, ACT.Sqrt).then_inc(*sig("deviation").up())
                    if gain is not None:
                        act.wait_ge(*sig("normed").at(1))
                        for k in range(kt):
                            nc.scalar.activation(dst[:, k, :], dst[:, k, :], func, scale=gain(k),
                                                 bias=bias(k) if bias else 0.0)

        rows = sbuf("rows", [P, 4, T])
        part2 = rows[:, 3, :]

        def small_row(i):
            return rows[:, i, :]

        def start():
            xtok = big(2).rearrange("p k t -> p (k t)").rearrange("p (a n) -> p a n", a=TT)
            stage = big(3).rearrange("p k t -> p (k t)")[:, 0:VTILES * P].rearrange("p (a n) -> p a n", a=VTILES)
            with phase() as block:
                @block.gpsimd
                def _(pool):
                    nc.gpsimd.memset(stage, 0.0).then_inc(*sig("stage_zero").up())

                @block.sync
                def _(sp):
                    sp.dma_start(cst[:, :], a["constants"]).then_inc(sig("loaded").handle, 16)
                    sp.dma_start(xtok, a["x"][0].rearrange("(a p) n -> p a n", p=P)).then_inc(sig("loaded").handle, 16)
                    feed(sp, None)

                n = 0
                pieces = []
                for name, rows_ in VECTORS:
                    src = a[name]
                    flat = src.rearrange(" ".join("abcd"[:len(src.shape)]) + " -> (" + " ".join("abcd"[:len(src.shape)]) + ")")
                    v = flat.rearrange("(r p) -> r p", p=P)
                    at, left, r0 = COLUMN[name], rows_, 0
                    while left:
                        m = min(left, P - at % P)
                        pieces.append((at // P, at % P, m, v[r0:r0 + m, :]))
                        at, left, r0 = at + m, left - m, r0 + m

                @block.scalar
                def _(act):
                    act.wait_ge(*sig("stage_zero").at(1))
                    for tile, p0, m, src in pieces:
                        act.dma_start(stage[p0:p0 + m, tile, :], src).then_inc(sig("vectors").handle, 16)

                @block.tensor
                def _(pe):
                    pe.wait_ge(sig("loaded").handle, 32)
                    for k in range(KT):
                        for i in range(TT):
                            last = nc.tensor.transpose(ps[:, k % 4, i * P:(i + 1) * P], xtok[:, i, k * P:(k + 1) * P], ident)
                        last.then_inc(*sig("turned").up())
                        if k >= 3:
                            pe.wait_ge(sig("turned_out").handle, k - 2)
                    pe.wait_ge(sig("vectors").handle, 16 * len(pieces))
                    for i in range(VTILES):
                        last = nc.tensor.transpose(ps[:, 4 + i // 4, (i % 4) * P:(i % 4 + 1) * P], stage[:, i, :], ident)
                    last.then_inc(*sig("turned").up())

                @block.vector
                def _(dve):
                    for k in range(KT):
                        dve.wait_ge(*sig("turned").at(k + 1))
                        nc.vector.tensor_copy(X[:, k, :], ps[:, k % 4, :]).then_inc(*sig("turned_out").up())
                    dve.wait_ge(*sig("turned").at(KT + 1))
                    nc.vector.tensor_copy(cols[:, :], ps[:, 4:6, :].rearrange("p a n -> p (a n)")[:, 0:VTILES * P])
                    for i in range(2):
                        nc.vector.memset(small[:, i:i + 1], 0.0).then_inc(sig("hidden_done").handle, 1)

        def finish():
            otok = big(2).rearrange("p k t -> p (k t)").rearrange("p (a n) -> p a n", a=TT)
            with phase() as block:
                @block.tensor
                def _(pe):
                    for n in range(8):
                        i, half = n // 2, n % 2
                        if n >= 4:
                            pe.wait_ge(*sig("turned_out").at(n - 3))
                        for k in range(4):
                            last = nc.tensor.transpose(ps[:, n % 4, k * P:(k + 1) * P],
                                                       X[:, half * 4 + k, i * P:(i + 1) * P], ident)
                        last.then_inc(*sig("turned").up())

                @block.vector
                def _(dve):
                    for n in range(8):
                        dve.wait_ge(*sig("turned").at(n + 1))
                        nc.vector.tensor_copy(otok[:, n // 2, (n % 2) * 512:(n % 2) * 512 + 512], ps[:, n % 4, :])\
                          .then_inc(*sig("turned_out").up())

                @block.sync
                def _(sp):
                    for i in range(TT):
                        sp.wait_ge(*sig("turned_out").at(2 * i + 2))
                        sp.dma_start(out[0, i * P:(i + 1) * P, :], otok[:, i, :]).then_inc(sig("stored").handle, 16)
                    sp.wait_ge(sig("stored").handle, 16 * TT)

        def products(jobs):
            with phase() as block:
                @block.sync
                def _(sp):
                    feed(sp, jobs[-1][0])

                @block.tensor
                def _(pe):
                    for name, x, _, _ in jobs:
                        mm_gemm(pe, name, x)

                @block.scalar
                def _(act):
                    for name, _, who, fn in jobs:
                        if who == "act":
                            take(act, name, "tile_act", range(len(plan[name].tiles)), fn)

                @block.vector
                def _(dve):
                    for name, _, who, fn in jobs:
                        if who == "dve":
                            take(dve, name, "tile_dve", range(len(plan[name].tiles)), fn)

        def to(view, func=ACT.Identity, first=0, bias=None, scale=1.0):
            def fn(u, t, bank, nt=None):
                m = u * fn.nt + (first + t)
                b = bias(m) if bias else 0.0
                return nc.scalar.activation(at_tile(view, m), ps[:, bank, :], func, bias=b, scale=scale)
            return fn

        def nt_of(name, fn):
            fn.nt = len(plan[name].tiles)
            return fn

        def fjob(name, x, view, func=ACT.Identity, bias=None):
            return name, x, "act", nt_of(name, to(view, func, bias=bias))

        def tjob(name, x, view, func=ACT.Identity):
            def fn(u, t, bank):
                return nc.scalar.activation(view[:, t, bass.ds(u * 256, 256)] if not isinstance(u, int)
                                            else view[:, t, u * 256:u * 256 + 256], ps[:, bank, 0:256], func)
            return name, x, "act", fn

        def resjob(name, x, gain=None, alpha=1.0):
            nt = len(plan[name].tiles)

            def fn(u, t, bank):
                m = u * nt + t
                xt = at_tile(X, m)
                if gain is None:
                    return nc.vector.scalar_tensor_tensor(xt, xt, alpha, ps[:, bank, :], ALU.mult, ALU.add)
                return nc.vector.scalar_tensor_tensor(xt, ps[:, bank, :], gain(m), xt, ALU.mult, ALU.add)
            return name, x, "dve", fn

        HIDDEN = arena[:, 2:5, :, :].rearrange("p a k t -> p (a k) t")[:, 0:HT, :]
        FBUF = arena[:, 5, :, :]

        def ffn_phase(tag, kind, taps=None, tap_bias=None, gain=None, alpha=1.0):
            g = plan[tag + "_in"]
            b = g.base
            rj = resjob(tag + "_out", None, gain, alpha)
            with phase() as block:
                @block.sync
                def _(sp):
                    feed(sp, tag + "_out")

                @block.tensor
                def _(pe):
                    mm_gemm(pe, tag + "_in", lambda k: H[:, k, :])
                    if kind == "conv":
                        pe.wait_ge(sig("hidden_done").handle, g.end["hidden_done"])
                    else:
                        pe.wait_ge(sig("tile_dve").handle, g.end["tile_dve"])
                    mm_gemm(pe, tag + "_out", lambda k: HIDDEN[:, k, :])

                @block.scalar
                def _(act):
                    def emit(u, j):
                        gate, up = bank_of(g, j, 0), bank_of(g, j, 1)
                        act.wait_ge(tiles_done.handle, b["tiles"] + u * 2 + 1)
                        if kind == "swiglu":
                            act.wait_ge(sig("tile_dve").handle, b["tile_dve"] - 1 + u)
                            nc.scalar.activation(FBUF[:, j % 2, :], ps[:, gate, :], ACT.Silu)\
                              .then_inc(sig("tile_act").handle, 1)
                            return
                        nt = 2 if kind == "conv" else 1
                        if kind == "conv":
                            act.wait_ge(sig("hidden_done").handle, b["hidden_done"] - 1 + u)
                        else:
                            act.wait_ge(sig("tile_dve").handle, b["tile_dve"] - 2 + u * 2)
                        for t in range(nt):
                            act.wait_ge(tiles_done.handle, b["tiles"] + u * 2 + (t + 1))
                            m = u + HT * t
                            nc.scalar.activation(FBUF[:, 2 * (j % 2) + t, :], ps[:, bank_of(g, j, t), :], ACT.Identity,
                                                 scale=taps(2, m), bias=tap_bias(m)).then_inc(sig("tap_act").handle, 1)
                        act.wait_ge(sig("tile_dve").handle, b["tile_dve"] + u * 2 + 1)
                        nc.scalar.activation(FBUF[:, 4 + j % 2, :], FBUF[:, 2 * (j % 2), :],
                                             ACT.Silu if kind == "conv" else GELU).then_inc(sig("gate_act").handle, 1)
                    units(act, g, emit)

                @block.vector
                def _(dve):
                    if gain is not None or alpha != 1.0:
                        if gain is not None:
                            nc.vector.tensor_scalar(X, X, ALPHA, None, ALU.mult).then_inc(*sig("scaled").up())
                            dve.wait_ge(*sig("scaled").at(1))

                    def emit(u, j):
                        gate, up = bank_of(g, j, 0), bank_of(g, j, 1)
                        hid = at_tile(HIDDEN, u)
                        if kind == "swiglu":
                            dve.wait_ge(sig("tile_act").handle, b["tile_act"] + u + 1)
                            dve.wait_ge(tiles_done.handle, b["tiles"] + u * 2 + 2)
                            nc.vector.tensor_tensor(hid, FBUF[:, j % 2, :], ps[:, up, :], ALU.mult)\
                              .then_inc(sig("tile_dve").handle, 1)
                            return
                        nt = 2 if kind == "conv" else 1
                        for t in range(nt):
                            m = u + HT * t
                            c = FBUF[:, 2 * (j % 2) + t, :]
                            bank = bank_of(g, j, t)
                            dve.wait_ge(sig("tap_act").handle, b["tap_act"] + u * nt + (t + 1))
                            nc.vector.scalar_tensor_tensor(c[:, 1:T], ps[:, bank, 0:T - 1], taps(1, m), c[:, 1:T],
                                                           ALU.mult, ALU.add).then_inc(sig("tap_step").handle, 1)
                            dve.wait_ge(sig("tap_step").handle, b["tap_step"] + u * nt + (t + 1))
                            nc.vector.scalar_tensor_tensor(c[:, 2:T], ps[:, bank, 0:T - 2], taps(0, m), c[:, 2:T],
                                                           ALU.mult, ALU.add).then_inc(sig("tile_dve").handle, 1)
                        dve.wait_ge(sig("gate_act").handle, b["gate_act"] + u + 1)
                        if kind == "conv":
                            dve.wait_ge(sig("tile_dve").handle, b["tile_dve"] + u * 2 + 2)
                            nc.vector.tensor_tensor(hid, FBUF[:, 4 + j % 2, :], FBUF[:, 2 * (j % 2) + 1, :], ALU.mult)\
                              .then_inc(sig("hidden_done").handle, 1)
                        else:
                            dve.wait_ge(tiles_done.handle, b["tiles"] + u * 2 + 2)
                            nc.vector.tensor_tensor(hid, FBUF[:, 4 + j % 2, :], ps[:, up, :], ALU.mult)\
                              .then_inc(sig("tile_dve").handle, 1)
                    units(dve, g, emit)
                    take(dve, tag + "_out", "tile_dve", [0], rj[3])

        GELU = ACT.Gelu_apprx_tanh
        def flat(view):
            return view.rearrange("p k t -> p (k t)")

        def merge_job(name, x, gate, total=None):
            nt = len(plan[name].tiles)

            def fn(u, t, bank):
                m = u * nt + t
                first = nc.vector.tensor_tensor(gate[:, m, :], gate[:, m, :], ps[:, bank, :], ALU.mult)
                if total is None:
                    return first
                first.then_inc(*sig("merge_step").up())
                nc.vector.wait_ge(sig("merge_step").handle, sig("merge_step").total)
                return nc.vector.tensor_tensor(total[:, m, :], total[:, m, :], gate[:, m, :], ALU.add)
            return name, x, "dve", fn

        PACK = [0, 512, 1024, 896]
        WIDE = [T - P * j for j in range(TT)]
        CAUSAL = sum(WIDE)

        def modulation():
            act_c = small[:, 0:8]
            g = plan["ada"]
            with phase() as block:
                @block.sync
                def _(sp):
                    feed(sp, "ada")

                @block.scalar
                def _(act):
                    nc.scalar.activation(act_c, cols[:, COLUMN["c"]:COLUMN["c"] + KT], ACT.Silu)\
                      .then_inc(*sig("c_ready").up())

                @block.tensor
                def _(pe):
                    pe.wait_ge(*sig("c_ready").at(1))
                    mm_gemm(pe, "ada", lambda k: act_c[:, k:k + 1])

                @block.vector
                def _(dve):
                    dve.wait_ge(tiles_done.handle, g.end["tiles"])
                    step = stepper(dve, "mod_step")
                    step(nc.vector.tensor_tensor(mod[:, :], ps[:, 4, 0:48],
                                                 cols[:, COLUMN["b_ada"]:COLUMN["b_ada"] + 48], ALU.add))
                    for part in (1, 2, 4, 5):
                        v = mod[:, part * KT:part * KT + KT]
                        nc.vector.tensor_scalar(v, v, 1.0, None, ALU.add)

        def mod_col(part):
            def at(k):
                i = part * KT + k
                return mod[:, i:i + 1] if isinstance(i, int) else mod[:, bass.ds(i, 1)]
            return at

        def stick_breaking(QK, V, out_view):
            scale = 64 ** -0.5
            f7, f8 = flat(big(7)), flat(big(8))
            LB = [f7[:, 0:CAUSAL], f7[:, CAUSAL:2 * CAUSAL]]
            OM = [f7[:, 2 * CAUSAL:3 * CAUSAL], f8[:, 0:CAUSAL]]
            EX = [f8[:, CAUSAL:2 * CAUSAL], f8[:, 2 * CAUSAL:3 * CAUSAL]]
            Z = ps[:, 0:3, :].rearrange("p b n -> p (b n)")
            AFTER = ps[:, 3:6, :].rearrange("p b n -> p (b n)")
            with phase() as block:
                @block.tensor
                def _(pe):
                    def scores(h):
                        r = 64 * (h % 2)
                        if h:
                            pe.wait_ge(*sig("scores_taken").at(h))
                        for j in range(TT):
                            last = nc.tensor.matmul(Z[:, PACK[j]:PACK[j] + WIDE[j]],
                                                    QK[r:r + 64, 4 + h // 2, j * P:(j + 1) * P],
                                                    QK[r:r + 64, h // 2, j * P:T], start=True, stop=True)
                        last.then_inc(*sig("scores_ready").up())
                    scores(0)
                    for h in range(8):
                        r = 64 * (h % 2)
                        if h + 1 < 8:
                            scores(h + 1)
                        pe.wait_ge(*sig("stick_ready").at(h + 1))
                        if h:
                            pe.wait_ge(*sig("weight_ready").at(h))
                        om = OM[h % 2]
                        for i in range(TT):
                            for j in range(i, TT):
                                last = nc.tensor.matmul(
                                    AFTER[:, PACK[i] + P * (j - i):PACK[i] + WIDE[i]],
                                    const("later" if i == j else "ones"),
                                    om[:, PACK[j]:PACK[j] + WIDE[j]], start=j == i, stop=j == TT - 1)
                        last.then_inc(*sig("after_ready").up())
                        pe.wait_ge(*sig("weight_masked").at(h + 1))
                        if h >= 2:
                            pe.wait_ge(*sig("head_out").at(h - 1))
                        for j in range(TT):
                            last = nc.tensor.matmul(ps[r:r + 64, 6 + h % 2, j * P:T], V[:, j, 64 * h:64 * h + 64],
                                                    EX[h % 2][:, PACK[j]:PACK[j] + WIDE[j]],
                                                    start=j == 0, stop=j == TT - 1)
                        last.then_inc(*sig("values_ready").up())

                @block.scalar
                def _(act):
                    step = stepper(act, "act_step")
                    for h in range(8):
                        ex = EX[h % 2]
                        act.wait_ge(*sig("scores_taken").at(h + 1))
                        if h >= 2:
                            act.wait_ge(*sig("values_ready").at(h - 1))
                        step(nc.scalar.activation(ex, OM[h % 2], ACT.Abs))
                        step(nc.scalar.activation(ex, ex, ACT.Exp, scale=-1.0))
                        nc.scalar.activation(ex, ex, ACT.Ln, bias=1.0).then_inc(*sig("soft_ready").up())
                        act.wait_ge(*sig("log_weight").at(h + 1))
                        nc.scalar.activation(ex, LB[h % 2], ACT.Exp).then_inc(*sig("weight_ready").up())

                @block.vector
                def _(dve):
                    step = stepper(dve, "dve_step")
                    for h in range(8):
                        lb, om, ex = LB[h % 2], OM[h % 2], EX[h % 2]
                        dve.wait_ge(*sig("scores_ready").at(h + 1))
                        nc.vector.tensor_scalar(om, Z[:, 0:CAUSAL], scale, None, ALU.mult)\
                          .then_inc(*sig("scores_taken").up())
                        dve.wait_ge(*sig("soft_ready").at(h + 1))
                        step(nc.vector.scalar_tensor_tensor(lb, om, 0.0, ex, ALU.min, ALU.subtract))
                        step(nc.vector.tensor_tensor(om, lb, om, ALU.subtract))
                        for j in range(TT):
                            d = om[:, PACK[j]:PACK[j] + P]
                            last = nc.vector.tensor_tensor(d, d, const("before"), ALU.mult)
                        last.then_inc(*sig("stick_ready").up())
                        dve.wait_ge(*sig("after_ready").at(h + 1))
                        nc.vector.tensor_tensor(lb, lb, AFTER[:, 0:CAUSAL], ALU.add).then_inc(*sig("log_weight").up())
                        dve.wait_ge(*sig("weight_ready").at(h + 1))
                        for j in range(TT):
                            d = ex[:, PACK[j]:PACK[j] + P]
                            last = nc.vector.tensor_tensor(d, d, const("before"), ALU.mult)
                        last.then_inc(*sig("weight_masked").up())
                        dve.wait_ge(*sig("values_ready").at(h + 1))
                        r = 64 * (h % 2)
                        nc.vector.tensor_copy(out_view[r:r + 64, h // 2, :], ps[r:r + 64, 6 + h % 2, :])\
                          .then_inc(*sig("head_out").up())

        def block1():
            c1 = lambda n: (lambda k: col(n, k))
            modulation()
            normalize(X, H, KT, True, LN_EPS, gain=mod_col(1), bias=mod_col(0))
            QK, U, V = big(2), arena[:, 3, 0:4, :], arena[:, 3, 4:8, :]
            G2 = arena[:, 4:6, :, :].rearrange("p a k t -> p (a k) t")
            hx = lambda k: H[:, k, :]
            products([fjob("qk", hx, QK), tjob("v", hx, V), fjob("u", hx, U),
                      fjob("gates", hx, G2, ACT.Sigmoid)])
            YSB, YS = arena[:, 6, 0:4, :], arena[:, 8, 4:8, :]
            stick_breaking(QK, V, YSB)
            s5(U, YS)
            ACTV, GL = arena[:, 7, 0:4, :], arena[:, 7, 4:8, :]
            with phase() as block:
                @block.vector
                def _(dve):
                    step = stepper(dve, "dve_step")
                    for k in range(4):
                        last = nc.vector.scalar_tensor_tensor(ACTV[:, k, :], U[:, k, :], col("ssm_d", k), YS[:, k, :],
                                                              ALU.mult, ALU.add)
                    last.then_inc(*sig("skip_added").up())

                @block.scalar
                def _(act):
                    act.wait_ge(*sig("skip_added").at(1))
                    nc.scalar.activation(ACTV, ACTV, GELU)
            products([merge_job("sb_up", lambda k: YSB[:, k, :], big(4)),
                      fjob("glu", lambda k: ACTV[:, k, :], GL, ACT.Sigmoid, bias=c1("b_glu"))])
            with phase() as block:
                @block.vector
                def _(dve):
                    nc.vector.tensor_tensor(ACTV, ACTV, GL, ALU.mult)
            products([merge_job("ssm_up", lambda k: ACTV[:, k, :], big(5), big(4))])
            with phase() as block:
                @block.vector
                def _(dve):
                    nc.vector.tensor_scalar(X, X, ALPHA, None, ALU.mult)
            products([resjob("out1", lambda k: big(4)[:, k, :], mod_col(2))])
            normalize(X, X, KT, True, LN_EPS, gain=c1("ln1_g"), bias=c1("ln1_b"))
            normalize(X, H, KT, True, LN_EPS, gain=mod_col(4), bias=mod_col(3))
            ffn_phase("ffn1", "swiglu", gain=mod_col(5))
            normalize(X, X, KT, True, LN_EPS, gain=c1("ln2_g"), bias=c1("ln2_b"))

        def s5(U, YS):
            L, NCH, NP = 8, T // 8, 16

            def words(i, at, n):
                return arena[:, i:i + 2, :, :].rearrange("p a k t -> p (a k t)")[:, at:at + n]

            def v16(i):
                return small[:, 16 + 16 * i:32 + 16 * i]
            (dt, lr, li, kq, red, mag, sn, sh, Lr, Li, den, xr, fr, fi, t0, t1, s2) = (v16(i) for i in range(17))
            L8, L8i, T1, T2 = (small[:, 320 + 32 * i:352 + 32 * i] for i in range(4))
            late = flat(arena[:, 6, 4:8, :])
            BB = late[:, 0:1024].rearrange("p (r j c) -> p r j c", r=2, j=NP)
            Bnat = late[:, 1024:1536].rearrange("p (r j c) -> p r j c", r=2, j=NP)
            Cnat = late[:, 1536:2048].rearrange("p (r m s) -> p r m s", r=2, m=4)
            rowsf = rows[:, :, :].rearrange("p a n -> p (a n)")
            Cpad = rowsf[:, 0:1024].rearrange("p (r m g s) -> p r m g s", r=2, m=4, g=2)
            tA = rowsf[:, 1024:1536].rearrange("p (j c) -> p j c", j=NP)
            tB = rowsf[:, 1536:2048].rearrange("p (j c) -> p j c", j=NP)
            R = words(1, 0, 8192).rearrange("p (r j d c) -> p r j d c", r=2, j=NP, d=L)
            RT = words(7, 0, 8192).rearrange("p (r h j s) -> p r h j s", r=2, h=2, j=NP)
            US = flat(arena[:, 3, 4:8, :]).rearrange("p (h j n) -> p h j n", h=2, j=NP)
            KB = flat(arena[:, 3, 4:8, :]).rearrange("p (b d c) -> p b d c", b=2, d=L)
            HS = words(1, 0, 65 * 32).rearrange("p (n r j) -> p n r j", r=2, j=NP)
            Gn = words(1, 2080, 4608).rearrange("p (d j c) -> p d j c", d=9, j=NP)
            Gr = words(7, 0, 4608).rearrange("p (d j c) -> p d j c", d=9, j=NP)
            C0 = late[:, 1536:2048]
            ldt = rowsf[0:16, 0:2]
            ldtw = rowsf[0:16, 128:256]
            ab = (COLUMN["ssm_a_re"], COLUMN["ssm_a_im"])
            ar, ai = cols[:, ab[0]:ab[0] + 16], cols[:, ab[1]:ab[1] + 16]
            PI2 = 2 * math.pi
            C1 = 6.28125
            C2 = float(np.float32(PI2 - C1) - np.float32(PI2 - C1) % np.float32(2.0 ** -21))
            C3 = float(np.float32(PI2 - C1 - C2))
            MAGIC = 1.5 * 2.0 ** 23
            UV = U.rearrange("p m (n l) -> p m n l", l=L)
            with phase() as block:
                @block.sync
                def _(sp):
                    sp.dma_start(ldt, a["ssm_log_dt"][0].rearrange("(j g) -> j g", g=2)).then_inc(sig("ssm_loaded").handle, 16)
                    for r, (b, c) in enumerate((("ssm_b_re", "ssm_c_re"), ("ssm_b_im", "ssm_c_im"))):
                        sp.dma_start(Bnat[:, r], a[b][0].rearrange("(j g) s c -> (g s) j c", g=2))\
                          .then_inc(sig("ssm_loaded").handle, 16)
                        sp.dma_start(Cnat[:, r], a[c][0].rearrange("g c s -> (g c) s")
                                     .rearrange("(m q) s -> q m s", q=P)).then_inc(sig("ssm_loaded").handle, 16)

                @block.vector
                def _(dve):
                    step = stepper(dve, "dve_step")
                    dve.wait_ge(sig("ssm_loaded").handle, 80)
                    step(nc.vector.tensor_copy(ldtw.rearrange("p (g s) -> p g s", g=2),
                                               ldt.rearrange("p (g s) -> p g s", s=1).broadcast_to([16, 2, 64])))
                    nc.vector.tensor_copy(ldtw, ldtw).then_inc(*sig("dt_rows").up())
                    dve.wait_ge(*sig("dt_ready").at(1))
                    TS, TTT, STT = nc.vector.tensor_scalar, nc.vector.tensor_tensor, nc.vector.scalar_tensor_tensor
                    TTT(lr, ar, dt, ALU.mult)
                    step(TTT(li, ai, dt, ALU.mult))
                    step(TS(kq, li, 1.0 / PI2, MAGIC, ALU.mult, ALU.add))
                    step(TS(kq, kq, MAGIC, None, ALU.subtract))
                    for c in (C1, C2, C3):
                        step(STT(red if c != C1 else red, kq, -c, li if c == C1 else red, ALU.mult, ALU.add))
                    TS(red, red, 3.1415925, -3.1415925, ALU.min, ALU.max).then_inc(*sig("angle_ready").up())
                    dve.wait_ge(*sig("polar_ready").at(1))
                    step(TTT(t0, sh, sh, ALU.mult))
                    step(TS(t0, t0, -2.0, 1.0, ALU.mult, ALU.add))
                    step(TTT(Lr, mag, t0, ALU.mult))
                    step(TTT(Li, mag, sn, ALU.mult))
                    step(TTT(t0, ar, ar, ALU.mult))
                    step(TTT(t1, ai, ai, ALU.mult))
                    step(TTT(den, t0, t1, ALU.add))
                    step(nc.vector.reciprocal(den, den))
                    step(TS(xr, Lr, 1.0, None, ALU.subtract))
                    step(TTT(t0, xr, ar, ALU.mult))
                    step(TTT(t1, Li, ai, ALU.mult))
                    step(TTT(t0, t0, t1, ALU.add))
                    step(TTT(fr, t0, den, ALU.mult))
                    step(TTT(t0, Li, ar, ALU.mult))
                    step(TTT(t1, xr, ai, ALU.mult))
                    step(TTT(t0, t0, t1, ALU.subtract))
                    step(TTT(fi, t0, den, ALU.mult))
                    for r in range(2):
                        for g in range(2):
                            step(TS(Cpad[:, r, :, g, :], Cnat[:, r], const(f"group{g}", 1), None, ALU.mult))
                    nc.vector.tensor_copy(s2, fr).then_inc(*sig("c_padded").up())
                    step(nc.vector.memset(BB, 0.0))
                    for g in range(2):
                        q = slice(64 * g, 64 * g + 64)
                        c = slice(16 * g, 16 * g + 16)
                        br, bi = Bnat[q, 0], Bnat[q, 1]
                        FR, FI = bl(fr[q], 16), bl(fi[q], 16)
                        step(TTT(tA[q, :, 0:16], br, FR, ALU.mult))
                        step(TTT(tB[q, :, 0:16], bi, FI, ALU.mult))
                        step(TTT(BB[q, 0, :, c], tA[q, :, 0:16], tB[q, :, 0:16], ALU.subtract))
                        step(TTT(tA[q, :, 0:16], br, FI, ALU.mult))
                        step(TTT(tB[q, :, 0:16], bi, FR, ALU.mult))
                        step(TTT(BB[q, 1, :, c], tA[q, :, 0:16], tB[q, :, 0:16], ALU.add))
                    for r in range(2):
                        step(nc.vector.tensor_copy(R[:, r, :, 0, :], BB[:, r]))
                    LR, LI = bl(Lr, 32), bl(Li, 32)
                    for d in range(1, L):
                        pr, pi = R[:, 0, :, d - 1, :], R[:, 1, :, d - 1, :]
                        step(TTT(tA, pr, LR, ALU.mult))
                        step(TTT(tB, pi, LI, ALU.mult))
                        step(TTT(R[:, 0, :, d, :], tA, tB, ALU.subtract))
                        step(TTT(tA, pr, LI, ALU.mult))
                        step(TTT(tB, pi, LR, ALU.mult))
                        step(TTT(R[:, 1, :, d, :], tA, tB, ALU.add))
                    nc.vector.tensor_copy(s2, fr).then_inc(*sig("powers_ready").up())
                    cr, ci = Lr, Li
                    er, ei = xr, mag
                    for _ in range(3):
                        step(TTT(t0, cr, cr, ALU.mult))
                        step(TTT(t1, ci, ci, ALU.mult))
                        step(TTT(s2, cr, ci, ALU.mult))
                        step(TTT(er, t0, t1, ALU.subtract))
                        step(TS(ei, s2, 2.0, None, ALU.mult))
                        cr, ci = er, ei
                    step(nc.vector.tensor_copy(L8[:, 0:16], cr))
                    step(nc.vector.tensor_copy(L8[:, 16:32], cr))
                    step(TS(L8i[:, 0:16], ci, -1.0, None, ALU.mult))
                    step(nc.vector.tensor_copy(L8i[:, 16:32], ci))
                    dve.wait_ge(*sig("chunks_in").at(1))
                    step(nc.vector.memset(HS[:, 0], 0.0))
                    for r in range(2):
                        step(nc.vector.tensor_copy(HS[:, 1:65, r, :].rearrange("p n j -> p j n"),
                                                   ps[:, 4 + 2 * r:6 + 2 * r, :].rearrange("p b (j n) -> p (b j) n", n=64)))
                    nc.vector.memset(KB, 0.0).then_inc(*sig("states_in").up())
                    base = sig("scan_step").total
                    with dve.Fori(0, NCH - 2) as i:
                        def state(k, lo, hi):
                            return HS.rearrange("p n r j -> p n (r j)")[:, bass.ds(i + k, 1), lo:hi]\
                                .rearrange("p a c -> p (a c)")
                        h = sig("scan_step").handle
                        nc.vector.tensor_tensor(T1, state(1, 0, 32), L8, ALU.mult).then_inc(h, 1)
                        nc.vector.tensor_tensor(T2[:, 0:16], state(1, 16, 32), L8i[:, 0:16], ALU.mult).then_inc(h, 1)
                        nc.vector.tensor_tensor(T2[:, 16:32], state(1, 0, 16), L8i[:, 16:32], ALU.mult).then_inc(h, 1)
                        dve.wait_ge(h, i * 5 + (base + 3))
                        nc.vector.tensor_tensor(T2, T1, T2, ALU.add).then_inc(h, 1)
                        dve.wait_ge(h, i * 5 + (base + 4))
                        nc.vector.tensor_tensor(state(2, 0, 32), state(2, 0, 32), T2, ALU.add).then_inc(h, 1)
                        dve.wait_ge(h, i * 5 + (base + 5))
                    sig("scan_step").total += 5 * (NCH - 2)
                    nc.vector.tensor_copy(s2, fr).then_inc(*sig("scanned").up())
                    for m in range(4):
                        dve.wait_ge(*sig("kernel_ready").at(m + 1))
                        if m >= 2:
                            dve.wait_ge(*sig("inside_done").at(m - 1))
                        for q in range(4):
                            w = slice(32 * q, 32 * q + 32)
                            last = nc.vector.tensor_copy(KB[w, m % 2, :, w],
                                                         ps[w, m % 2, 0:256].rearrange("p (d c) -> p d c", d=L))
                        last.then_inc(*sig("kernel_out").up())

                @block.scalar
                def _(act):
                    act.wait_ge(*sig("dt_turned").at(1))
                    nc.scalar.activation(dt, ps[:, 0, 0:16], ACT.Exp).then_inc(*sig("dt_ready").up())
                    act.wait_ge(*sig("angle_ready").at(1))
                    nc.scalar.activation(mag, lr, ACT.Exp)
                    nc.scalar.activation(sn, red, ACT.Sin)
                    nc.scalar.activation(sh, red, ACT.Sin, scale=0.5).then_inc(*sig("polar_ready").up())
                    for d in range(L):
                        for q in range(4):
                            last = nc.scalar.activation(
                                US[32 * (d % 4):32 * (d % 4) + 32, d // 4].rearrange("p (m r) n -> p r m n", r=4)[:, q],
                                UV[32 * q:32 * q + 32, :, :, L - 1 - d], ACT.Copy)
                    last.then_inc(*sig("steps_stacked").up())
                    for n in range(16):
                        r, h, j = n // 8, n // 4 % 2, 4 * (n % 4)
                        act.wait_ge(*sig("power_turned").at(n + 1))
                        nc.scalar.activation(RT[:, r, h, j:j + 4, :].rearrange("p j s -> p (j s)"), ps[:, n % 4, :],
                                             ACT.Copy).then_inc(*sig("power_out").up())
                    act.wait_ge(*sig("c_turned").at(1))
                    nc.scalar.activation(Gr[:, 0].rearrange("p j c -> p (j c)"), ps[:, 0, :], ACT.Copy)
                    nc.scalar.activation(Gn[:, 0].rearrange("p j c -> p (j c)"), ps[:, 1, :], ACT.Copy, scale=-1.0)\
                      .then_inc(*sig("g_first").up())
                    for m in range(4):
                        act.wait_ge(*sig("y_ready").at(m + 1))
                        nc.scalar.activation(YS[:, m, :], ps[:, 4 + m, :], ACT.Copy)

                @block.gpsimd
                def _(pool):
                    step = stepper(pool, "pool_step")
                    pool.wait_ge(*sig("g_first").at(1))
                    pool.wait_ge(*sig("powers_ready").at(1))
                    LR, LI = bl(Lr, 32), bl(Li, 32)
                    TTT = nc.gpsimd.tensor_tensor
                    for d in range(1, L + 1):
                        step(TTT(tA, Gr[:, d - 1], LR, ALU.mult))
                        step(TTT(tB, Gn[:, d - 1], LI, ALU.mult))
                        step(TTT(Gr[:, d], tA, tB, ALU.add))
                        step(TTT(tA, Gn[:, d - 1], LR, ALU.mult))
                        step(TTT(tB, Gr[:, d - 1], LI, ALU.mult))
                        last = TTT(Gn[:, d], tA, tB, ALU.subtract)
                        if d < L:
                            step(last)
                    last.then_inc(*sig("g_ready").up())

                @block.tensor
                def _(pe):
                    pe.wait_ge(*sig("dt_rows").at(1))
                    nc.tensor.transpose(ps[:, 0, 0:16], ldtw, ident[0:16, 0:16]).then_inc(*sig("dt_turned").up())
                    pe.wait_ge(*sig("powers_ready").at(1))
                    for n in range(16):
                        r, h, j = n // 8, n // 4 % 2, 4 * (n % 4)
                        if n >= 4:
                            pe.wait_ge(*sig("power_out").at(n - 3))
                        for q in range(4):
                            last = nc.tensor.transpose(ps[:, n % 4, q * P:(q + 1) * P],
                                                       R[:, r, j + q, 4 * h:4 * h + 4, :].rearrange("p d c -> p (d c)"), ident)
                        last.then_inc(*sig("power_turned").up())
                    pe.wait_ge(*sig("steps_stacked").at(1))
                    pe.wait_ge(*sig("power_out").at(16))
                    for r in range(2):
                        for j in range(NP):
                            for h in range(2):
                                last = nc.tensor.matmul(ps[:, 4 + 2 * r + j // 8, 64 * (j % 8):64 * (j % 8) + 64],
                                                        RT[:, r, h, j, :], US[:, h, j, :], start=h == 0, stop=h == 1)
                    last.then_inc(*sig("chunks_in").up())
                    pe.wait_ge(*sig("chunks_in").at(1))
                    for r in range(2):
                        for m in range(4):
                            last = nc.tensor.transpose(ps[:, r, m * P:(m + 1) * P],
                                                       Cpad[:, r, m].rearrange("p g s -> p (g s)"), ident)
                    last.then_inc(*sig("c_turned").up())
                    pe.wait_ge(*sig("g_ready").at(1))
                    pe.wait_ge(*sig("states_in").at(1))

                    def kernels(m):
                        if m >= 2:
                            pe.wait_ge(*sig("kernel_out").at(m - 1))
                        for q in range(4):
                            o = ps[32 * q:32 * q + 32, m % 2, 0:256]
                            nc.tensor.matmul(o, BB[:, 0, 4 * m + q, :], Gr[:, 0:L, 4 * m + q, :], start=True, stop=False)
                            last = nc.tensor.matmul(o, BB[:, 1, 4 * m + q, :], Gn[:, 0:L, 4 * m + q, :], start=False, stop=True)
                        last.then_inc(*sig("kernel_ready").up())
                    kernels(0)
                    for m in range(4):
                        if m < 3:
                            kernels(m + 1)
                        y = ps[:, 4 + m, :].rearrange("p (n l) -> p n l", l=L)
                        pe.wait_ge(*sig("kernel_out").at(m + 1))
                        pe.wait_ge(*sig("scanned").at(1))
                        for d in range(L):
                            last = nc.tensor.matmul(y[:, :, d:L], KB[:, m % 2, d, :], UV[:, m, :, 0:L - d],
                                                    start=d == 0, stop=False, skip_group_check=True)
                        last.then_inc(*sig("inside_done").up())
                        for q in range(4):
                            for t in range(L):
                                for G, r in ((Gr, 0), (Gn, 1)):
                                    last = nc.tensor.matmul(y[32 * q:32 * q + 32, :, t], G[:, t + 1, 4 * m + q, :],
                                                            HS[:, 0:NCH, r, 4 * m + q], start=False, stop=True,
                                                            skip_group_check=True)
                        last.then_inc(*sig("y_ready").up())
        def gla(AQ, AK, V, ALR, W2, AR, OUT):
            NC = T // 64
            B, DM, DL = arena[:, 5, 0:2, :], arena[:, 5, 2:4, :], arena[:, 5, 4:6, :]
            E1, E2, E3, E4 = (arena[:, 7, 2 * i:2 * i + 2, :] for i in range(4))
            QD, KD, KE, QE = (arena[:, 6, 2 * i:2 * i + 2, :] for i in range(4))
            KTOK = flat(arena[:, 8, 4:6, :]).rearrange("p (m i c) -> p m i c", m=2, i=TT)
            ATT = arena[:, 5, 4:8, :]
            S = flat(arena[:, 8, 0:4, :]).rearrange("p (m n v) -> p m n v", m=2, n=NC)
            O, SQ = arena[:, 7, 0:4, :], arena[:, 7, 4:8, :]
            VAR = arena[:, 6, 0:4, :]

            def ch(v):
                return v.rearrange("p m (n l) -> p (m n) l", l=64)

            def point(v, k):
                return ch(v)[:, :, k:k + 1].broadcast_to([P, 2 * NC, 64])
            with phase() as block:
                @block.sync
                def _(sp):
                    sp.dma_start(W2, a["gla_w_a2_2"][0]).then_inc(sig("gate_w").handle, 16)

                @block.tensor
                def _(pe):
                    pe.wait_ge(sig("gate_w").handle, 16)
                    for m in range(2):
                        last = nc.tensor.matmul(ps[:, m, :], W2[:, m * P:m * P + P], ALR, start=True, stop=True)
                    last.then_inc(*sig("decay_in").up())
                    pe.wait_ge(*sig("gla_factors").at(1))
                    for m in range(2):
                        for i in range(TT):
                            last = nc.tensor.transpose(ps[:, 2 + m, i * P:i * P + P], KE[:, m, i * P:i * P + P], ident)
                    last.then_inc(*sig("k_turned").up())
                    for h in range(4):
                        r = 64 * (h % 2)
                        for i in range(TT):
                            w = slice(i * P, i * P + P)
                            last = nc.tensor.matmul(ps[:, 4 + h, w], KD[r:r + 64, h // 2, w], QD[r:r + 64, h // 2, w],
                                                    start=True, stop=True)
                    last.then_inc(*sig("gla_scores").up())
                    pe.wait_ge(*sig("k_tok").at(1))
                    for m in range(2):
                        for n in range(NC - 1):
                            q = slice(64 * (n % 2), 64 * (n % 2) + 64)
                            for g in range(2):
                                h = 2 * m + g
                                last = nc.tensor.matmul(ps[64 * g:64 * g + 64, 2 * m + n % 2, P * (n // 2):P * (n // 2) + P],
                                                        KTOK[q, m, n // 2, 64 * g:64 * g + 64],
                                                        V[q, n // 2, h * P:h * P + P], start=True, stop=True)
                    last.then_inc(*sig("state_adds").up())
                    pe.wait_ge(*sig("att_masked").at(1))
                    pe.wait_ge(*sig("states_ready").at(1))
                    for h in range(4):
                        r = 64 * (h % 2)
                        for i in range(TT):
                            nc.tensor.matmul(ps[:, 4 + h, i * P:i * P + P], V[:, i, h * P:h * P + P],
                                             ATT[:, h, i * P:i * P + P], start=True, stop=False, skip_group_check=True)
                            for n in (2 * i, 2 * i + 1):
                                last = nc.tensor.matmul(ps[:, 4 + h, 64 * n:64 * n + 64], S[r:r + 64, h // 2, n, :],
                                                        QE[r:r + 64, h // 2, 64 * n:64 * n + 64],
                                                        start=False, stop=True, skip_group_check=True)
                    last.then_inc(*sig("heads_ready").up())
                    pe.wait_ge(*sig("heads_squared").at(1))
                    for h in range(4):
                        last = nc.tensor.matmul(ps[:, h, :], const("ones"), SQ[:, h, :], start=True, stop=True)
                    last.then_inc(*sig("heads_summed").up())

                @block.scalar
                def _(act):
                    step = stepper(act, "act_step")
                    act.wait_ge(*sig("decay_in").at(1))
                    for m in range(2):
                        last = nc.scalar.activation(DM[:, m, :], ps[:, m, :], ACT.Identity, bias=col("gla_b_a_2", m))
                    step(last)
                    step(nc.scalar.activation(DL, DM, ACT.Abs))
                    step(nc.scalar.activation(DL, DL, ACT.Exp, scale=-1.0))
                    nc.scalar.activation(DL, DL, ACT.Ln, bias=1.0).then_inc(*sig("soft_ready").up())
                    act.wait_ge(*sig("decays_ready").at(1))
                    nc.scalar.activation(E1, DM, ACT.Exp)
                    nc.scalar.activation(E2, DM, ACT.Exp, scale=-1.0)
                    nc.scalar.activation(E3, DL, ACT.Exp, scale=-1.0)
                    nc.scalar.activation(E4, B, ACT.Exp).then_inc(*sig("exps_ready").up())
                    act.wait_ge(*sig("k_turned").at(1))
                    nc.scalar.activation(KTOK.rearrange("p m i c -> p (m i c)"),
                                         ps[:, 2:4, :].rearrange("p b n -> p (b n)"), ACT.Copy).then_inc(*sig("k_tok").up())
                    act.wait_ge(*sig("heads_ready").at(1))
                    nc.scalar.activation(SQ, ps[:, 4:8, :], ACT.Square).then_inc(*sig("heads_squared").up())
                    act.wait_ge(*sig("variance").at(1))
                    nc.scalar.activation(VAR, VAR, ACT.Sqrt).then_inc(*sig("deviation").up())

                @block.vector
                def _(dve):
                    step = stepper(dve, "dve_step")
                    dve.wait_ge(*sig("soft_ready").at(1))
                    step(nc.vector.tensor_scalar(DM, DM, 0.0, None, ALU.min))
                    step(nc.vector.tensor_tensor(DM, DM, DL, ALU.subtract))
                    step(nc.vector.tensor_scalar(DM, DM, 1.0 / 16.0, None, ALU.mult))
                    for m in range(2):
                        step(nc.vector.tensor_tensor_scan(B[:, m, :], const("keep64", T), DM[:, m, :], 0.0, ALU.mult, ALU.add))
                    step(nc.vector.tensor_tensor(ch(DM), ch(B), point(B, 32), ALU.subtract))
                    nc.vector.tensor_tensor(ch(DL), ch(B), point(B, 63), ALU.subtract).then_inc(*sig("decays_ready").up())
                    dve.wait_ge(*sig("exps_ready").at(1))
                    nc.vector.scalar_tensor_tensor(QD, AQ, 0.125, E1, ALU.mult, ALU.mult)
                    nc.vector.tensor_tensor(KD, AK, E2, ALU.mult)
                    nc.vector.tensor_tensor(KE, AK, E3, ALU.mult)
                    nc.vector.scalar_tensor_tensor(QE, AQ, 0.125, E4, ALU.mult, ALU.mult).then_inc(*sig("gla_factors").up())
                    dve.wait_ge(*sig("gla_scores").at(1))
                    m64 = const("chunk64").rearrange("p (a c) -> p a c", a=1).broadcast_to([P, 16, P])
                    nc.vector.tensor_tensor(ATT.rearrange("p h (i c) -> p (h i) c", c=P),
                                            ps[:, 4:8, :].rearrange("p h (i c) -> p (h i) c", c=P), m64, ALU.mult)\
                      .then_inc(*sig("att_masked").up())
                    step(nc.vector.memset(S[:, :, 0, :], 0.0))
                    dve.wait_ge(*sig("state_adds").at(1))
                    for n in range(NC - 1):
                        for m in range(2):
                            last = nc.vector.scalar_tensor_tensor(
                                S[:, m, n + 1, :], S[:, m, n, :], E4[:, m, 64 * n + 63:64 * n + 64],
                                ps[:, 2 * m + n % 2, P * (n // 2):P * (n // 2) + P], ALU.mult, ALU.add)
                        if n < NC - 2:
                            step(last)
                    last.then_inc(*sig("states_ready").up())
                    dve.wait_ge(*sig("heads_summed").at(1))
                    nc.vector.tensor_scalar(VAR, ps[:, 0:4, :], 1.0 / P, RMS_EPS, ALU.mult, ALU.add).then_inc(*sig("variance").up())
                    dve.wait_ge(*sig("deviation").at(1))
                    step(nc.vector.reciprocal(VAR, VAR))
                    step(nc.vector.tensor_tensor(O, ps[:, 4:8, :], VAR, ALU.mult))
                    nc.vector.scalar_tensor_tensor(OUT, O, col("gla_head_g_2", 0), AR, ALU.mult, ALU.mult)

        def rotate(XS):
            TMP = big(5)
            with phase() as block:
                @block.tensor
                def _(pe):
                    for t in range(8):
                        last = nc.tensor.matmul(ps[:, t, :], const("turn"), XS[t // 4][:, t % 4, :], start=True, stop=True)
                    last.then_inc(*sig("turned").up())

                @block.vector
                def _(dve):
                    step = stepper(dve, "dve_step")
                    dve.wait_ge(*sig("turned").at(1))
                    step(nc.vector.tensor_tensor(TMP, ps[:, :, :], bc(const("sin", T), 8), ALU.mult))
                    for v in XS:
                        step(nc.vector.tensor_tensor(v, v, bc(const("cos", T), 4), ALU.mult))
                    for i, v in enumerate(XS):
                        last = nc.vector.tensor_tensor(v, v, TMP[:, 4 * i:4 * i + 4, :], ALU.add)

        MOFF = [0, 128, 384, 768]

        def select_keys(IQ, IK, NB, MASK):
            K, NB3 = TOPK, TT - 1
            f6, f7 = flat(big(6)), flat(big(7))
            SC = [f6[:, 512 * b:512 * b + 512] for b in range(NB3)]
            WK = [f6[:, 1536 + 512 * b:2048 + 512 * b] for b in range(NB3)]
            RL = [f6[:, 3072:3584], f6[:, 3584:4096]]
            ONE, EQ, CUM = (f7[:, 512 * i:512 * i + 512] for i in range(3))
            NS = [P * (b + 2) for b in range(NB3)]
            top = small[:, 0:24]
            cnt = small[:, 24:27]
            iw = small[:, 32:48].rearrange("p (i h) -> p i h", i=TT)
            with phase() as block:
                @block.tensor
                def _(pe):
                    for b in range(NB3):
                        i, ns = 1 + b, NS[b]
                        for h in range(4):
                            r = 64 * (h % 2)
                            if b == 2:
                                pe.wait_ge(*sig("index_relu").at(h + 1))
                            nc.tensor.matmul(ps[:, (4 * b + h) % 8, 0:ns], IQ[r:r + 64, h // 2, i * P:i * P + P],
                                             IK[r:r + 64, 0:ns], start=True, stop=True).then_inc(*sig("index_ready").up())

                @block.scalar
                def _(act):
                    for n in range(4 * NB3):
                        b = n // 4
                        act.wait_ge(*sig("index_ready").at(n + 1))
                        if n >= 2:
                            act.wait_ge(*sig("index_added").at(n - 1))
                        nc.scalar.activation(RL[n % 2][:, 0:NS[b]], ps[:, n % 8, 0:NS[b]], ACT.Relu, scale=0.125)\
                          .then_inc(*sig("index_relu").up())

                @block.vector
                def _(dve):
                    step = stepper(dve, "dve_step")
                    step(nc.vector.tensor_scalar(iw, NB[:, :, 64:68], 0.5, None, ALU.mult))
                    step(nc.vector.memset(ONE, 1.0))
                    step(nc.vector.tensor_copy(MASK[:, 0:P], const("notyet")))
                    for n in range(4 * NB3):
                        b, h = n // 4, n % 4
                        s, rl = SC[b][:, 0:NS[b]], RL[n % 2][:, 0:NS[b]]
                        w = iw[:, 1 + b, h:h + 1]
                        dve.wait_ge(*sig("index_relu").at(n + 1))
                        if h == 0:
                            last = nc.vector.tensor_scalar(s, rl, w, None, ALU.mult)
                        else:
                            last = nc.vector.scalar_tensor_tensor(s, rl, w, s, ALU.mult, ALU.add)
                        last.then_inc(*sig("index_added").up())
                        dve.wait_ge(*sig("index_added").at(n + 1))
                    for b in range(NB3):
                        d = SC[b][:, NS[b] - P:NS[b]]
                        step(nc.vector.tensor_tensor(d, d, const("notyet"), ALU.add))
                        step(nc.vector.tensor_copy(WK[b][:, 0:NS[b]], SC[b][:, 0:NS[b]]))
                    h = sig("top_step")
                    base = h.total
                    with dve.Fori(0, K // 8 - 1) as i:
                        for b in range(NB3):
                            nc.vector.max(top[:, 8 * b:8 * b + 8], WK[b][:, 0:NS[b]]).then_inc(h.handle, 1)
                        dve.wait_ge(h.handle, i * (2 * NB3) + (base + NB3))
                        nc.vector.memset(cnt, 0.0)
                        for b in range(NB3):
                            nc.vector.match_replace(WK[b][:, 0:NS[b]], top[:, 8 * b:8 * b + 8], WK[b][:, 0:NS[b]], NEG)\
                              .then_inc(h.handle, 1)
                        dve.wait_ge(h.handle, i * (2 * NB3) + (base + 2 * NB3))
                    h.total += 2 * NB3 * (K // 8 - 1)
                    for b in range(NB3):
                        ns = NS[b]
                        s, gt, eq, cum = SC[b][:, 0:ns], WK[b][:, 0:ns], EQ[:, 0:ns], CUM[:, 0:ns]
                        m = MASK[:, MOFF[1 + b]:MOFF[1 + b] + ns]
                        step(nc.vector.max(top[:, 8 * b:8 * b + 8], WK[b][:, 0:ns]))
                        th = top[:, 8 * b + 7:8 * b + 8]
                        step(nc.vector.tensor_scalar(gt, s, th, None, ALU.is_gt))
                        step(nc.vector.tensor_scalar(eq, s, th, None, ALU.is_equal))
                        step(nc.vector.tensor_reduce(cnt[:, b:b + 1], gt, AXX, ALU.add))
                        step(nc.vector.tensor_scalar(cnt[:, b:b + 1], cnt[:, b:b + 1], -1.0, float(K), ALU.mult, ALU.add))
                        step(nc.vector.tensor_tensor_scan(cum, ONE[:, 0:ns], eq, 0.0, ALU.mult, ALU.add))
                        step(nc.vector.scalar_tensor_tensor(eq, cum, cnt[:, b:b + 1], eq, ALU.is_le, ALU.mult))
                        step(nc.vector.tensor_tensor(gt, gt, eq, ALU.add))
                        step(nc.vector.tensor_scalar(m, gt, 1.0, -NEG, ALU.subtract, ALU.mult))

        def sparse_attention(BQ, BK, NB, MASK, OUT):
            SOFF = [0, 128, 512, 1024]
            f6, f7, f8 = flat(big(6)), flat(big(7)), flat(big(8))
            SM = [f6[:, 0:CAUSAL], f6[:, CAUSAL:2 * CAUSAL]]
            EX = [f7[:, 0:CAUSAL], f7[:, CAUSAL:2 * CAUSAL]]
            PT = [f8[:, 0:CAUSAL], f8[:, CAUSAL:2 * CAUSAL]]
            S = ps[:, 0:3, :].rearrange("p b n -> p (b n)")
            TP = ps[:, 3:6, :].rearrange("p b n -> p (b n)")
            mx = [small[:, 64 + 4 * i:68 + 4 * i] for i in range(2)]
            nm = [small[:, 72 + 4 * i:76 + 4 * i] for i in range(2)]
            sm = [small[:, 80 + 4 * i:84 + 4 * i] for i in range(2)]
            with phase() as block:
                @block.tensor
                def _(pe):
                    def scores(h):
                        r = 64 * (h % 2)
                        if h:
                            pe.wait_ge(*sig("masked").at(h))
                        for i in range(TT):
                            n = P * (i + 1)
                            last = nc.tensor.matmul(S[:, SOFF[i]:SOFF[i] + n], BQ[r:r + 64, h // 2, i * P:i * P + P],
                                                    BK[r:r + 64, 0:n], start=True, stop=True)
                        last.then_inc(*sig("scores_ready").up())
                    scores(0)
                    for h in range(8):
                        r = 64 * (h % 2)
                        if h < 7:
                            scores(h + 1)
                        pe.wait_ge(*sig("probs_ready").at(h + 1))
                        if h:
                            pe.wait_ge(*sig("probs_out").at(h))
                        for j in range(TT):
                            for i in range(j, TT):
                                last = nc.tensor.transpose(TP[:, PACK[j] + P * (i - j):PACK[j] + P * (i - j) + P],
                                                           EX[h % 2][:, MOFF[i] + j * P:MOFF[i] + j * P + P], ident)
                        last.then_inc(*sig("probs_turned").up())
                        pe.wait_ge(*sig("probs_out").at(h + 1))
                        if h >= 2:
                            pe.wait_ge(*sig("head_out").at(h - 1))
                        for j in range(TT):
                            last = nc.tensor.matmul(ps[r:r + 64, 6 + h % 2, j * P:T], NB[:, j, 0:64],
                                                    PT[h % 2][:, PACK[j]:PACK[j] + WIDE[j]], start=j == 0, stop=j == TT - 1)
                        last.then_inc(*sig("values_ready").up())

                @block.scalar
                def _(act):
                    def turn_out(h):
                        act.wait_ge(*sig("probs_turned").at(h + 1))
                        if h >= 2:
                            act.wait_ge(*sig("values_ready").at(h - 1))
                        nc.scalar.activation(PT[h % 2], TP[:, 0:CAUSAL], ACT.Copy).then_inc(*sig("probs_out").up())
                    for h in range(8):
                        act.wait_ge(*sig("maximum").at(h + 1))
                        if h >= 2:
                            act.wait_ge(*sig("probs_turned").at(h - 1))
                        for i in range(TT):
                            w = slice(MOFF[i], MOFF[i] + P * (i + 1))
                            last = nc.scalar.activation(EX[h % 2][:, w], SM[h % 2][:, w], ACT.Exp, scale=0.125,
                                                        bias=nm[h % 2][:, i:i + 1], accum_out=sm[h % 2][:, i:i + 1])
                        last.then_inc(*sig("exps_ready").up())
                        if h:
                            turn_out(h - 1)
                    turn_out(7)

                @block.vector
                def _(dve):
                    step = stepper(dve, "dve_step")

                    def masked(h):
                        dve.wait_ge(*sig("scores_ready").at(h + 1))
                        if h >= 2:
                            dve.wait_ge(*sig("exps_ready").at(h - 1))
                        for i in range(TT):
                            n = P * (i + 1)
                            w = slice(MOFF[i], MOFF[i] + n)
                            last = nc.vector.tensor_tensor_reduce(
                                out=SM[h % 2][:, w], in0=S[:, SOFF[i]:SOFF[i] + n], in1=MASK[:, w], scale=1.0,
                                scalar=NEG, op0=ALU.add, op1=ALU.max, accum_out=mx[h % 2][:, i:i + 1])
                        last.then_inc(*sig("masked").up())
                        dve.wait_ge(*sig("masked").at(h + 1))
                        nc.vector.tensor_scalar(nm[h % 2], mx[h % 2], -0.125, None, ALU.mult).then_inc(*sig("maximum").up())
                    masked(0)
                    for h in range(8):
                        if h < 7:
                            masked(h + 1)
                        dve.wait_ge(*sig("exps_ready").at(h + 1))
                        step(nc.vector.reciprocal(sm[h % 2], sm[h % 2]))
                        for i in range(TT):
                            w = slice(MOFF[i], MOFF[i] + P * (i + 1))
                            last = nc.vector.tensor_scalar(EX[h % 2][:, w], EX[h % 2][:, w], sm[h % 2][:, i:i + 1],
                                                           None, ALU.mult)
                        last.then_inc(*sig("probs_ready").up())
                        r = 64 * (h % 2)
                        dve.wait_ge(*sig("values_ready").at(h + 1))
                        nc.vector.tensor_copy(OUT[r:r + 64, h // 2, :], ps[r:r + 64, 6 + h % 2, :])\
                          .then_inc(*sig("head_out").up())

        def sgu(U, V):
            f4, f5 = flat(big(4)), flat(big(5))
            GB, BB, BS = f4[:, 0:1024], f4[:, 1024:2048], f4[:, 2048:3072].rearrange("p (g t) -> p g t", g=8)
            WS, WT = (f5[:, 1024 * i:1024 * i + 1024].rearrange("p (g s) -> p g s", g=8) for i in range(2))
            st = small[:, 0:48].rearrange("p (i h s) -> p i h s", i=TT, h=2)
            mv = small[:, 48:56].rearrange("p (i s) -> p i s", i=TT)
            sd = small[:, 56:60]
            TMP = [f5[:, 2048:2560], f5[:, 2560:3072]]
            with phase() as block:
                @block.sync
                def _(sp):
                    for dst, name in ((GB, "sgu_ln_g_2"), (BB, "sgu_ln_b_2")):
                        sp.dma_start(dst, a[name].broadcast_to([P, 1024])).then_inc(sig("sgu_rows").handle, 16)
                    sp.dma_start(f4[:, 2048:3072], a["sgu_b_s_2"].rearrange("a g t -> a (g t)").broadcast_to([P, 1024]))\
                      .then_inc(sig("sgu_rows").handle, 16)
                    sp.dma_start(WS, a["sgu_w_s_2"][0].rearrange("g t s -> t g s")).then_inc(sig("sgu_w").handle, 16)

                @block.tensor
                def _(pe):
                    pe.wait_ge(sig("sgu_w").handle, 16)
                    for g in range(8):
                        last = nc.tensor.transpose(ps[:, g // 4, P * (g % 4):P * (g % 4) + P], WS[:, g, :], ident)
                    last.then_inc(*sig("w_turned").up())
                    pe.wait_ge(*sig("v_normed").at(1))
                    for g in range(8):
                        if g >= 4:
                            pe.wait_ge(*sig("mixed_out").at(g - 3))
                        for i in range(TT):
                            last = nc.tensor.matmul(ps[:, 4 + g % 4, i * P:i * P + P], V[:, i, g * P:g * P + P], WT[:, g, :],
                                                    start=True, stop=True)
                        last.then_inc(*sig("mixed").up())

                @block.scalar
                def _(act):
                    act.wait_ge(*sig("variance").at(1))
                    nc.scalar.activation(sd, sd, ACT.Sqrt).then_inc(*sig("deviation").up())

                @block.vector
                def _(dve):
                    step = stepper(dve, "dve_step")
                    for i in range(TT):
                        for h in range(2):
                            last = nc.vector.bn_stats(st[:, i, h, :], V[:, i, 512 * h:512 * h + 512])
                    step(last)
                    for i in range(TT):
                        last = nc.vector.bn_aggr(mv[:, i, :], st[:, i].rearrange("p h s -> p (h s)"))
                    step(last)
                    nc.vector.tensor_scalar(sd, mv[:, :, 1], LN_EPS, None, ALU.add).then_inc(*sig("variance").up())
                    dve.wait_ge(*sig("w_turned").at(1))
                    nc.vector.tensor_tensor(WT, ps[:, 0:2, :].rearrange("p b (g t) -> p (b g) t", t=P),
                                            bc(const("upto"), 8), ALU.mult)
                    dve.wait_ge(*sig("deviation").at(1))
                    step(nc.vector.reciprocal(sd, sd))
                    for i in range(TT):
                        last = nc.vector.tensor_scalar(V[:, i, :], V[:, i, :], mv[:, i, 0:1], sd[:, i:i + 1],
                                                       ALU.subtract, ALU.mult)
                    step(last)
                    dve.wait_ge(sig("sgu_rows").handle, 48)
                    step(nc.vector.tensor_tensor(V, V, bc(GB, TT), ALU.mult))
                    nc.vector.tensor_tensor(V, V, bc(BB, TT), ALU.add).then_inc(*sig("v_normed").up())
                    for g in range(8):
                        dve.wait_ge(*sig("mixed").at(g + 1))
                        t = TMP[g % 2]
                        nc.vector.tensor_tensor(t.rearrange("p (i c) -> p i c", c=P),
                                                ps[:, 4 + g % 4, :].rearrange("p (i c) -> p i c", c=P),
                                                BS[:, g:g + 1, :].broadcast_to([P, TT, P]), ALU.add)\
                          .then_inc(*sig("mixed_out").up())
                        dve.wait_ge(*sig("mixed_out").at(g + 1))
                        nc.vector.tensor_tensor(U[:, g, :], U[:, g, :], t, ALU.mult)

        def column(name, first):
            return lambda k: col(name, k + first)

        def conv_taps(name, first, tiles):
            return lambda j, m: col(name, m + (first + tiles * j))

        def block2():
            hx = lambda k: H[:, k, :]
            normalize(X, H, KT, False, RMS_EPS, gain=column("attn_norm_2", 0))
            AQK, AR = arena[:, 2, 0:4, :], arena[:, 2, 4:8, :]
            V, BQ, IQK = arena[:, 3, 0:4, :], arena[:, 3, 4:8, :], arena[:, 4, 0:4, :]
            ALR = arena[0:16, 4, 4, :]
            NB = arena[:, 4, 5, 0:272].rearrange("p (i c) -> p i c", i=TT)
            W2 = arena[0:16, 4, 6, 0:256]

            def narrow(u, t, bank):
                if t == 0:
                    return nc.scalar.activation(ALR, ps[0:16, bank, :], ACT.Copy)
                return nc.scalar.activation(NB[:, t - 1, :], ps[:, bank, 0:68], ACT.Copy)
            products([fjob("aqk", hx, AQK), tjob("av", hx, V), fjob("ar", hx, AR, ACT.Silu), fjob("bq", hx, BQ),
                      fjob("iq", hx, IQK[:, 0:2]), fjob("shared", hx, IQK[:, 2:4]), ("narrow", hx, "act", narrow)])
            gla(AQK[:, 0:2], AQK[:, 2:4], V, ALR, W2, AR, H[:, 0:4, :])
            rotate([BQ, IQK])
            MASK = flat(big(2))[:, 0:CAUSAL]
            select_keys(IQK[:, 0:2], IQK[:, 3, :], NB, MASK)
            sparse_attention(BQ, IQK[:, 2, :], NB, MASK, H[:, 4:8, :])
            products([resjob("w_o", hx)])

            def ffn_layer(tag, l):
                normalize(X, H, KT, False, RMS_EPS, gain=column("ffn_norm_2", 8 * l))
                ffn_phase(tag, "conv", taps=conv_taps("ffn_conv_w_2", 132 * l, 44),
                          tap_bias=column("ffn_conv_b_2", 44 * l))
            ffn_layer("ffn2", 0)
            normalize(X, H, KT, False, RMS_EPS, gain=column("sgu_norm_2", 0))
            V2 = big(3).rearrange("p k t -> p (k t)").rearrange("p (i n) -> p i n", i=TT)
            products([fjob("sgu_u", hx, big(2), GELU), tjob("sgu_v", hx, V2, GELU)])
            sgu(big(2), V2)
            products([resjob("sgu_out", lambda k: big(2)[:, k, :])])
            ffn_layer("ffn3", 1)
            normalize(X, X, KT, False, RMS_EPS, gain=column("final_norm_2", 0))

        def hgrn(Q, Fz, V, K):
            lb, om = small[:, 0:8], small[:, 8:16]
            e0, e1, mm = small[:, 16:24], small[:, 24:32], small[:, 32:40]
            lg = COLUMN["hgrn_lb_logits_3"]
            l0, l1 = cols[:, lg:lg + 8], cols[:, lg + 8:lg + 16]
            with phase() as block:
                @block.vector
                def _(dve):
                    step = stepper(dve, "dve_step")
                    step(nc.vector.tensor_tensor(mm, l0, l1, ALU.max))
                    step(nc.vector.tensor_tensor(e0, l0, mm, ALU.subtract))
                    nc.vector.tensor_tensor(e1, l1, mm, ALU.subtract).then_inc(*sig("logits_ready").up())
                    dve.wait_ge(*sig("logit_exps").at(1))
                    step(nc.vector.tensor_tensor(mm, e0, e1, ALU.add))
                    step(nc.vector.reciprocal(mm, mm))
                    step(nc.vector.tensor_tensor(lb, e0, mm, ALU.mult))
                    step(nc.vector.tensor_scalar(om, lb, -1.0, 1.0, ALU.mult, ALU.add))
                    for k in range(KT):
                        dve.wait_ge(*sig("sigmoids").at(k + 1))
                        nc.vector.tensor_scalar(K[:, k, :], K[:, k, :], om[:, k:k + 1], None, ALU.mult)
                        nc.vector.tensor_scalar(Fz[:, k, :], Fz[:, k, :], om[:, k:k + 1], lb[:, k:k + 1],
                                                ALU.mult, ALU.add).then_inc(*sig("forget_ready").up())
                    for k in range(KT):
                        dve.wait_ge(*sig("log_ready").at(k + 1))
                        nc.vector.tensor_tensor_scan(Fz[:, k, :], const("keep128", T), big(7)[:, k, :], 0.0,
                                                     ALU.mult, ALU.add)

                @block.scalar
                def _(act):
                    act.wait_ge(*sig("logits_ready").at(1))
                    nc.scalar.activation(small[:, 16:32], small[:, 16:32], ACT.Exp).then_inc(*sig("logit_exps").up())
                    for k in range(KT):
                        nc.scalar.activation(K[:, k, :], Fz[:, k, :], ACT.Sigmoid, scale=-1.0).then_inc(*sig("act_step").up())
                        act.wait_ge(sig("act_step").handle, sig("act_step").total)
                        nc.scalar.activation(Fz[:, k, :], Fz[:, k, :], ACT.Sigmoid).then_inc(*sig("sigmoids").up())
                    for k in range(KT):
                        act.wait_ge(*sig("forget_ready").at(k + 1))
                        nc.scalar.activation(big(7)[:, k, :], Fz[:, k, :], ACT.Ln).then_inc(*sig("log_ready").up())
            for half in range(2):
                hgrn_heads(Q[:, 4 * half:4 * half + 4], K[:, 4 * half:4 * half + 4], Fz[:, 4 * half:4 * half + 4], V, 4 * half)

        def hgrn_heads(Q, K, B, V, h0):
            QE, KE, KTOK = arena[:, 7, 0:4, :], arena[:, 7, 4:8, :], arena[:, 8, 0:4, :]
            S = flat(arena[:, 8, 4:8, :]).rearrange("p (h n v) -> p h n v", h=4, n=4)
            XL = [arena[:, 2, 4:8, :], KTOK]
            ATT, TMP = KE, KTOK
            dec = small[:, 64:80].rearrange("p (h n) -> p h n", h=4)
            C = P
            LEVELS = 7

            def ch(v, l=C):
                return v.rearrange("p h (n l) -> p (h n) l", l=l)

            def halves(v, lv):
                h = 64 >> lv
                return v.rearrange("p h (n s l) -> p (h n) s l", s=2, l=h)
            DIFF = arena[:, 2, 4:8, :]
            XLV = arena[:, 8, 0:4, :]
            with phase() as block:
                @block.scalar
                def _(act):
                    act.wait_ge(*sig("tail_diff").at(1))
                    nc.scalar.activation(KE, KE, ACT.Exp)
                    nc.scalar.activation(QE, B, ACT.Exp)
                    nc.scalar.activation(dec, B.rearrange("p h (n l) -> p h n l", l=C)[:, :, :, C - 1], ACT.Exp)\
                      .then_inc(*sig("exps_ready").up())
                    for m in range(4):
                        act.wait_ge(*sig("k_turned").at(m + 1))
                        nc.scalar.activation(KTOK[:, m, :], ps[:, m, :], ACT.Copy).then_inc(*sig("k_tok").up())
                    for lv in range(LEVELS):
                        act.wait_ge(*sig("level_diff").at(lv + 1))
                        nc.scalar.activation(DIFF, DIFF, ACT.Exp).then_inc(*sig("level_exp").up())
                    act.wait_ge(*sig("heads_ready").at(1))
                    nc.scalar.activation(DIFF, ps[:, 0:4, :], ACT.Square).then_inc(*sig("heads_squared").up())
                    act.wait_ge(*sig("variance").at(1))
                    nc.scalar.activation(TMP, TMP, ACT.Sqrt).then_inc(*sig("deviation").up())

                @block.vector
                def _(dve):
                    step = stepper(dve, "dve_step")
                    nc.vector.tensor_tensor(ch(KE), ch(B)[:, :, C - 1:C].broadcast_to([P, 16, C]), ch(B), ALU.subtract)\
                      .then_inc(*sig("tail_diff").up())
                    dve.wait_ge(*sig("exps_ready").at(1))
                    step(nc.vector.tensor_tensor(QE, QE, Q, ALU.mult))
                    nc.vector.tensor_tensor(KE, KE, K, ALU.mult).then_inc(*sig("tail_ready").up())
                    dve.wait_ge(*sig("state_adds").at(1))
                    step(nc.vector.tensor_copy(S[:, :, 1, :], ps[:, 4:7, :].rearrange("p n (h v) -> p h n v", h=4)[:, :, 0]))
                    for n in (1, 2):
                        for h in range(4):
                            last = nc.vector.scalar_tensor_tensor(S[:, h, n + 1, :], S[:, h, n, :], dec[:, h, n:n + 1],
                                                                  ps[:, 4 + n, h * P:h * P + P], ALU.mult, ALU.add)
                        step(last)
                    step(nc.vector.memset(ATT, 0.0))
                    att = ATT.rearrange("p h (i c) -> p (h i) c", c=P)
                    for lv in range(-1, LEVELS):
                        def diff(l):
                            b, d = halves(B, l), halves(DIFF, l)
                            hh = 64 >> l
                            ref = b[:, :, 0, hh - 1:hh].broadcast_to([P, b.shape[1], hh])
                            if l:
                                dve.wait_ge(*sig("level_ready").at(l))
                            step(nc.vector.tensor_tensor(d[:, :, 0, :], ref, b[:, :, 0, :], ALU.subtract))
                            nc.vector.tensor_tensor(d[:, :, 1, :], b[:, :, 1, :], ref, ALU.subtract)\
                              .then_inc(*sig("level_diff").up())
                        if lv < 0:
                            diff(0)
                        if lv >= 0:
                            dve.wait_ge(*sig("level_exp").at(lv + 1))
                            if lv:
                                dve.wait_ge(*sig("level_scores").at(lv + 1))
                            x, d = halves(XLV, lv), halves(DIFF, lv)
                            step(nc.vector.tensor_tensor(x[:, :, 0, :], halves(K, lv)[:, :, 0, :], d[:, :, 0, :], ALU.mult))
                            nc.vector.tensor_tensor(x[:, :, 1, :], halves(Q, lv)[:, :, 1, :], d[:, :, 1, :], ALU.mult)\
                              .then_inc(*sig("level_ready").up())
                            if lv + 1 < LEVELS:
                                diff(lv + 1)
                        dve.wait_ge(*sig("level_scores").at(lv + 2))
                        bank = 4 * ((lv + 1) % 2)
                        mask = const("ident" if lv < 0 else f"level{lv}").bitcast(I32)
                        nc.vector.copy_predicated(att, bc(mask, 16), ps[:, bank:bank + 4, :].rearrange("p h (i c) -> p (h i) c", c=P))\
                          .then_inc(*sig("level_taken").up())
                    dve.wait_ge(*sig("heads_summed").at(1))
                    nc.vector.tensor_scalar(TMP, ps[:, 4:8, :], 1.0 / P, RMS_EPS, ALU.mult, ALU.add)\
                      .then_inc(*sig("variance").up())
                    dve.wait_ge(*sig("deviation").at(1))
                    step(nc.vector.reciprocal(TMP, TMP))
                    step(nc.vector.tensor_tensor(TMP, ps[:, 0:4, :], TMP, ALU.mult))
                    for h in range(4):
                        nc.vector.tensor_scalar(Q[:, h, :], TMP[:, h, :], col("hgrn_norm_g_3", h0 + h), None, ALU.mult)

                @block.tensor
                def _(pe):
                    pe.wait_ge(*sig("tail_ready").at(1))
                    for h in range(4):
                        for i in range(TT):
                            last = nc.tensor.transpose(ps[:, h, i * P:i * P + P], KE[:, h, i * P:i * P + P], ident)
                        last.then_inc(*sig("k_turned").up())
                    for h in range(4):
                        pe.wait_ge(*sig("k_tok").at(h + 1))
                        for n in range(3):
                            last = nc.tensor.matmul(ps[:, 4 + n, h * P:h * P + P], KTOK[:, h, n * P:n * P + P],
                                                    V[:, n, (h0 + h) * P:(h0 + h) * P + P], start=True, stop=True)
                    last.then_inc(*sig("state_adds").up())
                    for lv in range(-1, LEVELS):
                        bank = 4 * ((lv + 1) % 2)
                        if lv >= 0:
                            pe.wait_ge(*sig("level_ready").at(lv + 1))
                        if lv >= 1:
                            pe.wait_ge(*sig("level_taken").at(lv))
                        for h in range(4):
                            for i in range(TT):
                                w = slice(i * P, i * P + P)
                                lhs, rhs = (K[:, h, w], Q[:, h, w]) if lv < 0 else (XLV[:, h, w], XLV[:, h, w])
                                last = nc.tensor.matmul(ps[:, bank + h, w], lhs, rhs, start=True, stop=True)
                        last.then_inc(*sig("level_scores").up())
                    pe.wait_ge(*sig("level_taken").at(LEVELS + 1))
                    for h in range(4):
                        for i in range(TT):
                            w = slice(i * P, i * P + P)
                            last = nc.tensor.matmul(ps[:, h, w], V[:, i, (h0 + h) * P:(h0 + h) * P + P], ATT[:, h, w],
                                                    start=True, stop=i == 0)
                            if i:
                                last = nc.tensor.matmul(ps[:, h, w], S[:, h, i, :], QE[:, h, w], start=False, stop=True)
                    last.then_inc(*sig("heads_ready").up())
                    pe.wait_ge(*sig("heads_squared").at(1))
                    for h in range(4):
                        last = nc.tensor.matmul(ps[:, 4 + h, :], const("ones"), DIFF[:, h, :], start=True, stop=True)
                    last.then_inc(*sig("heads_summed").up())

        def block3():
            nx = lambda k: X[:, k, :]
            CV, CG, CACC = arena[:, 2, 0:4, :], arena[:, 2, 4:8, :], arena[:, 6, 0:4, :]
            V = big(5).rearrange("p k t -> p (k t)").rearrange("p (i n) -> p i n", i=TT)
            products([fjob("cval", nx, CV), fjob("cgate", nx, CG, ACT.Sigmoid)])
            NTAP = 31
            with phase() as block:
                @block.sync
                def _(sp):
                    feed(sp, "iv")

                @block.tensor
                def _(pe):
                    for name in ("qz", "fz", "iv"):
                        mm_gemm(pe, name, nx)

                @block.scalar
                def _(act):
                    for job in (fjob("qz", nx, big(3), ACT.Silu), fjob("fz", nx, big(4)), tjob("iv", nx, V)):
                        take(act, job[0], "tile_act", range(len(plan[job[0]].tiles)), job[3])

                @block.vector
                def _(dve):
                    step = stepper(dve, "dve_step")
                    step(nc.vector.tensor_tensor(CV, CV, CG, ALU.mult))
                    for s in range(NTAP):
                        for k in range(4):
                            w = col("w_conv_dw_3", 4 * (NTAP - 1 - s) + k)
                            if s == 0:
                                last = nc.vector.tensor_scalar(CACC[:, k, :], CV[:, k, :], w, col("b_conv_dw_3", k),
                                                               ALU.mult, ALU.add)
                            else:
                                last = nc.vector.scalar_tensor_tensor(CACC[:, k, s:T], CV[:, k, 0:T - s], w,
                                                                      CACC[:, k, s:T], ALU.mult, ALU.add)
                        step(last)
            normalize(CACC, CV, 4, True, LN_EPS, gain=column("conv_ln_g_3", 0), bias=column("conv_ln_b_3", 0),
                      func=ACT.Silu, tmp=7)
            hgrn(big(3), big(4), V, big(6))
            M2 = arena[:, 4:6, :, :].rearrange("p a k t -> p (a k) t")
            products([fjob("gz", nx, big(7), ACT.Silu), fjob("mz", nx, M2, ACT.Sigmoid)])
            with phase() as block:
                @block.vector
                def _(dve):
                    nc.vector.tensor_tensor(big(3), big(3), big(7), ALU.mult)
            products([merge_job("conv_out", lambda k: CV[:, k, :], big(4)),
                      merge_job("hgrn_out", lambda k: big(3)[:, k, :], big(5), big(4)),
                      ])
            products([resjob("out3", lambda k: big(4)[:, k, :], alpha=ALPHA)])
            normalize(X, X, KT, True, LN_EPS, gain=column("ln1_g_3", 0), bias=column("ln1_b_3", 0))
            with phase() as block:
                @block.scalar
                def _(act):
                    nc.scalar.activation(H, X, ACT.Copy)
            ffn_phase("ffn4", "convgelu", taps=conv_taps("w_ffn_dw_3", 0, 22), tap_bias=column("b_ffn_dw_3", 0),
                      alpha=ALPHA)
            normalize(X, X, KT, True, LN_EPS, gain=column("ln2_g_3", 0), bias=column("ln2_b_3", 0))

        start()
        if 1 in blocks:
            block1()
        if 2 in blocks:
            block2()
        if 3 in blocks:
            block3()
        finish()


_INS = ["x", "c", "w_ada", "b_ada", "w_in", "w_sb_up", "ssm_a_re", "ssm_a_im", "ssm_log_dt", "ssm_b_re", "ssm_b_im",
        "ssm_c_re", "ssm_c_im", "ssm_d", "w_glu", "b_glu", "w_ssm_up", "w_out", "ln1_g", "ln1_b", "w_ffn_in",
        "w_ffn_out", "ln2_g", "ln2_b", "attn_norm_2", "attn_w_in_2", "gla_w_a2_2", "gla_b_a_2", "gla_head_g_2",
        "attn_w_o_2", "sgu_norm_2", "sgu_w_uv_2", "sgu_ln_g_2", "sgu_ln_b_2", "sgu_w_s_2", "sgu_b_s_2", "sgu_w_out_2",
        "ffn_norm_2", "ffn_w_up_2", "ffn_conv_w_2", "ffn_conv_b_2", "ffn_w_down_2", "final_norm_2", "w_in_3",
        "w_conv_dw_3", "b_conv_dw_3", "conv_ln_g_3", "conv_ln_b_3", "w_conv_out_3", "hgrn_lb_logits_3",
        "hgrn_norm_g_3", "w_hgrn_out_3", "w_out_3", "ln1_g_3", "ln1_b_3", "w_ffn_in_3", "w_ffn_dw_3", "b_ffn_dw_3",
        "w_ffn_out_3", "ln2_g_3", "ln2_b_3"]


def kernel(**inputs):
    import numpy as _np
    import concourse.bacc as _bacc
    from concourse import mybir as _mybir
    from concourse.bass_utils import run_bass_kernel_spmd as _run

    nc = _bacc.Bacc("TRN2", target_bir_lowering=False, num_devices=1)
    arrays, args = {"constants": constants()}, {}
    for name in _INS:
        arrays[name] = _np.ascontiguousarray(inputs[name])
    for name, v in arrays.items():
        args[name] = nc.dram_tensor(name, v.shape, _mybir.dt.from_np(v.dtype), kind="ExternalInput").ap()
    out = nc.dram_tensor("out", (1, T, D), F32, kind="ExternalOutput").ap()
    build_program(nc, args, out)
    r = _run(nc, [arrays], core_ids=[0])
    return r.results[0]["out"]
```

```python
import math
from contextlib import ExitStack

import numpy as np
import concourse.bass as bass
from concourse import mybir

F32 = mybir.dt.float32
F32R = mybir.dt.float32r
I32 = mybir.dt.int32
ALU = mybir.AluOpType
ACT = mybir.ActivationFunctionType
AXX = mybir.AxisListType.X

P = 128
T = 512
D = 1024
KT = D // P
TT = T // P
HID = 2816
HT = HID // P
SLOTS = 2
SLOT = 2048
BANKS = 4
LN_EPS, RMS_EPS = 1e-5, 1e-6
ALPHA = 2.0 ** 0.25
NEG = -3.0e38
TOPK = min(256, T // 4)

VECTORS = [
    ("b_ada", 48), ("ssm_a_re", 16), ("ssm_a_im", 16), ("ssm_d", 4), ("b_glu", 4), ("c", 8),
    ("ln1_g", 8), ("ln1_b", 8), ("ln2_g", 8), ("ln2_b", 8), ("attn_norm_2", 8),
    ("gla_b_a_2", 2), ("gla_head_g_2", 1), ("sgu_norm_2", 8), ("ffn_norm_2", 16),
    ("ffn_conv_w_2", 264), ("ffn_conv_b_2", 88), ("final_norm_2", 8),
    ("w_conv_dw_3", 124), ("b_conv_dw_3", 4), ("conv_ln_g_3", 4), ("conv_ln_b_3", 4),
    ("hgrn_lb_logits_3", 16), ("hgrn_norm_g_3", 8), ("ln1_g_3", 8), ("ln1_b_3", 8),
    ("w_ffn_dw_3", 66), ("b_ffn_dw_3", 22), ("ln2_g_3", 8), ("ln2_b_3", 8),
]
COLUMN, _at = {}, 0
for _name, _rows in VECTORS:
    COLUMN[_name] = _at
    _at += _rows
VROWS = _at
VTILES = -(-VROWS // P)

CONST_AT = {}


def constants():
    r, c = np.arange(P)[:, None], np.arange(P)[None, :]
    parts, at = [], 0

    def put(name, a):
        nonlocal at
        CONST_AT[name] = at
        a = np.broadcast_to(np.asarray(a, np.float32), (P, a.shape[-1]))
        parts.append(a)
        at += a.shape[1]

    put("ident", (r == c).astype(np.float32))
    put("ones", np.ones((P, P)))
    put("later", (r > c).astype(np.float32))
    put("before", (r < c).astype(np.float32))
    put("upto", (r <= c).astype(np.float32))
    put("chunk64", ((r <= c) & (r // 64 == c // 64)).astype(np.float32))
    put("notyet", np.where(c <= r, 0.0, NEG))
    perm = np.zeros((P, P))
    for h in range(2):
        for i in range(8):
            perm[64 * h + 8 + i, 64 * h + i] = -1.0
            perm[64 * h + i, 64 * h + 8 + i] = 1.0
    put("turn", perm)
    for lv in range(7):
        h = 64 >> lv
        put(f"level{lv}", ((r // (2 * h) == c // (2 * h)) & (r % (2 * h) < h) & (c % (2 * h) >= h)).astype(np.float32))
    put("group0", ((r // 16) % 2 == 0).astype(np.float32))
    put("group1", ((r // 16) % 2 == 1).astype(np.float32))
    inv = np.power(np.float32(500000.0), -(np.arange(8, dtype=np.float32) * 2.0 / 16)).astype(np.float32)
    ang = (np.arange(T, dtype=np.float32)[None, :] * inv[:, None]).astype(np.float32)
    cos, sin = np.ones((P, T)), np.zeros((P, T))
    for h in range(2):
        for k in range(2):
            cos[64 * h + 8 * k:64 * h + 8 * k + 8] = np.cos(ang)
            sin[64 * h + 8 * k:64 * h + 8 * k + 8] = np.sin(ang)
    CONST_AT["tables"] = at
    put("cos", cos)
    put("sin", sin)
    put("keep64", (np.arange(T)[None, :] % 64 != 0).astype(np.float32))
    put("keep128", (np.arange(T)[None, :] % 128 != 0).astype(np.float32))
    return np.ascontiguousarray(np.concatenate(parts, axis=1), np.float32)


class Signal:

    def __init__(self, handle):
        self.handle, self.base, self.total = handle, 0, 0

    def up(self):
        self.total += 1
        return self.handle, 1

    def at(self, k):
        return self.handle, self.base + k


class Gemm:

    def __init__(self, name, n, panels, tiles, kt, evac, ppt=1):
        self.name, self.n, self.panels, self.tiles, self.kt = name, n, panels, tiles, kt
        self.evac, self.ppt = evac, ppt
        self.ppu = len(panels)


def build_program(nc, a, out, debug=None, blocks=(1, 2, 3)):
    ctx = ExitStack()
    with ctx:
        def sbuf(name, shape, dt=F32):
            return ctx.enter_context(nc.sbuf_tensor(name, shape, dt))

        signals = {}

        def sig(name):
            if name not in signals:
                signals[name] = Signal(ctx.enter_context(nc.semaphore(name)))
            return signals[name]

        base_at = [nc.sbuf_base + (-nc.sbuf_base) % 64]

        def place(name, shape, dt=F32, at=None):
            size = -(-4 * int(np.prod(shape[1:])) // 64) * 64
            if at is None:
                at = base_at[0]
                base_at[0] += size
            return nc.alloc_sbuf_tensor_at(name, shape, dt, offset=at)

        TILE = T * 4
        arena_at = base_at[0]
        arena_t = place("arena", [P, 68, T])
        act_hi = place("act_hi", [P, KT, T], F32R, arena_at + 8 * TILE)
        act_lo = place("act_lo", [P, KT, T], F32R, arena_at + 16 * TILE)
        hid_hi = place("hid_hi", [P, HT, T], F32R, arena_at + 24 * TILE)
        hid_lo = place("hid_lo", [P, HT, T], F32R, arena_at + 46 * TILE)
        conv_hi = place("conv_hi", [P, 4, T], F32R, arena_at + 24 * TILE)
        conv_lo = place("conv_lo", [P, 4, T], F32R, arena_at + 28 * TILE)
        weights = place("weights", [P, SLOTS, SLOT])
        w_hi = place("w_hi", [P, SLOTS, SLOT], F32R)
        w_lo = place("w_lo", [P, SLOTS, SLOT], F32R)
        constants()
        ncst = CONST_AT["tables"]
        cst = place("cst", [P, ncst])
        cols = place("cols", [P, VTILES * P])
        rows = place("rows", [P, 4, T])
        mod = place("mod", [P, 48])
        small = place("small", [P, 512])
        ps = ctx.enter_context(nc.psum_tensor("ps", [P, 8, 512], F32))

        def big(i):
            return arena_t[:, 8 * i:8 * i + 8, :]

        def part_of(i, lo, hi):
            return arena_t[:, 8 * i + lo:8 * i + hi, :]

        def const(name, n=P):
            return cst[:, CONST_AT[name]:CONST_AT[name] + n]

        def col(name, i=0):
            at = COLUMN[name] + i
            return cols[:, at:at + 1] if isinstance(i, int) else cols[:, bass.ds(at, 1)]

        X = big(0)

        def parts(hi, lo, first=0):
            return lambda k: (hi[:, first + k, :], lo[:, first + k, :])
        ACTS = parts(act_hi, act_lo)
        ident = const("ident")

        def kview(w):
            return w.rearrange("(k p) n -> p k n", p=P)

        def slot_view(s, kt, n, of=None):
            return (weights if of is None else of)[:, s, 0:kt * n].rearrange("p (k n) -> p k n", k=kt)

        def cols_panel(w, kt, c0, width):
            def dmas(u, s):
                return [(slot_view(s, kt, width), kview(w)[:, :, bass.ds(c0 + u * width, width)])]
            return dmas

        def pair_panel(w):
            v = kview(w).rearrange("p k (h n) -> p k h n", h=2)
            return lambda u, s: [(slot_view(s, KT, 256)[:, :, h * P:h * P + P], v[:, :, h, bass.ds(u * P, P)])
                                 for h in range(2)]

        def half_panel(w, half):
            v = w.rearrange("(h k p) n -> p h k n", p=P, h=2)[:, half]
            return lambda u, s: [(slot_view(s, HT // 2, P), v[:, :, bass.ds(u * P, P)])]

        plan, order = {}, []

        def gemm(name, *args, **kw):
            plan[name] = Gemm(name, *args, **kw)
            order.append(plan[name])

        def feat(name, w, kt, n, evac, c0=0):
            width = 256 if kt == 8 else 512
            tiles = [("w", i * P, P, 0) for i in range(width // P)]
            gemm(name, n, [cols_panel(w, kt, c0, width)], tiles, kt, evac)

        def tok(name, w, kt, n, evac, c0=0):
            gemm(name, n, [cols_panel(w, kt, c0, 256)], [("x", 0, 256, i) for i in range(TT)], kt, evac)

        def ffn(tag, w_in, w_out, evac):
            gemm(tag + "_in", HT, [pair_panel(w_in)], [("w", 0, P, 0), ("w", P, P, 0)], KT, evac)
            gemm(tag + "_out", KT, [half_panel(w_out, 0), half_panel(w_out, 1)], [("w", 0, P, 0)], HT, "dve")

        if 1 in blocks:
            w = a["w_in"][0]
            feat("qk", w, KT, 4, "act")
            tok("v", w, KT, 2, "act", c0=1024)
            feat("u", w, KT, 2, "act", c0=1536)
            feat("gates", w, KT, 8, "act", c0=2048)
            feat("sb_up", a["w_sb_up"][0], 4, 2, "dve")
            feat("glu", a["w_glu"][0], 4, 1, "act")
            feat("ssm_up", a["w_ssm_up"][0], 4, 2, "dve")
            feat("out1", a["w_out"][0], KT, 4, "dve")
            ffn("ffn1", a["w_ffn_in"][0], a["w_ffn_out"][0], "swiglu")
        if 2 in blocks:
            w = a["attn_w_in_2"][0]
            feat("aqk", w, KT, 2, "act")
            tok("av", w, KT, 2, "act", c0=512)
            feat("ar", w, KT, 2, "act", c0=1024)
            feat("bq", w, KT, 2, "act", c0=1552)
            feat("iq", w, KT, 1, "act", c0=2192)
            wk = kview(w)
            gemm("shared", 1, [lambda u, s: [
                (slot_view(s, KT, 256)[:, :, 64 * i:64 * i + 64], wk[:, :, c0:c0 + 64])
                for i, c0 in enumerate((2064, 2064, 2448, 2448))]],
                [("w", 0, P, 0), ("w", P, P, 0)], KT, "act")
            gemm("narrow", 1, [lambda u, s: [
                (slot_view(s, KT, 256)[:, :, o:o + n], wk[:, :, c0:c0 + n])
                for o, n, c0 in ((0, 16, 1536), (16, 64, 2128), (80, 4, 2512))]],
                [("w", 0, P, 0)] + [("x", 16, 68, i) for i in range(TT)], KT, "act")
            feat("w_o", a["attn_w_o_2"][0], KT, 4, "dve")
            ffn("ffn2", a["ffn_w_up_2"][0], a["ffn_w_down_2"][0], "conv")
            feat("sgu_u", a["sgu_w_uv_2"][0], KT, 4, "act")
            tok("sgu_v", a["sgu_w_uv_2"][0], KT, 4, "act", c0=1024)
            feat("sgu_out", a["sgu_w_out_2"][0], KT, 4, "dve")
            ffn("ffn3", a["ffn_w_up_2"][1], a["ffn_w_down_2"][1], "conv")
        if 3 in blocks:
            w = a["w_in_3"][0]
            feat("cval", w, KT, 2, "act")
            feat("cgate", w, KT, 2, "act", c0=512)
            feat("qz", w, KT, 4, "act", c0=1024)
            feat("fz", w, KT, 4, "act", c0=2048)
            tok("iv", w, KT, 4, "act", c0=3072)
            feat("gz", w, KT, 4, "act", c0=4096)
            feat("mz", w, KT, 8, "act", c0=5120)
            feat("conv_out", a["w_conv_out_3"][0], 4, 2, "dve")
            feat("hgrn_out", a["w_hgrn_out_3"][0], KT, 4, "dve")
            feat("out3", a["w_out_3"][0], KT, 4, "dve")
            ffn("ffn4", a["w_ffn_in_3"][0], a["w_ffn_out_3"][0], "convgelu")

        RATES = {"act": {"tile_act": "t"}, "dve": {"tile_dve": "t"},
                 "swiglu": {"tile_act": 1, "tile_dve": 1, "hid_hi": 1, "hidden_done": 1},
                 "conv": {"tap_act": 2, "tap_step": 2, "tile_dve": 2, "gate_act": 1, "hidden_mul": 1, "hid_hi": 1,
                          "hidden_done": 1},
                 "convgelu": {"tap_act": 1, "tap_step": 1, "tile_dve": 2, "gate_act": 1, "hid_hi": 1,
                              "hidden_done": 1}}
        running = dict.fromkeys(["marks", "bank", "tile_act", "tile_dve", "tap_act", "tap_step", "gate_act",
                                 "hidden_mul", "hid_hi"], 0)
        running["hidden_done"] = 2
        panel_list, slot_count = [], [0] * SLOTS
        for g in order:
            g.base, g.first_panel, g.dmas = dict(running), len(panel_list), len(g.panels[0](0, 0))
            g.marks = len(g.tiles) * g.ppu
            for u in range(g.n):
                for j, dmas in enumerate(g.panels):
                    s = len(panel_list) % SLOTS
                    slot_count[s] += 16 * len(dmas(0, s))
                    panel_list.append(dict(g=g, u=u, j=j, slot=s, filled=slot_count[s]))
            running["marks"] += g.n * g.marks
            running["bank"] += g.n * len(g.tiles)
            for k, v in RATES[g.evac].items():
                running[k] += g.n * (len(g.tiles) if v == "t" else v)
            g.end = dict(running)
        marks = sig("marks")
        panel_in = [sig(f"panel_in{s}") for s in range(SLOTS)]
        hi_ready, lo_ready = sig("hi_ready"), sig("lo_ready")
        fed = [0]

        def one_panel(sp, p, p_value, u):
            info = panel_list[p]
            if p >= SLOTS:
                sp.wait_ge(lo_ready.handle, p_value - (SLOTS - 1))
            for dst, src in info["g"].panels[info["j"]](u, info["slot"]):
                sp.dma_start(dst, src).then_inc(panel_in[info["slot"]].handle, 16)

        def feed(sp, last):
            g = plan[last] if last else None
            end = min((g.first_panel + g.n * g.ppu if g else 0) + SLOTS, len(panel_list))
            while fed[0] < end:
                p = fed[0]
                g, ppu = panel_list[p]["g"], panel_list[p]["g"].ppu
                per = SLOTS // ppu
                stop = min(end, g.first_panel + g.n * ppu)
                turns = (stop - p) // SLOTS
                if p >= SLOTS and (p - g.first_panel) % ppu == 0 and turns >= 3:
                    u0 = panel_list[p]["u"]
                    with sp.Fori(0, turns) as i:
                        for j in range(SLOTS):
                            one_panel(sp, p + j, i * SLOTS + (p + j), i * per + (u0 + j // ppu))
                    fed[0] += turns * SLOTS
                else:
                    one_panel(sp, p, p, panel_list[p]["u"])
                    fed[0] += 1

        def units(eng, g, emit):
            turns = (g.n - (g is order[-1])) // 4
            done = 0
            if turns >= 2:
                with eng.Fori(0, turns) as i:
                    for j in range(4):
                        emit(i * 4 + j, j)
                done = turns * 4
            for u in range(done, g.n):
                emit(u, u)

        def split_hi(act, g, u, j):
            for jj in range(g.ppu):
                p = g.first_panel + j * g.ppu + jj + 1
                if p >= len(panel_list):
                    continue
                s = p % SLOTS
                act.wait_ge(panel_in[s].handle, (u - j) * (g.dmas * g.ppu * 16 // SLOTS) + panel_list[p]["filled"])
                read = u * g.marks + (g.base["marks"] + jj)
                if not isinstance(read, int) or read > 0:
                    act.wait_ge(marks.handle, read)
                nc.scalar.activation(w_hi[:, s, :], weights[:, s, :], ACT.Copy).then_inc(hi_ready.handle, 1)

        def split_lo(dve, g, u, j):
            for jj in range(g.ppu):
                p = g.first_panel + j * g.ppu + jj + 1
                if p >= len(panel_list):
                    continue
                s = p % SLOTS
                dve.wait_ge(hi_ready.handle, (u - j) * g.ppu + (p + 1))
                nc.vector.tensor_tensor(w_lo[:, s, :], weights[:, s, :], w_hi[:, s, :].bitcast(F32), ALU.subtract)\
                  .then_inc(lo_ready.handle, 1)

        def bank_of(g, j, t):
            return (g.base["bank"] + j * len(g.tiles) + t) % BANKS

        def width_of(g):
            return P if g.kt == HT else 256 if g.kt == KT else 512

        def mm_gemm(pe, name, x, ready=None):
            g = plan[name]
            nt = len(g.tiles)
            for k in ("tile_act", "tile_dve"):
                if g.base[k]:
                    pe.wait_ge(sig(k).handle, g.base[k])
            pairs = {"swiglu": [("tile_act", 0, 1), ("tile_dve", 0, 1)],
                     "conv": [("tile_dve", 0, 2), ("tile_dve", 1, 2)],
                     "convgelu": [("tile_dve", 0, 2), ("tile_dve", 1, 2)]}

            def emit(u, j):
                for t, (kind, c0, width, tt) in enumerate(g.tiles):
                    bank = bank_of(g, j, t)
                    if j * nt + t >= BANKS or not isinstance(u, int):
                        back = j * nt + t - BANKS
                        bu, bt = back // nt, back % nt
                        k, idx, rate = pairs[g.evac][bt] if g.evac in pairs else ("tile_" + g.evac, bt, nt)
                        assert isinstance(u, int) or g.base[k] >= BANKS
                        pe.wait_ge(sig(k).handle, (u + (bu - j)) * rate + (g.base[k] + idx + 1))
                    kk, kt = 0, g.kt // g.ppu
                    for i in range(g.ppu):
                        p = g.first_panel + j * g.ppu + i
                        s = p % SLOTS
                        if t == 0:
                            pe.wait_ge(lo_ready.handle, (u - j) * g.ppu + (p + 1))
                        wh, wl = (slot_view(s, kt, width_of(g), of) for of in (w_hi, w_lo))
                        for k in range(kt):
                            if ready is not None and j == 0 and t == 0:
                                pe.wait_ge(*sig(ready).at(kk + 1))
                            xh, xl = x(kk)
                            if kind == "w":
                                c = slice(c0, c0 + width)
                                ops = ((wh[:, k, c], xh), (wh[:, k, c], xl), (wl[:, k, c], xh))
                                o = ps[:, bank, :]
                            else:
                                c, r = slice(c0, c0 + width), slice(tt * P, tt * P + P)
                                ops = ((xh[:, r], wh[:, k, c]), (xh[:, r], wl[:, k, c]), (xl[:, r], wh[:, k, c]))
                                o = ps[:, bank, 0:width]
                            for n, (lhs, rhs) in enumerate(ops):
                                last = nc.tensor.matmul(o, lhs, rhs, start=kk == 0 and n == 0,
                                                        stop=kk == g.kt - 1 and n == 2)
                            kk += 1
                        if i < g.ppu - 1:
                            last.then_inc(marks.handle, 1)
                    last.then_inc(marks.handle, 1)

            units(pe, g, emit)

        def take(eng, name, signal, tiles, fn, split, extra=None):
            g = plan[name]

            def emit(u, j):
                split(eng, g, u, j)
                if extra is not None and isinstance(u, int):
                    extra(name, u)
                for t in tiles:
                    eng.wait_ge(marks.handle, u * g.marks + (g.base["marks"] + (t + 1) * g.ppu))
                    fn(u, t, bank_of(g, j, t)).then_inc(sig(signal).handle, 1)
            units(eng, g, emit)

        def at_tile(view, i):
            if isinstance(i, int):
                return view[:, i, :]
            return view[:, bass.ds(i, 1), :].rearrange("p a t -> p (a t)")

        def phase(last=None):
            for s in signals.values():
                s.base = s.total
            block = nc.Block()
            return block

        def stepper(eng, name):
            s = sig(name)

            def step(ins):
                ins.then_inc(*s.up())
                eng.wait_ge(s.handle, s.total)
                return ins
            return step

        def bc(row, n):
            return row.rearrange("p (a t) -> p a t", a=1).broadcast_to([row.shape[0], n, row.shape[1]])

        def bl(c, n):
            return c.rearrange("p (a b) -> p a b", b=1).broadcast_to([c.shape[0], c.shape[1], n])

        def small_row(i):
            return rows[:, i, :]

        def normalize(src, kt, center, eps, gain, bias=None, func=ACT.Identity, dst=None, split=None,
                      cen=24, sq=32, part_ready=False, product=None):
            n = kt * P
            CEN, SQ = arena_t[:, cen:cen + kt, :], arena_t[:, sq:sq + kt, :]
            part, mean, var = (small_row(i) for i in range(3))
            Y = dst if dst is not None else CEN
            with phase() as block:
                @block.vector
                def _(dve):
                    step = stepper(dve, "norm_step")
                    cur = src
                    if center:
                        if not part_ready:
                            nc.vector.tensor_reduce(part, src.rearrange("p k t -> p t k"), AXX, ALU.add)\
                              .then_inc(*sig("part_sum").up())
                        dve.wait_ge(*sig("summed").at(1))
                        step(nc.vector.tensor_scalar(mean, ps[:, 4, :], 1.0 / n, None, ALU.mult))
                        for k in range(kt):
                            nc.vector.tensor_tensor(CEN[:, k, :], src[:, k, :], mean, ALU.subtract)\
                              .then_inc(*sig("centered").up())
                        cur = CEN
                    dve.wait_ge(*sig("squares_summed").at(1))
                    nc.vector.tensor_scalar(var, ps[:, 5, :], 1.0 / n, eps, ALU.mult, ALU.add)\
                      .then_inc(*sig("variance").up())
                    dve.wait_ge(*sig("deviation").at(1))
                    step(nc.vector.reciprocal(var, var))

                    def lower(k):
                        dve.wait_ge(*sig("upper_ready").at(k + 1))
                        nc.vector.tensor_tensor(split[1][:, k, :], Y[:, k, :], split[0][:, k, :].bitcast(F32),
                                                ALU.subtract).then_inc(*sig("lower_ready").up())
                    for k in range(kt):
                        nc.vector.tensor_tensor(CEN[:, k, :], cur[:, k, :], var, ALU.mult).then_inc(*sig("normed").up())
                        if split and k >= 2:
                            lower(k - 2)
                    if split:
                        lower(kt - 2)
                        lower(kt - 1)

                @block.tensor
                def _(pe):
                    if center:
                        if not part_ready:
                            pe.wait_ge(*sig("part_sum").at(1))
                        nc.tensor.matmul(ps[:, 4, :], const("ones"), part, start=True, stop=True)\
                          .then_inc(*sig("summed").up())
                    for k in range(kt):
                        pe.wait_ge(*sig("squared").at(k + 1))
                        last = nc.tensor.matmul(ps[:, 5, :], const("ones"), SQ[:, k, :], start=k == 0, stop=k == kt - 1)
                    last.then_inc(*sig("squares_summed").up())

                @block.scalar
                def _(act):
                    cur = CEN if center else src
                    for k in range(kt):
                        if center:
                            act.wait_ge(*sig("centered").at(k + 1))
                        nc.scalar.activation(SQ[:, k, :], cur[:, k, :], ACT.Square).then_inc(*sig("squared").up())
                    act.wait_ge(*sig("variance").at(1))
                    nc.scalar.activation(var, var, ACT.Sqrt).then_inc(*sig("deviation").up())

                    def upper(k):
                        act.wait_ge(*sig("affine_ready").at(k + 1))
                        nc.scalar.activation(split[0][:, k, :], Y[:, k, :], ACT.Copy).then_inc(*sig("upper_ready").up())
                    for k in range(kt):
                        act.wait_ge(*sig("normed").at(k + 1))
                        nc.scalar.activation(Y[:, k, :], CEN[:, k, :], func, scale=gain(k), bias=bias(k) if bias else 0.0)\
                          .then_inc(*sig("affine_ready").up())
                        if split and k:
                            upper(k - 1)
                    if split:
                        upper(kt - 1)

        def split_phase(jobs, before=None):
            jobs = [(s_[:, k, :], h[:, k, :], l[:, k, :]) for s_, h, l in jobs for k in range(s_.shape[1])]
            with phase() as block:
                @block.scalar
                def _(act):
                    if before:
                        before[1](act)
                    for s_, h, _ in jobs:
                        nc.scalar.activation(h, s_, ACT.Copy).then_inc(*sig("upper_ready").up())

                @block.vector
                def _(dve):
                    if before:
                        before[0](dve)
                    for k, (s_, h, l) in enumerate(jobs):
                        dve.wait_ge(*sig("upper_ready").at(k + 1))
                        nc.vector.tensor_tensor(l, s_, h.bitcast(F32), ALU.subtract)

        def start():
            xtok = big(2).rearrange("p k t -> p (k t)").rearrange("p (a n) -> p a n", a=TT)
            stage = big(3).rearrange("p k t -> p (k t)")[:, 0:VTILES * P].rearrange("p (a n) -> p a n", a=VTILES)
            with phase() as block:
                @block.gpsimd
                def _(pool):
                    nc.gpsimd.memset(stage, 0.0).then_inc(*sig("stage_zero").up())

                @block.sync
                def _(sp):
                    sp.dma_start(cst[:, :], a["constants"][:, 0:ncst]).then_inc(sig("loaded").handle, 16)
                    sp.dma_start(xtok, a["x"][0].rearrange("(a p) n -> p a n", p=P)).then_inc(sig("loaded").handle, 16)
                    feed(sp, None)

                n = 0
                pieces = []
                for name, rows_ in VECTORS:
                    src = a[name]
                    flat = src.rearrange(" ".join("abcd"[:len(src.shape)]) + " -> (" + " ".join("abcd"[:len(src.shape)]) + ")")
                    v = flat.rearrange("(r p) -> r p", p=P)
                    at, left, r0 = COLUMN[name], rows_, 0
                    while left:
                        m = min(left, P - at % P)
                        pieces.append((at // P, at % P, m, v[r0:r0 + m, :]))
                        at, left, r0 = at + m, left - m, r0 + m

                @block.scalar
                def _(act):
                    act.wait_ge(*sig("stage_zero").at(1))
                    for tile, p0, m, src in pieces:
                        act.dma_start(stage[p0:p0 + m, tile, :], src).then_inc(sig("vectors").handle, 16)
                    act.wait_ge(panel_in[0].handle, panel_list[0]["filled"])
                    nc.scalar.activation(w_hi[:, 0, :], weights[:, 0, :], ACT.Copy).then_inc(hi_ready.handle, 1)

                @block.tensor
                def _(pe):
                    pe.wait_ge(sig("loaded").handle, 32)
                    for k in range(KT):
                        for i in range(TT):
                            last = nc.tensor.transpose(ps[:, k % 4, i * P:(i + 1) * P], xtok[:, i, k * P:(k + 1) * P], ident)
                        last.then_inc(*sig("turned").up())
                        if k >= 3:
                            pe.wait_ge(sig("turned_out").handle, k - 2)
                    pe.wait_ge(sig("vectors").handle, 16 * len(pieces))
                    for i in range(VTILES):
                        last = nc.tensor.transpose(ps[:, 4 + i // 4, (i % 4) * P:(i % 4 + 1) * P], stage[:, i, :], ident)
                    last.then_inc(*sig("turned").up())

                @block.vector
                def _(dve):
                    for k in range(KT):
                        dve.wait_ge(*sig("turned").at(k + 1))
                        nc.vector.tensor_copy(X[:, k, :], ps[:, k % 4, :]).then_inc(*sig("turned_out").up())
                    dve.wait_ge(*sig("turned").at(KT + 1))
                    nc.vector.tensor_copy(cols[:, :], ps[:, 4:6, :].rearrange("p a n -> p (a n)")[:, 0:VTILES * P])
                    for i in range(2):
                        nc.vector.memset(small[:, i:i + 1], 0.0).then_inc(sig("hidden_done").handle, 1)
                    dve.wait_ge(hi_ready.handle, 1)
                    nc.vector.tensor_tensor(w_lo[:, 0, :], weights[:, 0, :], w_hi[:, 0, :].bitcast(F32), ALU.subtract)\
                      .then_inc(lo_ready.handle, 1)

        def finish():
            otok = big(2).rearrange("p k t -> p (k t)").rearrange("p (a n) -> p a n", a=TT)
            with phase() as block:
                @block.tensor
                def _(pe):
                    for n in range(8):
                        i, half = n // 2, n % 2
                        if n >= 4:
                            pe.wait_ge(*sig("turned_out").at(n - 3))
                        for k in range(4):
                            last = nc.tensor.transpose(ps[:, n % 4, k * P:(k + 1) * P],
                                                       X[:, half * 4 + k, i * P:(i + 1) * P], ident)
                        last.then_inc(*sig("turned").up())

                @block.vector
                def _(dve):
                    for n in range(8):
                        dve.wait_ge(*sig("turned").at(n + 1))
                        nc.vector.tensor_copy(otok[:, n // 2, (n % 2) * 512:(n % 2) * 512 + 512], ps[:, n % 4, :])\
                          .then_inc(*sig("turned_out").up())

                @block.sync
                def _(sp):
                    for i in range(TT):
                        sp.wait_ge(*sig("turned_out").at(2 * i + 2))
                        sp.dma_start(out[0, i * P:(i + 1) * P, :], otok[:, i, :]).then_inc(sig("stored").handle, 16)
                    sp.wait_ge(sig("stored").handle, 16 * TT)

        def products(jobs, extra=None, after=None):
            with phase() as block:
                @block.sync
                def _(sp):
                    feed(sp, jobs[-1][0])

                @block.tensor
                def _(pe):
                    for name, x, _, _ in jobs:
                        mm_gemm(pe, name, x)
                        if after:
                            after("tensor", pe, name)

                @block.scalar
                def _(act):
                    for name, _, who, fn in jobs:
                        take(act, name, "tile_act", range(len(plan[name].tiles)) if who == "act" else [], fn, split_hi)

                @block.vector
                def _(dve):
                    for name, _, who, fn in jobs:
                        take(dve, name, "tile_dve", range(len(plan[name].tiles)) if who == "dve" else [], fn, split_lo,
                             extra and (lambda nm, u: extra(dve, nm, u)))
                    if after:
                        after("vector", dve, None)

                @block.gpsimd
                def _(pool):
                    if after:
                        after("gpsimd", pool, None)

        def to(view, func=ACT.Identity, first=0, bias=None, scale=1.0):
            def fn(u, t, bank, nt=None):
                m = u * fn.nt + (first + t)
                b = bias(m) if bias else 0.0
                return nc.scalar.activation(at_tile(view, m), ps[:, bank, :], func, bias=b, scale=scale)
            return fn

        def nt_of(name, fn):
            fn.nt = len(plan[name].tiles)
            return fn

        def fjob(name, x, view, func=ACT.Identity, bias=None):
            return name, x, "act", nt_of(name, to(view, func, bias=bias))

        def tjob(name, x, view, func=ACT.Identity):
            def fn(u, t, bank):
                return nc.scalar.activation(view[:, t, bass.ds(u * 256, 256)] if not isinstance(u, int)
                                            else view[:, t, u * 256:u * 256 + 256], ps[:, bank, 0:256], func)
            return name, x, "act", fn

        def resjob(name, x, gain=None, alpha=1.0):
            nt = len(plan[name].tiles)

            def fn(u, t, bank):
                m = u * nt + t
                xt = at_tile(X, m)
                if gain is None:
                    return nc.vector.scalar_tensor_tensor(xt, xt, alpha, ps[:, bank, :], ALU.mult, ALU.add)
                return nc.vector.scalar_tensor_tensor(xt, ps[:, bank, :], gain(m), xt, ALU.mult, ALU.add)
            return name, x, "dve", fn

        def ffn_phase(tag, kind, taps=None, tap_bias=None, gain=None, alpha=1.0):
            g, go = plan[tag + "_in"], plan[tag + "_out"]
            b = g.base
            rj = resjob(tag + "_out", None, gain, alpha)
            mul = "hidden_mul" if kind == "conv" else "tile_dve"
            mul_rate = {"conv": 1, "swiglu": 1, "convgelu": 2}[kind]

            def buf(j, t):
                return rows[:, 2 * (j % 2) + t, :]
            with phase() as block:
                @block.sync
                def _(sp):
                    feed(sp, tag + "_out")

                @block.tensor
                def _(pe):
                    mm_gemm(pe, tag + "_in", ACTS)
                    pe.wait_ge(sig("hidden_done").handle, g.end["hidden_done"])
                    mm_gemm(pe, tag + "_out", parts(hid_hi, hid_lo))

                @block.scalar
                def _(act):
                    def emit(u, j):
                        split_hi(act, g, u, j)
                        gate, up = bank_of(g, j, 0), bank_of(g, j, 1)
                        act.wait_ge(sig("hidden_done").handle, u + (b["hidden_done"] - 1))
                        res = buf(j, 1 if kind != "convgelu" else 0)
                        if kind == "swiglu":
                            act.wait_ge(marks.handle, u * 2 + (b["marks"] + 1))
                            nc.scalar.activation(buf(j, 0), ps[:, gate, :], ACT.Silu).then_inc(sig("tile_act").handle, 1)
                        else:
                            nt = 2 if kind == "conv" else 1
                            for t in range(nt):
                                act.wait_ge(marks.handle, u * 2 + (b["marks"] + t + 1))
                                m = u + HT * t
                                nc.scalar.activation(buf(j, t), ps[:, bank_of(g, j, t), :], ACT.Identity,
                                                     scale=taps(2, m), bias=tap_bias(m)).then_inc(sig("tap_act").handle, 1)
                            act.wait_ge(sig("tile_dve").handle, u * 2 + (b["tile_dve"] + 1))
                            nc.scalar.activation(buf(j, 0), buf(j, 0), ACT.Silu if kind == "conv" else GELU)\
                              .then_inc(sig("gate_act").handle, 1)
                        act.wait_ge(sig(mul).handle, u * mul_rate + (b[mul] + mul_rate))
                        nc.scalar.activation(at_tile(hid_hi, u), res, ACT.Copy).then_inc(sig("hid_hi").handle, 1)
                    units(act, g, emit)
                    take(act, tag + "_out", None, [], None, split_hi)

                @block.vector
                def _(dve):
                    if gain is not None:
                        nc.vector.tensor_scalar(X, X, ALPHA, None, ALU.mult).then_inc(*sig("scaled").up())
                        dve.wait_ge(*sig("scaled").at(1))

                    def emit(u, j):
                        split_lo(dve, g, u, j)
                        gate, up = bank_of(g, j, 0), bank_of(g, j, 1)
                        res = buf(j, 1 if kind != "convgelu" else 0)
                        if kind == "swiglu":
                            dve.wait_ge(sig("tile_act").handle, u + (b["tile_act"] + 1))
                            dve.wait_ge(marks.handle, u * 2 + (b["marks"] + 2))
                            nc.vector.tensor_tensor(res, buf(j, 0), ps[:, up, :], ALU.mult).then_inc(sig(mul).handle, 1)
                        else:
                            nt = 2 if kind == "conv" else 1
                            for t in range(nt):
                                m = u + HT * t
                                c = buf(j, t)
                                bank = bank_of(g, j, t)
                                dve.wait_ge(sig("tap_act").handle, u * nt + (b["tap_act"] + t + 1))
                                nc.vector.scalar_tensor_tensor(c[:, 1:T], ps[:, bank, 0:T - 1], taps(1, m), c[:, 1:T],
                                                               ALU.mult, ALU.add).then_inc(sig("tap_step").handle, 1)
                                dve.wait_ge(sig("tap_step").handle, u * nt + (b["tap_step"] + t + 1))
                                nc.vector.scalar_tensor_tensor(c[:, 2:T], ps[:, bank, 0:T - 2], taps(0, m), c[:, 2:T],
                                                               ALU.mult, ALU.add).then_inc(sig("tile_dve").handle, 1)
                            dve.wait_ge(sig("gate_act").handle, u + (b["gate_act"] + 1))
                            if kind == "conv":
                                dve.wait_ge(sig("tile_dve").handle, u * 2 + (b["tile_dve"] + 2))
                                other = buf(j, 1)
                            else:
                                dve.wait_ge(marks.handle, u * 2 + (b["marks"] + 2))
                                other = ps[:, up, :]
                            nc.vector.tensor_tensor(res, buf(j, 0), other, ALU.mult).then_inc(sig(mul).handle, 1)
                        dve.wait_ge(sig("hid_hi").handle, u + (b["hid_hi"] + 1))
                        nc.vector.tensor_tensor(at_tile(hid_lo, u), res, at_tile(hid_hi, u).bitcast(F32), ALU.subtract)\
                          .then_inc(sig("hidden_done").handle, 1)
                    units(dve, g, emit)
                    take(dve, tag + "_out", "tile_dve", [0], rj[3], split_lo)

        GELU = ACT.Gelu_apprx_tanh
        def flat(view):
            return view.rearrange("p k t -> p (k t)")

        def merge_job(name, x, gate, total=None):
            nt = len(plan[name].tiles)

            def fn(u, t, bank):
                m = u * nt + t
                first = nc.vector.tensor_tensor(gate[:, m, :], gate[:, m, :], ps[:, bank, :], ALU.mult)
                if total is None:
                    return first
                first.then_inc(*sig("merge_step").up())
                nc.vector.wait_ge(sig("merge_step").handle, sig("merge_step").total)
                return nc.vector.tensor_tensor(total[:, m, :], total[:, m, :], gate[:, m, :], ALU.add)
            return name, x, "dve", fn

        PACK = [0, 512, 1024, 896]
        WIDE = [T - P * j for j in range(TT)]
        CAUSAL = sum(WIDE)

        def modulation(first):
            act_c = small[:, 0:8]
            with phase() as block:
                @block.sync
                def _(sp):
                    for k in range(KT):
                        sp.dma_start(big_words(3, 2048 * k, 2048), a["w_ada"][0, k * P:k * P + P, 0:2048])\
                          .then_inc(sig("ada_in").handle, 16)

                @block.scalar
                def _(act):
                    nc.scalar.activation(act_c, cols[:, COLUMN["c"]:COLUMN["c"] + KT], ACT.Silu)\
                      .then_inc(*sig("c_ready").up())

                @block.tensor
                def _(pe):
                    pe.wait_ge(*sig("ada_summed").at(1))
                    ada_columns(pe, ADA[0], 0)

                @block.vector
                def _(dve):
                    dve.wait_ge(*sig("c_ready").at(1))
                    step = stepper(dve, "mod_step")
                    dve.wait_ge(sig("ada_in").handle, 16 * KT)
                    for k in range(KT):
                        last = ada_add(ADA[0], big_words(3, 2048 * k, 2048), k)
                        if k < KT - 1:
                            step(last)
                    last.then_inc(*sig("ada_summed").up())
                    dve.wait_ge(*sig("ada_columns").at(1))
                    mod_bias(step, 0, 2)

        def big_words(i, at, n):
            return arena_t[:, :, :].rearrange("p k t -> p (k t)")[:, 4096 * i + at:4096 * i + at + n]

        ADA = [big_words(8, 0, 2048), rows[:, :, :].rearrange("p k t -> p (k t)")]

        def ada_add(acc, w, k):
            c = small[:, k:k + 1]
            if k == 0:
                return nc.vector.tensor_scalar(acc, w, c, None, ALU.mult)
            return nc.vector.scalar_tensor_tensor(acc, w, c, acc, ALU.mult, ALU.add)

        def ada_columns(pe, acc, part):
            for m in range(16):
                last = nc.tensor.matmul(ps[:, 7, 16 * part + m:16 * part + m + 1], acc[:, m * P:m * P + P],
                                        const("ones")[:, 0:1], start=True, stop=True)
            last.then_inc(*sig("ada_columns").up())

        def mod_bias(step, lo, hi):
            c = slice(lo * KT, hi * KT)
            b = COLUMN["b_ada"]
            step(nc.vector.tensor_tensor(mod[:, c], ps[:, 7, c], cols[:, b + lo * KT:b + hi * KT], ALU.add))
            for part in (1, 2, 4, 5):
                if lo <= part < hi:
                    v = mod[:, part * KT:part * KT + KT]
                    step(nc.vector.tensor_scalar(v, v, 1.0, None, ALU.add))

        def ada_rest_add(dve, name, u):
            first = {"qk": 0, "v": 4, "u": 6}.get(name)
            if first is None:
                return
            for n in (2 * (first + u), 2 * (first + u) + 1):
                half, k = n // KT, n % KT
                dve.wait_ge(sig(f"ada_slot{n % 2}").handle, 16 * (n // 2 + 1))
                if k:
                    dve.wait_ge(*sig("ada_step").at(n))
                ada_add(ADA[half], big_words(3, 2048 * (n % 2), 2048), k).then_inc(*sig("ada_step").up())

        def ada_rest(engine, eng, name):
            if engine == "gpsimd":
                for n in range(16):
                    half, k = n // KT, n % KT
                    if n >= 2:
                        eng.wait_ge(*sig("ada_step").at(n - 1))
                    eng.dma_start(big_words(3, 2048 * (n % 2), 2048),
                                  a["w_ada"][0, k * P:k * P + P, 2048 * (half + 1):2048 * (half + 2)])\
                       .then_inc(sig(f"ada_slot{n % 2}").handle, 16)
            elif engine == "tensor" and name in ("v", "gates"):
                half = int(name == "gates")
                eng.wait_ge(*sig("ada_step").at(8 * (half + 1)))
                ada_columns(eng, ADA[half], half + 1)
            elif engine == "vector":
                eng.wait_ge(*sig("ada_columns").at(2))
                mod_bias(stepper(eng, "mod_step"), 2, 6)

        def mod_col(part):
            def at(k):
                i = part * KT + k
                return mod[:, i:i + 1] if isinstance(i, int) else mod[:, bass.ds(i, 1)]
            return at

        def stick_breaking(QK, V, out_view):
            scale = 64 ** -0.5
            f7, f8 = flat(big(1)), flat(big(2))
            LB = [f7[:, 0:CAUSAL], f7[:, CAUSAL:2 * CAUSAL]]
            OM = [f7[:, 2 * CAUSAL:3 * CAUSAL], f8[:, 0:CAUSAL]]
            EX = [f8[:, CAUSAL:2 * CAUSAL], f8[:, 2 * CAUSAL:3 * CAUSAL]]
            Z = ps[:, 0:3, :].rearrange("p b n -> p (b n)")
            AFTER = ps[:, 3:6, :].rearrange("p b n -> p (b n)")
            with phase() as block:
                @block.tensor
                def _(pe):
                    def scores(h):
                        r = 64 * (h % 2)
                        if h:
                            pe.wait_ge(*sig("scores_taken").at(h))
                        for j in range(TT):
                            last = nc.tensor.matmul(Z[:, PACK[j]:PACK[j] + WIDE[j]],
                                                    QK[r:r + 64, 4 + h // 2, j * P:(j + 1) * P],
                                                    QK[r:r + 64, h // 2, j * P:T], start=True, stop=True)
                        last.then_inc(*sig("scores_ready").up())
                    scores(0)
                    for h in range(8):
                        r = 64 * (h % 2)
                        if h + 1 < 8:
                            scores(h + 1)
                        pe.wait_ge(*sig("stick_ready").at(h + 1))
                        if h:
                            pe.wait_ge(*sig("weight_ready").at(h))
                        om = OM[h % 2]
                        for i in range(TT):
                            for j in range(i, TT):
                                last = nc.tensor.matmul(
                                    AFTER[:, PACK[i] + P * (j - i):PACK[i] + WIDE[i]],
                                    const("later" if i == j else "ones"),
                                    om[:, PACK[j]:PACK[j] + WIDE[j]], start=j == i, stop=j == TT - 1)
                        last.then_inc(*sig("after_ready").up())
                        pe.wait_ge(*sig("weight_masked").at(h + 1))
                        if h >= 2:
                            pe.wait_ge(*sig("head_out").at(h - 1))
                        for j in range(TT):
                            last = nc.tensor.matmul(ps[r:r + 64, 6 + h % 2, j * P:T], V[:, j, 64 * h:64 * h + 64],
                                                    EX[h % 2][:, PACK[j]:PACK[j] + WIDE[j]],
                                                    start=j == 0, stop=j == TT - 1)
                        last.then_inc(*sig("values_ready").up())

                @block.scalar
                def _(act):
                    step = stepper(act, "act_step")
                    for h in range(8):
                        ex = EX[h % 2]
                        act.wait_ge(*sig("scores_taken").at(h + 1))
                        if h >= 2:
                            act.wait_ge(*sig("values_ready").at(h - 1))
                        step(nc.scalar.activation(ex, OM[h % 2], ACT.Abs))
                        step(nc.scalar.activation(ex, ex, ACT.Exp, scale=-1.0))
                        nc.scalar.activation(ex, ex, ACT.Ln, bias=1.0).then_inc(*sig("soft_ready").up())
                        act.wait_ge(*sig("log_weight").at(h + 1))
                        nc.scalar.activation(ex, LB[h % 2], ACT.Exp).then_inc(*sig("weight_ready").up())

                @block.vector
                def _(dve):
                    step = stepper(dve, "dve_step")
                    for h in range(8):
                        lb, om, ex = LB[h % 2], OM[h % 2], EX[h % 2]
                        dve.wait_ge(*sig("scores_ready").at(h + 1))
                        nc.vector.tensor_scalar(om, Z[:, 0:CAUSAL], scale, None, ALU.mult)\
                          .then_inc(*sig("scores_taken").up())
                        dve.wait_ge(*sig("soft_ready").at(h + 1))
                        step(nc.vector.scalar_tensor_tensor(lb, om, 0.0, ex, ALU.min, ALU.subtract))
                        step(nc.vector.tensor_tensor(om, lb, om, ALU.subtract))
                        for j in range(TT):
                            d = om[:, PACK[j]:PACK[j] + P]
                            last = nc.vector.tensor_tensor(d, d, const("before"), ALU.mult)
                        last.then_inc(*sig("stick_ready").up())
                        dve.wait_ge(*sig("after_ready").at(h + 1))
                        nc.vector.tensor_tensor(lb, lb, AFTER[:, 0:CAUSAL], ALU.add).then_inc(*sig("log_weight").up())
                        dve.wait_ge(*sig("weight_ready").at(h + 1))
                        for j in range(TT):
                            d = ex[:, PACK[j]:PACK[j] + P]
                            last = nc.vector.tensor_tensor(d, d, const("before"), ALU.mult)
                        last.then_inc(*sig("weight_masked").up())
                        dve.wait_ge(*sig("values_ready").at(h + 1))
                        r = 64 * (h % 2)
                        nc.vector.tensor_copy(out_view[r:r + 64, h // 2, :], ps[r:r + 64, 6 + h % 2, :])\
                          .then_inc(*sig("head_out").up())

        def block1():
            c1 = lambda n: (lambda k: col(n, k))
            modulation(True)
            normalize(X, KT, True, LN_EPS, mod_col(1), mod_col(0), split=(act_hi, act_lo))
            QK, V, U = big(4), part_of(5, 0, 4), part_of(5, 4, 8)
            G2 = arena_t[:, 48:64, :]
            YSB, YS = part_of(8, 0, 4), part_of(4, 4, 8)
            products([fjob("qk", ACTS, QK), tjob("v", ACTS, V), fjob("u", ACTS, U),
                      fjob("gates", ACTS, G2, ACT.Sigmoid)], ada_rest_add, ada_rest)
            stick_breaking(QK, V, YSB)
            s5(U, YS)
            YG, GL = part_of(3, 4, 8), part_of(3, 0, 4)

            def skip(dve):
                for k in range(4):
                    last = nc.vector.scalar_tensor_tensor(YG[:, k, :], U[:, k, :], col("ssm_d", k), YS[:, k, :],
                                                          ALU.mult, ALU.add)
                last.then_inc(*sig("skip_added").up())

            def gelu(act):
                act.wait_ge(*sig("skip_added").at(1))
                nc.scalar.activation(YG, YG, GELU).then_inc(*sig("gelu_done").up())
                act.wait_ge(*sig("gelu_done").at(1))
            split_phase([(YSB, act_hi[:, 0:4], act_lo[:, 0:4]), (YG, act_hi[:, 4:8], act_lo[:, 4:8])], (skip, gelu))
            products([merge_job("sb_up", ACTS, big(6)),
                      fjob("glu", parts(act_hi, act_lo, 4), GL, ACT.Sigmoid, bias=c1("b_glu"))])

            def gated(dve):
                nc.vector.tensor_tensor(YG, YG, GL, ALU.mult).then_inc(*sig("glu_done").up())

            def gated_wait(act):
                act.wait_ge(*sig("glu_done").at(1))
            split_phase([(YG, act_hi[:, 0:4], act_lo[:, 0:4])], (gated, gated_wait))
            products([merge_job("ssm_up", ACTS, big(7), big(6))])

            def scaled(dve):
                nc.vector.tensor_scalar(X, X, ALPHA, None, ALU.mult)
            split_phase([(big(6), act_hi, act_lo)], (scaled, lambda act: None))
            products([resjob("out1", ACTS, mod_col(2))])
            normalize(X, KT, True, LN_EPS, c1("ln1_g"), c1("ln1_b"), dst=X)
            normalize(X, KT, True, LN_EPS, mod_col(4), mod_col(3), split=(act_hi, act_lo))
            ffn_phase("ffn1", "swiglu", gain=mod_col(5))
            normalize(X, KT, True, LN_EPS, c1("ln2_g"), c1("ln2_b"), dst=X)

        def s5(U, YS):
            L, NCH, NP = 8, T // 8, 16

            def words(i, at, n):
                return big_words(i, at, n)

            def v16(i):
                return small[:, 16 + 16 * i:32 + 16 * i]
            (dt, lr, li, kq, red, mag, sn, sh, Lr, Li, den, xr, fr, fi, t0, t1, s2) = (v16(i) for i in range(17))
            L8, L8i, T1, T2 = (small[:, 320 + 32 * i:352 + 32 * i] for i in range(4))
            nat = words(3, 0, 1024)
            Bnat = nat[:, 0:512].rearrange("p (r j c) -> p r j c", r=2, j=NP)
            Cnat = nat[:, 512:1024].rearrange("p (r m s) -> p r m s", r=2, m=4)
            rowsf = rows[:, :, :].rearrange("p a n -> p (a n)")
            Cpad = rowsf[:, 0:1024].rearrange("p (r m g s) -> p r m g s", r=2, m=4, g=2)
            tA = rowsf[:, 1024:1536].rearrange("p (j c) -> p j c", j=NP)
            tB = rowsf[:, 1536:2048].rearrange("p (j c) -> p j c", j=NP)
            R = words(1, 0, 8192).rearrange("p (r j d c) -> p r j d c", r=2, j=NP, d=L)
            BB = words(3, 4608, 1024).rearrange("p (r j c) -> p r j c", r=2, j=NP)
            RT = words(3, 0, 8192).rearrange("p (r h j s) -> p r h j s", r=2, h=2, j=NP)
            US = words(5, 0, 2048).rearrange("p (h j n) -> p h j n", h=2, j=NP)
            KB = words(5, 0, 2048).rearrange("p (b d c) -> p b d c", b=2, d=L)
            HS = words(1, 1024, 65 * 32).rearrange("p (n r j) -> p n r j", r=2, j=NP)
            Gn = words(1, 3104, 4608).rearrange("p (d j c) -> p d j c", d=9, j=NP)
            Gr = words(3, 0, 4608).rearrange("p (d j c) -> p d j c", d=9, j=NP)
            ldt = rowsf[0:16, 0:2]
            ldtw = rowsf[0:16, 128:256]
            ab = (COLUMN["ssm_a_re"], COLUMN["ssm_a_im"])
            ar, ai = cols[:, ab[0]:ab[0] + 16], cols[:, ab[1]:ab[1] + 16]
            PI2 = 2 * math.pi
            C1 = 6.28125
            C2 = float(np.float32(PI2 - C1) - np.float32(PI2 - C1) % np.float32(2.0 ** -21))
            C3 = float(np.float32(PI2 - C1 - C2))
            MAGIC = 1.5 * 2.0 ** 23
            UV = U.rearrange("p m (n l) -> p m n l", l=L)
            with phase() as block:
                @block.sync
                def _(sp):
                    sp.dma_start(ldt, a["ssm_log_dt"][0].rearrange("(j g) -> j g", g=2)).then_inc(sig("ssm_loaded").handle, 16)
                    for r, (b, c) in enumerate((("ssm_b_re", "ssm_c_re"), ("ssm_b_im", "ssm_c_im"))):
                        sp.dma_start(Bnat[:, r], a[b][0].rearrange("(j g) s c -> (g s) j c", g=2))\
                          .then_inc(sig("ssm_loaded").handle, 16)
                        sp.dma_start(Cnat[:, r], a[c][0].rearrange("g c s -> (g c) s")
                                     .rearrange("(m q) s -> q m s", q=P)).then_inc(sig("ssm_loaded").handle, 16)

                @block.vector
                def _(dve):
                    step = stepper(dve, "dve_step")
                    dve.wait_ge(sig("ssm_loaded").handle, 80)
                    step(nc.vector.tensor_copy(ldtw.rearrange("p (g s) -> p g s", g=2),
                                               ldt.rearrange("p (g s) -> p g s", s=1).broadcast_to([16, 2, 64])))
                    nc.vector.tensor_copy(ldtw, ldtw).then_inc(*sig("dt_rows").up())
                    dve.wait_ge(*sig("dt_ready").at(1))
                    TS, TTT, STT = nc.vector.tensor_scalar, nc.vector.tensor_tensor, nc.vector.scalar_tensor_tensor
                    TTT(lr, ar, dt, ALU.mult)
                    step(TTT(li, ai, dt, ALU.mult))
                    step(TS(kq, li, 1.0 / PI2, MAGIC, ALU.mult, ALU.add))
                    step(TS(kq, kq, MAGIC, None, ALU.subtract))
                    for c in (C1, C2, C3):
                        step(STT(red if c != C1 else red, kq, -c, li if c == C1 else red, ALU.mult, ALU.add))
                    TS(red, red, 3.1415925, -3.1415925, ALU.min, ALU.max).then_inc(*sig("angle_ready").up())
                    dve.wait_ge(*sig("polar_ready").at(1))
                    step(TTT(t0, sh, sh, ALU.mult))
                    step(TS(t0, t0, -2.0, 1.0, ALU.mult, ALU.add))
                    step(TTT(Lr, mag, t0, ALU.mult))
                    step(TTT(Li, mag, sn, ALU.mult))
                    step(TTT(t0, ar, ar, ALU.mult))
                    step(TTT(t1, ai, ai, ALU.mult))
                    step(TTT(den, t0, t1, ALU.add))
                    step(nc.vector.reciprocal(den, den))
                    step(TS(xr, Lr, 1.0, None, ALU.subtract))
                    step(TTT(t0, xr, ar, ALU.mult))
                    step(TTT(t1, Li, ai, ALU.mult))
                    step(TTT(t0, t0, t1, ALU.add))
                    step(TTT(fr, t0, den, ALU.mult))
                    step(TTT(t0, Li, ar, ALU.mult))
                    step(TTT(t1, xr, ai, ALU.mult))
                    step(TTT(t0, t0, t1, ALU.subtract))
                    step(TTT(fi, t0, den, ALU.mult))
                    for r in range(2):
                        for g in range(2):
                            step(TS(Cpad[:, r, :, g, :], Cnat[:, r], const(f"group{g}", 1), None, ALU.mult))
                    nc.vector.tensor_copy(s2, fr).then_inc(*sig("c_padded").up())
                    step(nc.vector.memset(R[:, :, :, 0, :], 0.0))
                    for g in range(2):
                        q = slice(64 * g, 64 * g + 64)
                        c = slice(16 * g, 16 * g + 16)
                        br, bi = Bnat[q, 0], Bnat[q, 1]
                        FR, FI = bl(fr[q], 16), bl(fi[q], 16)
                        step(TTT(tA[q, :, 0:16], br, FR, ALU.mult))
                        step(TTT(tB[q, :, 0:16], bi, FI, ALU.mult))
                        step(TTT(R[q, 0, :, 0, c], tA[q, :, 0:16], tB[q, :, 0:16], ALU.subtract))
                        step(TTT(tA[q, :, 0:16], br, FI, ALU.mult))
                        step(TTT(tB[q, :, 0:16], bi, FR, ALU.mult))
                        step(TTT(R[q, 1, :, 0, c], tA[q, :, 0:16], tB[q, :, 0:16], ALU.add))
                    LR, LI = bl(Lr, 32), bl(Li, 32)
                    for d in range(1, L):
                        pr, pi = R[:, 0, :, d - 1, :], R[:, 1, :, d - 1, :]
                        step(TTT(tA, pr, LR, ALU.mult))
                        step(TTT(tB, pi, LI, ALU.mult))
                        step(TTT(R[:, 0, :, d, :], tA, tB, ALU.subtract))
                        step(TTT(tA, pr, LI, ALU.mult))
                        step(TTT(tB, pi, LR, ALU.mult))
                        step(TTT(R[:, 1, :, d, :], tA, tB, ALU.add))
                    nc.vector.tensor_copy(s2, fr).then_inc(*sig("powers_ready").up())
                    cr, ci = Lr, Li
                    er, ei = xr, mag
                    for _ in range(3):
                        step(TTT(t0, cr, cr, ALU.mult))
                        step(TTT(t1, ci, ci, ALU.mult))
                        step(TTT(s2, cr, ci, ALU.mult))
                        step(TTT(er, t0, t1, ALU.subtract))
                        step(TS(ei, s2, 2.0, None, ALU.mult))
                        cr, ci = er, ei
                    step(nc.vector.tensor_copy(L8[:, 0:16], cr))
                    step(nc.vector.tensor_copy(L8[:, 16:32], cr))
                    step(TS(L8i[:, 0:16], ci, -1.0, None, ALU.mult))
                    step(nc.vector.tensor_copy(L8i[:, 16:32], ci))
                    dve.wait_ge(*sig("chunks_in").at(1))
                    nc.vector.tensor_copy(BB, R[:, :, :, 0, :]).then_inc(*sig("input_kept").up())
                    dve.wait_ge(*sig("input_kept").at(1))
                    step(nc.vector.memset(HS[:, 0], 0.0))
                    for r in range(2):
                        step(nc.vector.tensor_copy(HS[:, 1:65, r, :].rearrange("p n j -> p j n"),
                                                   ps[:, 4 + 2 * r:6 + 2 * r, :].rearrange("p b (j n) -> p (b j) n", n=64)))
                    nc.vector.memset(KB, 0.0).then_inc(*sig("states_in").up())
                    base = sig("scan_step").total
                    with dve.Fori(0, NCH - 2) as i:
                        def state(k, lo, hi):
                            return HS.rearrange("p n r j -> p n (r j)")[:, bass.ds(i + k, 1), lo:hi]\
                                .rearrange("p a c -> p (a c)")
                        h = sig("scan_step").handle
                        nc.vector.tensor_tensor(T1, state(1, 0, 32), L8, ALU.mult).then_inc(h, 1)
                        nc.vector.tensor_tensor(T2[:, 0:16], state(1, 16, 32), L8i[:, 0:16], ALU.mult).then_inc(h, 1)
                        nc.vector.tensor_tensor(T2[:, 16:32], state(1, 0, 16), L8i[:, 16:32], ALU.mult).then_inc(h, 1)
                        dve.wait_ge(h, i * 5 + (base + 3))
                        nc.vector.tensor_tensor(T2, T1, T2, ALU.add).then_inc(h, 1)
                        dve.wait_ge(h, i * 5 + (base + 4))
                        nc.vector.tensor_tensor(state(2, 0, 32), state(2, 0, 32), T2, ALU.add).then_inc(h, 1)
                        dve.wait_ge(h, i * 5 + (base + 5))
                    sig("scan_step").total += 5 * (NCH - 2)
                    nc.vector.tensor_copy(s2, fr).then_inc(*sig("scanned").up())
                    for m in range(4):
                        dve.wait_ge(*sig("kernel_ready").at(m + 1))
                        if m >= 2:
                            dve.wait_ge(*sig("inside_done").at(m - 1))
                        for q in range(4):
                            w = slice(32 * q, 32 * q + 32)
                            last = nc.vector.tensor_copy(KB[w, m % 2, :, w],
                                                         ps[w, m % 2, 0:256].rearrange("p (d c) -> p d c", d=L))
                        last.then_inc(*sig("kernel_out").up())

                @block.scalar
                def _(act):
                    act.wait_ge(*sig("dt_turned").at(1))
                    nc.scalar.activation(dt, ps[:, 0, 0:16], ACT.Exp).then_inc(*sig("dt_ready").up())
                    act.wait_ge(*sig("angle_ready").at(1))
                    nc.scalar.activation(mag, lr, ACT.Exp)
                    nc.scalar.activation(sn, red, ACT.Sin)
                    nc.scalar.activation(sh, red, ACT.Sin, scale=0.5).then_inc(*sig("polar_ready").up())
                    for d in range(L):
                        for q in range(4):
                            last = nc.scalar.activation(
                                US[32 * (d % 4):32 * (d % 4) + 32, d // 4].rearrange("p (m r) n -> p r m n", r=4)[:, q],
                                UV[32 * q:32 * q + 32, :, :, L - 1 - d], ACT.Copy)
                    last.then_inc(*sig("steps_stacked").up())
                    for n in range(16):
                        r, h, j = n // 8, n // 4 % 2, 4 * (n % 4)
                        act.wait_ge(*sig("power_turned").at(n + 1))
                        nc.scalar.activation(RT[:, r, h, j:j + 4, :].rearrange("p j s -> p (j s)"), ps[:, n % 4, :],
                                             ACT.Copy).then_inc(*sig("power_out").up())
                    act.wait_ge(*sig("input_kept").at(1))
                    act.wait_ge(*sig("c_turned").at(1))
                    nc.scalar.activation(Gr[:, 0].rearrange("p j c -> p (j c)"), ps[:, 0, :], ACT.Copy)
                    nc.scalar.activation(Gn[:, 0].rearrange("p j c -> p (j c)"), ps[:, 1, :], ACT.Copy, scale=-1.0)\
                      .then_inc(*sig("g_first").up())
                    for m in range(4):
                        act.wait_ge(*sig("y_ready").at(m + 1))
                        nc.scalar.activation(YS[:, m, :], ps[:, 4 + m, :], ACT.Copy)

                @block.gpsimd
                def _(pool):
                    step = stepper(pool, "pool_step")
                    pool.wait_ge(*sig("g_first").at(1))
                    pool.wait_ge(*sig("powers_ready").at(1))
                    LR, LI = bl(Lr, 32), bl(Li, 32)
                    TTT = nc.gpsimd.tensor_tensor
                    for d in range(1, L + 1):
                        step(TTT(tA, Gr[:, d - 1], LR, ALU.mult))
                        step(TTT(tB, Gn[:, d - 1], LI, ALU.mult))
                        step(TTT(Gr[:, d], tA, tB, ALU.add))
                        step(TTT(tA, Gn[:, d - 1], LR, ALU.mult))
                        step(TTT(tB, Gr[:, d - 1], LI, ALU.mult))
                        last = TTT(Gn[:, d], tA, tB, ALU.subtract)
                        if d < L:
                            step(last)
                    last.then_inc(*sig("g_ready").up())

                @block.tensor
                def _(pe):
                    pe.wait_ge(*sig("dt_rows").at(1))
                    nc.tensor.transpose(ps[:, 0, 0:16], ldtw, ident[0:16, 0:16]).then_inc(*sig("dt_turned").up())
                    pe.wait_ge(*sig("powers_ready").at(1))
                    for n in range(16):
                        r, h, j = n // 8, n // 4 % 2, 4 * (n % 4)
                        if n >= 4:
                            pe.wait_ge(*sig("power_out").at(n - 3))
                        for q in range(4):
                            last = nc.tensor.transpose(ps[:, n % 4, q * P:(q + 1) * P],
                                                       R[:, r, j + q, 4 * h:4 * h + 4, :].rearrange("p d c -> p (d c)"), ident)
                        last.then_inc(*sig("power_turned").up())
                    pe.wait_ge(*sig("steps_stacked").at(1))
                    pe.wait_ge(*sig("power_out").at(16))
                    for r in range(2):
                        for j in range(NP):
                            for h in range(2):
                                last = nc.tensor.matmul(ps[:, 4 + 2 * r + j // 8, 64 * (j % 8):64 * (j % 8) + 64],
                                                        RT[:, r, h, j, :], US[:, h, j, :], start=h == 0, stop=h == 1)
                    last.then_inc(*sig("chunks_in").up())
                    pe.wait_ge(*sig("chunks_in").at(1))
                    for r in range(2):
                        for m in range(4):
                            last = nc.tensor.transpose(ps[:, r, m * P:(m + 1) * P],
                                                       Cpad[:, r, m].rearrange("p g s -> p (g s)"), ident)
                    last.then_inc(*sig("c_turned").up())
                    pe.wait_ge(*sig("g_ready").at(1))
                    pe.wait_ge(*sig("states_in").at(1))

                    def kernels(m):
                        if m >= 2:
                            pe.wait_ge(*sig("kernel_out").at(m - 1))
                        for q in range(4):
                            o = ps[32 * q:32 * q + 32, m % 2, 0:256]
                            nc.tensor.matmul(o, BB[:, 0, 4 * m + q, :], Gr[:, 0:L, 4 * m + q, :], start=True, stop=False)
                            last = nc.tensor.matmul(o, BB[:, 1, 4 * m + q, :], Gn[:, 0:L, 4 * m + q, :], start=False, stop=True)
                        last.then_inc(*sig("kernel_ready").up())
                    kernels(0)
                    for m in range(4):
                        if m < 3:
                            kernels(m + 1)
                        y = ps[:, 4 + m, :].rearrange("p (n l) -> p n l", l=L)
                        pe.wait_ge(*sig("kernel_out").at(m + 1))
                        pe.wait_ge(*sig("scanned").at(1))
                        for d in range(L):
                            last = nc.tensor.matmul(y[:, :, d:L], KB[:, m % 2, d, :], UV[:, m, :, 0:L - d],
                                                    start=d == 0, stop=False, skip_group_check=True)
                        last.then_inc(*sig("inside_done").up())
                        for q in range(4):
                            for t in range(L):
                                for G, r in ((Gr, 0), (Gn, 1)):
                                    last = nc.tensor.matmul(y[32 * q:32 * q + 32, :, t], G[:, t + 1, 4 * m + q, :],
                                                            HS[:, 0:NCH, r, 4 * m + q], start=False, stop=True,
                                                            skip_group_check=True)
                        last.then_inc(*sig("y_ready").up())
        def gla(AQ, AK, V, ALR, W2, AR, OUT):
            NC = T // 64
            B, DM, DL = part_of(1, 0, 2), part_of(1, 2, 4), part_of(1, 4, 6)
            E1, E2, E3, E4 = (part_of(2, 2 * i, 2 * i + 2) for i in range(4))
            QD, KD, KE, QE = (part_of(6, 2 * i, 2 * i + 2) for i in range(4))
            KTOK = flat(part_of(7, 4, 6)).rearrange("p (m i c) -> p m i c", m=2, i=TT)
            ATT = part_of(1, 4, 8)
            S = flat(part_of(7, 0, 4)).rearrange("p (m n v) -> p m n v", m=2, n=NC)
            O, SQ = part_of(2, 0, 4), part_of(2, 4, 8)
            VAR = part_of(6, 0, 4)
            KEEP = flat(part_of(5, 7, 8))

            def ch(v):
                return v.rearrange("p m (n l) -> p (m n) l", l=64)

            def point(v, k):
                return ch(v)[:, :, k:k + 1].broadcast_to([P, 2 * NC, 64])
            with phase() as block:
                @block.sync
                def _(sp):
                    sp.dma_start(W2, a["gla_w_a2_2"][0]).then_inc(sig("gate_w").handle, 16)
                    at = CONST_AT["keep64"]
                    sp.dma_start(KEEP, a["constants"][:, at:at + T]).then_inc(sig("keep_in").handle, 16)

                @block.tensor
                def _(pe):
                    pe.wait_ge(sig("gate_w").handle, 16)
                    for m in range(2):
                        last = nc.tensor.matmul(ps[:, m, :], W2[:, m * P:m * P + P], ALR, start=True, stop=True)
                    last.then_inc(*sig("decay_in").up())
                    pe.wait_ge(*sig("gla_factors").at(1))
                    for m in range(2):
                        for i in range(TT):
                            last = nc.tensor.transpose(ps[:, 2 + m, i * P:i * P + P], KE[:, m, i * P:i * P + P], ident)
                    last.then_inc(*sig("k_turned").up())
                    for h in range(4):
                        r = 64 * (h % 2)
                        for i in range(TT):
                            w = slice(i * P, i * P + P)
                            last = nc.tensor.matmul(ps[:, 4 + h, w], KD[r:r + 64, h // 2, w], QD[r:r + 64, h // 2, w],
                                                    start=True, stop=True)
                    last.then_inc(*sig("gla_scores").up())
                    pe.wait_ge(*sig("k_tok").at(1))
                    for m in range(2):
                        for n in range(NC - 1):
                            q = slice(64 * (n % 2), 64 * (n % 2) + 64)
                            for g in range(2):
                                h = 2 * m + g
                                last = nc.tensor.matmul(ps[64 * g:64 * g + 64, 2 * m + n % 2, P * (n // 2):P * (n // 2) + P],
                                                        KTOK[q, m, n // 2, 64 * g:64 * g + 64],
                                                        V[q, n // 2, h * P:h * P + P], start=True, stop=True)
                    last.then_inc(*sig("state_adds").up())
                    pe.wait_ge(*sig("att_masked").at(1))
                    pe.wait_ge(*sig("states_ready").at(1))
                    for h in range(4):
                        r = 64 * (h % 2)
                        for i in range(TT):
                            nc.tensor.matmul(ps[:, 4 + h, i * P:i * P + P], V[:, i, h * P:h * P + P],
                                             ATT[:, h, i * P:i * P + P], start=True, stop=False, skip_group_check=True)
                            for n in (2 * i, 2 * i + 1):
                                last = nc.tensor.matmul(ps[:, 4 + h, 64 * n:64 * n + 64], S[r:r + 64, h // 2, n, :],
                                                        QE[r:r + 64, h // 2, 64 * n:64 * n + 64],
                                                        start=False, stop=True, skip_group_check=True)
                    last.then_inc(*sig("heads_ready").up())
                    pe.wait_ge(*sig("heads_squared").at(1))
                    for h in range(4):
                        last = nc.tensor.matmul(ps[:, h, :], const("ones"), SQ[:, h, :], start=True, stop=True)
                    last.then_inc(*sig("heads_summed").up())

                @block.scalar
                def _(act):
                    step = stepper(act, "act_step")
                    act.wait_ge(*sig("decay_in").at(1))
                    for m in range(2):
                        last = nc.scalar.activation(DM[:, m, :], ps[:, m, :], ACT.Identity, bias=col("gla_b_a_2", m))
                    step(last)
                    step(nc.scalar.activation(DL, DM, ACT.Abs))
                    step(nc.scalar.activation(DL, DL, ACT.Exp, scale=-1.0))
                    nc.scalar.activation(DL, DL, ACT.Ln, bias=1.0).then_inc(*sig("soft_ready").up())
                    act.wait_ge(*sig("decays_ready").at(1))
                    nc.scalar.activation(E1, DM, ACT.Exp)
                    nc.scalar.activation(E2, DM, ACT.Exp, scale=-1.0)
                    nc.scalar.activation(E3, DL, ACT.Exp, scale=-1.0)
                    nc.scalar.activation(E4, B, ACT.Exp).then_inc(*sig("exps_ready").up())
                    act.wait_ge(*sig("k_turned").at(1))
                    nc.scalar.activation(KTOK.rearrange("p m i c -> p (m i c)"),
                                         ps[:, 2:4, :].rearrange("p b n -> p (b n)"), ACT.Copy).then_inc(*sig("k_tok").up())
                    act.wait_ge(*sig("heads_ready").at(1))
                    nc.scalar.activation(SQ, ps[:, 4:8, :], ACT.Square).then_inc(*sig("heads_squared").up())
                    act.wait_ge(*sig("variance").at(1))
                    nc.scalar.activation(VAR, VAR, ACT.Sqrt).then_inc(*sig("deviation").up())

                @block.vector
                def _(dve):
                    step = stepper(dve, "dve_step")
                    dve.wait_ge(*sig("soft_ready").at(1))
                    step(nc.vector.tensor_scalar(DM, DM, 0.0, None, ALU.min))
                    step(nc.vector.tensor_tensor(DM, DM, DL, ALU.subtract))
                    step(nc.vector.tensor_scalar(DM, DM, 1.0 / 16.0, None, ALU.mult))
                    dve.wait_ge(sig("keep_in").handle, 16)
                    for m in range(2):
                        step(nc.vector.tensor_tensor_scan(B[:, m, :], KEEP, DM[:, m, :], 0.0, ALU.mult, ALU.add))
                    step(nc.vector.tensor_tensor(ch(DM), ch(B), point(B, 32), ALU.subtract))
                    nc.vector.tensor_tensor(ch(DL), ch(B), point(B, 63), ALU.subtract).then_inc(*sig("decays_ready").up())
                    dve.wait_ge(*sig("exps_ready").at(1))
                    nc.vector.scalar_tensor_tensor(QD, AQ, 0.125, E1, ALU.mult, ALU.mult)
                    nc.vector.tensor_tensor(KD, AK, E2, ALU.mult)
                    nc.vector.tensor_tensor(KE, AK, E3, ALU.mult)
                    nc.vector.scalar_tensor_tensor(QE, AQ, 0.125, E4, ALU.mult, ALU.mult).then_inc(*sig("gla_factors").up())
                    dve.wait_ge(*sig("gla_scores").at(1))
                    m64 = const("chunk64").rearrange("p (a c) -> p a c", a=1).broadcast_to([P, 16, P])
                    nc.vector.tensor_tensor(ATT.rearrange("p h (i c) -> p (h i) c", c=P),
                                            ps[:, 4:8, :].rearrange("p h (i c) -> p (h i) c", c=P), m64, ALU.mult)\
                      .then_inc(*sig("att_masked").up())
                    step(nc.vector.memset(S[:, :, 0, :], 0.0))
                    dve.wait_ge(*sig("state_adds").at(1))
                    for n in range(NC - 1):
                        for m in range(2):
                            last = nc.vector.scalar_tensor_tensor(
                                S[:, m, n + 1, :], S[:, m, n, :], E4[:, m, 64 * n + 63:64 * n + 64],
                                ps[:, 2 * m + n % 2, P * (n // 2):P * (n // 2) + P], ALU.mult, ALU.add)
                        if n < NC - 2:
                            step(last)
                    last.then_inc(*sig("states_ready").up())
                    dve.wait_ge(*sig("heads_summed").at(1))
                    nc.vector.tensor_scalar(VAR, ps[:, 0:4, :], 1.0 / P, RMS_EPS, ALU.mult, ALU.add).then_inc(*sig("variance").up())
                    dve.wait_ge(*sig("deviation").at(1))
                    step(nc.vector.reciprocal(VAR, VAR))
                    step(nc.vector.tensor_tensor(O, ps[:, 4:8, :], VAR, ALU.mult))
                    nc.vector.scalar_tensor_tensor(OUT, O, col("gla_head_g_2", 0), AR, ALU.mult, ALU.mult)

        def rotate(XS):
            TMP = big(1)
            COS, SIN = flat(part_of(2, 0, 1)), flat(part_of(2, 1, 2))
            with phase() as block:
                @block.sync
                def _(sp):
                    for dst, name in ((COS, "cos"), (SIN, "sin")):
                        sp.dma_start(dst, a["constants"][:, CONST_AT[name]:CONST_AT[name] + T])\
                          .then_inc(sig("tables_in").handle, 16)

                @block.tensor
                def _(pe):
                    for t in range(8):
                        last = nc.tensor.matmul(ps[:, t, :], const("turn"), XS[t // 4][:, t % 4, :], start=True, stop=True)
                    last.then_inc(*sig("turned").up())

                @block.vector
                def _(dve):
                    step = stepper(dve, "dve_step")
                    dve.wait_ge(*sig("turned").at(1))
                    dve.wait_ge(sig("tables_in").handle, 32)
                    step(nc.vector.tensor_tensor(TMP, ps[:, :, :], bc(SIN, 8), ALU.mult))
                    for v in XS:
                        step(nc.vector.tensor_tensor(v, v, bc(COS, 4), ALU.mult))
                    for i, v in enumerate(XS):
                        last = nc.vector.tensor_tensor(v, v, TMP[:, 4 * i:4 * i + 4, :], ALU.add)

        MOFF = [0, 128, 384, 768]

        def select_keys(IQ, IK, NB, MASK):
            K, NB3 = TOPK, TT - 1
            f6, f7 = flat(big(1)), flat(big(2))
            SC = [f6[:, 512 * b:512 * b + 512] for b in range(NB3)]
            WK = [f6[:, 1536 + 512 * b:2048 + 512 * b] for b in range(NB3)]
            RL = [f6[:, 3072:3584], f6[:, 3584:4096]]
            ONE, EQ, CUM = (f7[:, 512 * i:512 * i + 512] for i in range(3))
            NS = [P * (b + 2) for b in range(NB3)]
            top = small[:, 0:24]
            cnt = small[:, 24:27]
            iw = small[:, 32:48].rearrange("p (i h) -> p i h", i=TT)
            with phase() as block:
                @block.tensor
                def _(pe):
                    for b in range(NB3):
                        i, ns = 1 + b, NS[b]
                        for h in range(4):
                            r = 64 * (h % 2)
                            if b == 2:
                                pe.wait_ge(*sig("index_relu").at(h + 1))
                            nc.tensor.matmul(ps[:, (4 * b + h) % 8, 0:ns], IQ[r:r + 64, h // 2, i * P:i * P + P],
                                             IK[r:r + 64, 0:ns], start=True, stop=True).then_inc(*sig("index_ready").up())

                @block.scalar
                def _(act):
                    for n in range(4 * NB3):
                        b = n // 4
                        act.wait_ge(*sig("index_ready").at(n + 1))
                        if n >= 2:
                            act.wait_ge(*sig("index_added").at(n - 1))
                        nc.scalar.activation(RL[n % 2][:, 0:NS[b]], ps[:, n % 8, 0:NS[b]], ACT.Relu, scale=0.125)\
                          .then_inc(*sig("index_relu").up())

                @block.vector
                def _(dve):
                    step = stepper(dve, "dve_step")
                    step(nc.vector.tensor_scalar(iw, NB[:, :, 64:68], 0.5, None, ALU.mult))
                    step(nc.vector.memset(ONE, 1.0))
                    step(nc.vector.tensor_copy(MASK[:, 0:P], const("notyet")))
                    for n in range(4 * NB3):
                        b, h = n // 4, n % 4
                        s, rl = SC[b][:, 0:NS[b]], RL[n % 2][:, 0:NS[b]]
                        w = iw[:, 1 + b, h:h + 1]
                        dve.wait_ge(*sig("index_relu").at(n + 1))
                        if h == 0:
                            last = nc.vector.tensor_scalar(s, rl, w, None, ALU.mult)
                        else:
                            last = nc.vector.scalar_tensor_tensor(s, rl, w, s, ALU.mult, ALU.add)
                        last.then_inc(*sig("index_added").up())
                        dve.wait_ge(*sig("index_added").at(n + 1))
                    for b in range(NB3):
                        d = SC[b][:, NS[b] - P:NS[b]]
                        step(nc.vector.tensor_tensor(d, d, const("notyet"), ALU.add))
                        step(nc.vector.tensor_copy(WK[b][:, 0:NS[b]], SC[b][:, 0:NS[b]]))
                    h = sig("top_step")
                    base = h.total
                    with dve.Fori(0, K // 8 - 1) as i:
                        for b in range(NB3):
                            nc.vector.max(top[:, 8 * b:8 * b + 8], WK[b][:, 0:NS[b]]).then_inc(h.handle, 1)
                        dve.wait_ge(h.handle, i * (2 * NB3) + (base + NB3))
                        nc.vector.memset(cnt, 0.0)
                        for b in range(NB3):
                            nc.vector.match_replace(WK[b][:, 0:NS[b]], top[:, 8 * b:8 * b + 8], WK[b][:, 0:NS[b]], NEG)\
                              .then_inc(h.handle, 1)
                        dve.wait_ge(h.handle, i * (2 * NB3) + (base + 2 * NB3))
                    h.total += 2 * NB3 * (K // 8 - 1)
                    for b in range(NB3):
                        ns = NS[b]
                        s, gt, eq, cum = SC[b][:, 0:ns], WK[b][:, 0:ns], EQ[:, 0:ns], CUM[:, 0:ns]
                        m = MASK[:, MOFF[1 + b]:MOFF[1 + b] + ns]
                        step(nc.vector.max(top[:, 8 * b:8 * b + 8], WK[b][:, 0:ns]))
                        th = top[:, 8 * b + 7:8 * b + 8]
                        step(nc.vector.tensor_scalar(gt, s, th, None, ALU.is_gt))
                        step(nc.vector.tensor_scalar(eq, s, th, None, ALU.is_equal))
                        step(nc.vector.tensor_reduce(cnt[:, b:b + 1], gt, AXX, ALU.add))
                        step(nc.vector.tensor_scalar(cnt[:, b:b + 1], cnt[:, b:b + 1], -1.0, float(K), ALU.mult, ALU.add))
                        step(nc.vector.tensor_tensor_scan(cum, ONE[:, 0:ns], eq, 0.0, ALU.mult, ALU.add))
                        step(nc.vector.scalar_tensor_tensor(eq, cum, cnt[:, b:b + 1], eq, ALU.is_le, ALU.mult))
                        step(nc.vector.tensor_tensor(gt, gt, eq, ALU.add))
                        step(nc.vector.tensor_scalar(m, gt, 1.0, -NEG, ALU.subtract, ALU.mult))

        def sparse_attention(BQ, BK, NB, MASK, OUT):
            SOFF = [0, 128, 512, 1024]
            f6, f7, f8 = flat(big(1)), flat(big(2)), flat(big(6))
            SM = [f6[:, 0:CAUSAL], f6[:, CAUSAL:2 * CAUSAL]]
            EX = [f7[:, 0:CAUSAL], f7[:, CAUSAL:2 * CAUSAL]]
            PT = [f8[:, 0:CAUSAL], f8[:, CAUSAL:2 * CAUSAL]]
            S = ps[:, 0:3, :].rearrange("p b n -> p (b n)")
            TP = ps[:, 3:6, :].rearrange("p b n -> p (b n)")
            mx = [small[:, 64 + 4 * i:68 + 4 * i] for i in range(2)]
            nm = [small[:, 72 + 4 * i:76 + 4 * i] for i in range(2)]
            sm = [small[:, 80 + 4 * i:84 + 4 * i] for i in range(2)]
            with phase() as block:
                @block.tensor
                def _(pe):
                    def scores(h):
                        r = 64 * (h % 2)
                        if h:
                            pe.wait_ge(*sig("masked").at(h))
                        for i in range(TT):
                            n = P * (i + 1)
                            last = nc.tensor.matmul(S[:, SOFF[i]:SOFF[i] + n], BQ[r:r + 64, h // 2, i * P:i * P + P],
                                                    BK[r:r + 64, 0:n], start=True, stop=True)
                        last.then_inc(*sig("scores_ready").up())
                    scores(0)
                    for h in range(8):
                        r = 64 * (h % 2)
                        if h < 7:
                            scores(h + 1)
                        pe.wait_ge(*sig("probs_ready").at(h + 1))
                        if h:
                            pe.wait_ge(*sig("probs_out").at(h))
                        for j in range(TT):
                            for i in range(j, TT):
                                last = nc.tensor.transpose(TP[:, PACK[j] + P * (i - j):PACK[j] + P * (i - j) + P],
                                                           EX[h % 2][:, MOFF[i] + j * P:MOFF[i] + j * P + P], ident)
                        last.then_inc(*sig("probs_turned").up())
                        pe.wait_ge(*sig("probs_out").at(h + 1))
                        if h >= 2:
                            pe.wait_ge(*sig("head_out").at(h - 1))
                        for j in range(TT):
                            last = nc.tensor.matmul(ps[r:r + 64, 6 + h % 2, j * P:T], NB[:, j, 0:64],
                                                    PT[h % 2][:, PACK[j]:PACK[j] + WIDE[j]], start=j == 0, stop=j == TT - 1)
                        last.then_inc(*sig("values_ready").up())

                @block.scalar
                def _(act):
                    def turn_out(h):
                        act.wait_ge(*sig("probs_turned").at(h + 1))
                        if h >= 2:
                            act.wait_ge(*sig("values_ready").at(h - 1))
                        nc.scalar.activation(PT[h % 2], TP[:, 0:CAUSAL], ACT.Copy).then_inc(*sig("probs_out").up())
                    for h in range(8):
                        act.wait_ge(*sig("maximum").at(h + 1))
                        if h >= 2:
                            act.wait_ge(*sig("probs_turned").at(h - 1))
                        for i in range(TT):
                            w = slice(MOFF[i], MOFF[i] + P * (i + 1))
                            last = nc.scalar.activation(EX[h % 2][:, w], SM[h % 2][:, w], ACT.Exp, scale=0.125,
                                                        bias=nm[h % 2][:, i:i + 1], accum_out=sm[h % 2][:, i:i + 1])
                        last.then_inc(*sig("exps_ready").up())
                        if h:
                            turn_out(h - 1)
                    turn_out(7)

                @block.vector
                def _(dve):
                    step = stepper(dve, "dve_step")

                    def masked(h):
                        dve.wait_ge(*sig("scores_ready").at(h + 1))
                        if h >= 2:
                            dve.wait_ge(*sig("exps_ready").at(h - 1))
                        for i in range(TT):
                            n = P * (i + 1)
                            w = slice(MOFF[i], MOFF[i] + n)
                            last = nc.vector.tensor_tensor_reduce(
                                out=SM[h % 2][:, w], in0=S[:, SOFF[i]:SOFF[i] + n], in1=MASK[:, w], scale=1.0,
                                scalar=NEG, op0=ALU.add, op1=ALU.max, accum_out=mx[h % 2][:, i:i + 1])
                        last.then_inc(*sig("masked").up())
                        dve.wait_ge(*sig("masked").at(h + 1))
                        nc.vector.tensor_scalar(nm[h % 2], mx[h % 2], -0.125, None, ALU.mult).then_inc(*sig("maximum").up())
                    masked(0)
                    for h in range(8):
                        if h < 7:
                            masked(h + 1)
                        dve.wait_ge(*sig("exps_ready").at(h + 1))
                        step(nc.vector.reciprocal(sm[h % 2], sm[h % 2]))
                        for i in range(TT):
                            w = slice(MOFF[i], MOFF[i] + P * (i + 1))
                            last = nc.vector.tensor_scalar(EX[h % 2][:, w], EX[h % 2][:, w], sm[h % 2][:, i:i + 1],
                                                           None, ALU.mult)
                        last.then_inc(*sig("probs_ready").up())
                        r = 64 * (h % 2)
                        dve.wait_ge(*sig("values_ready").at(h + 1))
                        nc.vector.tensor_copy(OUT[r:r + 64, h // 2, :], ps[r:r + 64, 6 + h % 2, :])\
                          .then_inc(*sig("head_out").up())

        def sgu(U, V):
            f4, f5 = flat(big(5)), flat(big(6))
            GB, BB, BS = f4[:, 0:1024], f4[:, 1024:2048], f4[:, 2048:3072].rearrange("p (g t) -> p g t", g=8)
            WS, WT = (f5[:, 1024 * i:1024 * i + 1024].rearrange("p (g s) -> p g s", g=8) for i in range(2))
            st = small[:, 0:48].rearrange("p (i h s) -> p i h s", i=TT, h=2)
            mv = small[:, 48:56].rearrange("p (i s) -> p i s", i=TT)
            sd = small[:, 56:60]
            TMP = [f5[:, 2048:2560], f5[:, 2560:3072]]
            with phase() as block:
                @block.sync
                def _(sp):
                    for dst, name in ((GB, "sgu_ln_g_2"), (BB, "sgu_ln_b_2")):
                        sp.dma_start(dst, a[name].broadcast_to([P, 1024])).then_inc(sig("sgu_rows").handle, 16)
                    sp.dma_start(f4[:, 2048:3072], a["sgu_b_s_2"].rearrange("a g t -> a (g t)").broadcast_to([P, 1024]))\
                      .then_inc(sig("sgu_rows").handle, 16)
                    sp.dma_start(WS, a["sgu_w_s_2"][0].rearrange("g t s -> t g s")).then_inc(sig("sgu_w").handle, 16)

                @block.tensor
                def _(pe):
                    pe.wait_ge(sig("sgu_w").handle, 16)
                    for g in range(8):
                        last = nc.tensor.transpose(ps[:, g // 4, P * (g % 4):P * (g % 4) + P], WS[:, g, :], ident)
                    last.then_inc(*sig("w_turned").up())
                    pe.wait_ge(*sig("v_normed").at(1))
                    for g in range(8):
                        if g >= 4:
                            pe.wait_ge(*sig("mixed_out").at(g - 3))
                        for i in range(TT):
                            last = nc.tensor.matmul(ps[:, 4 + g % 4, i * P:i * P + P], V[:, i, g * P:g * P + P], WT[:, g, :],
                                                    start=True, stop=True)
                        last.then_inc(*sig("mixed").up())

                @block.scalar
                def _(act):
                    act.wait_ge(*sig("variance").at(1))
                    nc.scalar.activation(sd, sd, ACT.Sqrt).then_inc(*sig("deviation").up())

                @block.vector
                def _(dve):
                    step = stepper(dve, "dve_step")
                    for i in range(TT):
                        for h in range(2):
                            last = nc.vector.bn_stats(st[:, i, h, :], V[:, i, 512 * h:512 * h + 512])
                    step(last)
                    for i in range(TT):
                        last = nc.vector.bn_aggr(mv[:, i, :], st[:, i].rearrange("p h s -> p (h s)"))
                    step(last)
                    nc.vector.tensor_scalar(sd, mv[:, :, 1], LN_EPS, None, ALU.add).then_inc(*sig("variance").up())
                    dve.wait_ge(*sig("w_turned").at(1))
                    nc.vector.tensor_tensor(WT, ps[:, 0:2, :].rearrange("p b (g t) -> p (b g) t", t=P),
                                            bc(const("upto"), 8), ALU.mult)
                    dve.wait_ge(*sig("deviation").at(1))
                    step(nc.vector.reciprocal(sd, sd))
                    for i in range(TT):
                        last = nc.vector.tensor_scalar(V[:, i, :], V[:, i, :], mv[:, i, 0:1], sd[:, i:i + 1],
                                                       ALU.subtract, ALU.mult)
                    step(last)
                    dve.wait_ge(sig("sgu_rows").handle, 48)
                    step(nc.vector.tensor_tensor(V, V, bc(GB, TT), ALU.mult))
                    nc.vector.tensor_tensor(V, V, bc(BB, TT), ALU.add).then_inc(*sig("v_normed").up())
                    for g in range(8):
                        dve.wait_ge(*sig("mixed").at(g + 1))
                        t = TMP[g % 2]
                        nc.vector.tensor_tensor(t.rearrange("p (i c) -> p i c", c=P),
                                                ps[:, 4 + g % 4, :].rearrange("p (i c) -> p i c", c=P),
                                                BS[:, g:g + 1, :].broadcast_to([P, TT, P]), ALU.add)\
                          .then_inc(*sig("mixed_out").up())
                        dve.wait_ge(*sig("mixed_out").at(g + 1))
                        nc.vector.tensor_tensor(U[:, g, :], U[:, g, :], t, ALU.mult)

        def column(name, first):
            return lambda k: col(name, k + first)

        def conv_taps(name, first, tiles):
            return lambda j, m: col(name, m + (first + tiles * j))

        def block2():
            normalize(X, KT, False, RMS_EPS, column("attn_norm_2", 0), split=(act_hi, act_lo))
            AQK, AR = part_of(3, 0, 4), part_of(3, 4, 8)
            V, BQ, IQK = part_of(4, 0, 4), part_of(4, 4, 8), part_of(5, 0, 4)
            ALR = part_of(5, 4, 5)[0:16, 0, :]
            NB = part_of(5, 5, 6)[:, 0, 0:272].rearrange("p (i c) -> p i c", i=TT)
            W2 = part_of(5, 6, 7)[0:16, 0, 0:256]
            OA, OB = part_of(8, 0, 4), part_of(7, 0, 4)

            def narrow(u, t, bank):
                if t == 0:
                    return nc.scalar.activation(ALR, ps[0:16, bank, :], ACT.Copy)
                return nc.scalar.activation(NB[:, t - 1, :], ps[:, bank, 0:68], ACT.Copy)
            products([fjob("aqk", ACTS, AQK), tjob("av", ACTS, V), fjob("ar", ACTS, AR, ACT.Silu), fjob("bq", ACTS, BQ),
                      fjob("iq", ACTS, IQK[:, 0:2]), fjob("shared", ACTS, IQK[:, 2:4]), ("narrow", ACTS, "act", narrow)])
            gla(AQK[:, 0:2], AQK[:, 2:4], V, ALR, W2, AR, OA)
            rotate([BQ, IQK])
            MASK = flat(big(3))[:, 0:CAUSAL]
            select_keys(IQK[:, 0:2], IQK[:, 3, :], NB, MASK)
            sparse_attention(BQ, IQK[:, 2, :], NB, MASK, OB)
            split_phase([(OA, act_hi[:, 0:4], act_lo[:, 0:4]), (OB, act_hi[:, 4:8], act_lo[:, 4:8])])
            products([resjob("w_o", ACTS)])

            def ffn_layer(tag, l):
                normalize(X, KT, False, RMS_EPS, column("ffn_norm_2", 8 * l), split=(act_hi, act_lo))
                ffn_phase(tag, "conv", taps=conv_taps("ffn_conv_w_2", 132 * l, 44),
                          tap_bias=column("ffn_conv_b_2", 44 * l))
            ffn_layer("ffn2", 0)
            normalize(X, KT, False, RMS_EPS, column("sgu_norm_2", 0), split=(act_hi, act_lo))
            V2 = big(4).rearrange("p k t -> p (k t)").rearrange("p (i n) -> p i n", i=TT)
            products([fjob("sgu_u", ACTS, big(3), GELU), tjob("sgu_v", ACTS, V2, GELU)])
            sgu(big(3), V2)
            split_phase([(big(3), act_hi, act_lo)])
            products([resjob("sgu_out", ACTS)])
            ffn_layer("ffn3", 1)
            normalize(X, KT, False, RMS_EPS, column("final_norm_2", 0), dst=X)

        def hgrn(Q, Fz, V, K):
            lb, om = small[:, 0:8], small[:, 8:16]
            e0, e1, mm = small[:, 16:24], small[:, 24:32], small[:, 32:40]
            lg = COLUMN["hgrn_lb_logits_3"]
            l0, l1 = cols[:, lg:lg + 8], cols[:, lg + 8:lg + 16]
            LOGS, KEEP = big(1), flat(part_of(2, 0, 1))
            with phase() as block:
                @block.sync
                def _(sp):
                    at = CONST_AT["keep128"]
                    sp.dma_start(KEEP, a["constants"][:, at:at + T]).then_inc(sig("keep3_in").handle, 16)

                @block.vector
                def _(dve):
                    step = stepper(dve, "dve_step")
                    step(nc.vector.tensor_tensor(mm, l0, l1, ALU.max))
                    step(nc.vector.tensor_tensor(e0, l0, mm, ALU.subtract))
                    nc.vector.tensor_tensor(e1, l1, mm, ALU.subtract).then_inc(*sig("logits_ready").up())
                    dve.wait_ge(*sig("logit_exps").at(1))
                    step(nc.vector.tensor_tensor(mm, e0, e1, ALU.add))
                    step(nc.vector.reciprocal(mm, mm))
                    step(nc.vector.tensor_tensor(lb, e0, mm, ALU.mult))
                    step(nc.vector.tensor_scalar(om, lb, -1.0, 1.0, ALU.mult, ALU.add))
                    for k in range(KT):
                        dve.wait_ge(*sig("sigmoids").at(k + 1))
                        nc.vector.tensor_scalar(K[:, k, :], K[:, k, :], om[:, k:k + 1], None, ALU.mult)
                        nc.vector.tensor_scalar(Fz[:, k, :], Fz[:, k, :], om[:, k:k + 1], lb[:, k:k + 1],
                                                ALU.mult, ALU.add).then_inc(*sig("forget_ready").up())
                    dve.wait_ge(sig("keep3_in").handle, 16)
                    for k in range(KT):
                        dve.wait_ge(*sig("log_ready").at(k + 1))
                        nc.vector.tensor_tensor_scan(Fz[:, k, :], KEEP, LOGS[:, k, :], 0.0,
                                                     ALU.mult, ALU.add)

                @block.scalar
                def _(act):
                    act.wait_ge(*sig("logits_ready").at(1))
                    nc.scalar.activation(small[:, 16:32], small[:, 16:32], ACT.Exp).then_inc(*sig("logit_exps").up())
                    for k in range(KT):
                        nc.scalar.activation(K[:, k, :], Fz[:, k, :], ACT.Sigmoid, scale=-1.0).then_inc(*sig("act_step").up())
                        act.wait_ge(sig("act_step").handle, sig("act_step").total)
                        nc.scalar.activation(Fz[:, k, :], Fz[:, k, :], ACT.Sigmoid).then_inc(*sig("sigmoids").up())
                    for k in range(KT):
                        act.wait_ge(*sig("forget_ready").at(k + 1))
                        nc.scalar.activation(LOGS[:, k, :], Fz[:, k, :], ACT.Ln).then_inc(*sig("log_ready").up())
            for half in range(2):
                hgrn_heads(Q[:, 4 * half:4 * half + 4], K[:, 4 * half:4 * half + 4], Fz[:, 4 * half:4 * half + 4], V, 4 * half)

        def hgrn_heads(Q, K, B, V, h0):
            QE, KE, KTOK = part_of(7, 0, 4), part_of(7, 4, 8), part_of(1, 0, 4)
            S = flat(part_of(1, 4, 8)).rearrange("p (h n v) -> p h n v", h=4, n=4)
            ATT, TMP = KE, KTOK
            dec = small[:, 64:80].rearrange("p (h n) -> p h n", h=4)
            C = P
            LEVELS = 7

            def ch(v, l=C):
                return v.rearrange("p h (n l) -> p (h n) l", l=l)

            def halves(v, lv):
                h = 64 >> lv
                return v.rearrange("p h (n s l) -> p (h n) s l", s=2, l=h)
            DIFF = part_of(2, 4, 8)
            XLV = KTOK
            with phase() as block:
                @block.scalar
                def _(act):
                    act.wait_ge(*sig("tail_diff").at(1))
                    nc.scalar.activation(KE, KE, ACT.Exp)
                    nc.scalar.activation(QE, B, ACT.Exp)
                    nc.scalar.activation(dec, B.rearrange("p h (n l) -> p h n l", l=C)[:, :, :, C - 1], ACT.Exp)\
                      .then_inc(*sig("exps_ready").up())
                    for m in range(4):
                        act.wait_ge(*sig("k_turned").at(m + 1))
                        nc.scalar.activation(KTOK[:, m, :], ps[:, m, :], ACT.Copy).then_inc(*sig("k_tok").up())
                    for lv in range(LEVELS):
                        act.wait_ge(*sig("level_diff").at(lv + 1))
                        nc.scalar.activation(DIFF, DIFF, ACT.Exp).then_inc(*sig("level_exp").up())
                    act.wait_ge(*sig("heads_ready").at(1))
                    nc.scalar.activation(DIFF, ps[:, 0:4, :], ACT.Square).then_inc(*sig("heads_squared").up())
                    act.wait_ge(*sig("variance").at(1))
                    nc.scalar.activation(TMP, TMP, ACT.Sqrt).then_inc(*sig("deviation").up())

                @block.vector
                def _(dve):
                    step = stepper(dve, "dve_step")
                    nc.vector.tensor_tensor(ch(KE), ch(B)[:, :, C - 1:C].broadcast_to([P, 16, C]), ch(B), ALU.subtract)\
                      .then_inc(*sig("tail_diff").up())
                    dve.wait_ge(*sig("exps_ready").at(1))
                    step(nc.vector.tensor_tensor(QE, QE, Q, ALU.mult))
                    nc.vector.tensor_tensor(KE, KE, K, ALU.mult).then_inc(*sig("tail_ready").up())
                    dve.wait_ge(*sig("state_adds").at(1))
                    step(nc.vector.tensor_copy(S[:, :, 1, :], ps[:, 4:7, :].rearrange("p n (h v) -> p h n v", h=4)[:, :, 0]))
                    for n in (1, 2):
                        for h in range(4):
                            last = nc.vector.scalar_tensor_tensor(S[:, h, n + 1, :], S[:, h, n, :], dec[:, h, n:n + 1],
                                                                  ps[:, 4 + n, h * P:h * P + P], ALU.mult, ALU.add)
                        step(last)
                    step(nc.vector.memset(ATT, 0.0))
                    att = ATT.rearrange("p h (i c) -> p (h i) c", c=P)
                    for lv in range(-1, LEVELS):
                        def diff(l):
                            b, d = halves(B, l), halves(DIFF, l)
                            hh = 64 >> l
                            ref = b[:, :, 0, hh - 1:hh].broadcast_to([P, b.shape[1], hh])
                            if l:
                                dve.wait_ge(*sig("level_ready").at(l))
                            step(nc.vector.tensor_tensor(d[:, :, 0, :], ref, b[:, :, 0, :], ALU.subtract))
                            nc.vector.tensor_tensor(d[:, :, 1, :], b[:, :, 1, :], ref, ALU.subtract)\
                              .then_inc(*sig("level_diff").up())
                        if lv < 0:
                            diff(0)
                        if lv >= 0:
                            dve.wait_ge(*sig("level_exp").at(lv + 1))
                            if lv:
                                dve.wait_ge(*sig("level_scores").at(lv + 1))
                            x, d = halves(XLV, lv), halves(DIFF, lv)
                            step(nc.vector.tensor_tensor(x[:, :, 0, :], halves(K, lv)[:, :, 0, :], d[:, :, 0, :], ALU.mult))
                            nc.vector.tensor_tensor(x[:, :, 1, :], halves(Q, lv)[:, :, 1, :], d[:, :, 1, :], ALU.mult)\
                              .then_inc(*sig("level_ready").up())
                            if lv + 1 < LEVELS:
                                diff(lv + 1)
                        dve.wait_ge(*sig("level_scores").at(lv + 2))
                        bank = 4 * ((lv + 1) % 2)
                        mask = const("ident" if lv < 0 else f"level{lv}").bitcast(I32)
                        nc.vector.copy_predicated(att, bc(mask, 16), ps[:, bank:bank + 4, :].rearrange("p h (i c) -> p (h i) c", c=P))\
                          .then_inc(*sig("level_taken").up())
                    dve.wait_ge(*sig("heads_summed").at(1))
                    nc.vector.tensor_scalar(TMP, ps[:, 4:8, :], 1.0 / P, RMS_EPS, ALU.mult, ALU.add)\
                      .then_inc(*sig("variance").up())
                    dve.wait_ge(*sig("deviation").at(1))
                    step(nc.vector.reciprocal(TMP, TMP))
                    step(nc.vector.tensor_tensor(TMP, ps[:, 0:4, :], TMP, ALU.mult))
                    for h in range(4):
                        nc.vector.tensor_scalar(Q[:, h, :], TMP[:, h, :], col("hgrn_norm_g_3", h0 + h), None, ALU.mult)

                @block.tensor
                def _(pe):
                    pe.wait_ge(*sig("tail_ready").at(1))
                    for h in range(4):
                        for i in range(TT):
                            last = nc.tensor.transpose(ps[:, h, i * P:i * P + P], KE[:, h, i * P:i * P + P], ident)
                        last.then_inc(*sig("k_turned").up())
                    for h in range(4):
                        pe.wait_ge(*sig("k_tok").at(h + 1))
                        for n in range(3):
                            last = nc.tensor.matmul(ps[:, 4 + n, h * P:h * P + P], KTOK[:, h, n * P:n * P + P],
                                                    V[:, n, (h0 + h) * P:(h0 + h) * P + P], start=True, stop=True)
                    last.then_inc(*sig("state_adds").up())
                    for lv in range(-1, LEVELS):
                        bank = 4 * ((lv + 1) % 2)
                        if lv >= 0:
                            pe.wait_ge(*sig("level_ready").at(lv + 1))
                        if lv >= 1:
                            pe.wait_ge(*sig("level_taken").at(lv))
                        for h in range(4):
                            for i in range(TT):
                                w = slice(i * P, i * P + P)
                                lhs, rhs = (K[:, h, w], Q[:, h, w]) if lv < 0 else (XLV[:, h, w], XLV[:, h, w])
                                last = nc.tensor.matmul(ps[:, bank + h, w], lhs, rhs, start=True, stop=True)
                        last.then_inc(*sig("level_scores").up())
                    pe.wait_ge(*sig("level_taken").at(LEVELS + 1))
                    for h in range(4):
                        for i in range(TT):
                            w = slice(i * P, i * P + P)
                            last = nc.tensor.matmul(ps[:, h, w], V[:, i, (h0 + h) * P:(h0 + h) * P + P], ATT[:, h, w],
                                                    start=True, stop=i == 0)
                            if i:
                                last = nc.tensor.matmul(ps[:, h, w], S[:, h, i, :], QE[:, h, w], start=False, stop=True)
                    last.then_inc(*sig("heads_ready").up())
                    pe.wait_ge(*sig("heads_squared").at(1))
                    for h in range(4):
                        last = nc.tensor.matmul(ps[:, 4 + h, :], const("ones"), DIFF[:, h, :], start=True, stop=True)
                    last.then_inc(*sig("heads_summed").up())

        def block3():
            CV, CG, CACC, CN = part_of(3, 0, 4), part_of(3, 4, 8), part_of(7, 0, 4), part_of(8, 0, 4)
            V = flat(big(6)).rearrange("p (i n) -> p i n", i=TT)
            split_phase([(X, act_hi, act_lo)])
            products([fjob("cval", ACTS, CV), fjob("cgate", ACTS, CG, ACT.Sigmoid)])
            NTAP = 31

            def convolve(dve, name, u):
                unit = {"qz": 0, "fz": 4, "iv": 8}[name] + u
                if unit == 0:
                    nc.vector.tensor_tensor(CV, CV, CG, ALU.mult).then_inc(*sig("conv_step").up())
                per = -(-4 * NTAP // 12)
                for n in range(per * unit, min(per * unit + per, 4 * NTAP)):
                    t, k = n // 4, n % 4
                    w = col("w_conv_dw_3", 4 * (NTAP - 1 - t) + k)
                    dve.wait_ge(*sig("conv_step").at(max(1, n - 2)))
                    if t == 0:
                        last = nc.vector.tensor_scalar(CACC[:, k, :], CV[:, k, :], w, col("b_conv_dw_3", k),
                                                       ALU.mult, ALU.add)
                    else:
                        last = nc.vector.scalar_tensor_tensor(CACC[:, k, t:T], CV[:, k, 0:T - t], w,
                                                              CACC[:, k, t:T], ALU.mult, ALU.add)
                    last.then_inc(*sig("conv_step").up())
            products([fjob("qz", ACTS, big(4), ACT.Silu), fjob("fz", ACTS, big(5)), tjob("iv", ACTS, V)], convolve)
            normalize(CACC, 4, True, LN_EPS, column("conv_ln_g_3", 0), column("conv_ln_b_3", 0),
                      func=ACT.Silu, dst=CN, cen=24, sq=28)
            hgrn(big(4), big(5), V, big(3))
            M2 = arena_t[:, 40:56, :]
            split_phase([(X, act_hi, act_lo)])
            products([fjob("gz", ACTS, big(7), ACT.Silu), fjob("mz", ACTS, M2, ACT.Sigmoid)])

            def gated(dve):
                nc.vector.tensor_tensor(big(4), big(4), big(7), ALU.mult).then_inc(*sig("glu_done").up())

            def gated_wait(act):
                act.wait_ge(*sig("glu_done").at(1))
            split_phase([(big(4), act_hi, act_lo), (CN, conv_hi, conv_lo)], (gated, gated_wait))
            products([merge_job("conv_out", parts(conv_hi, conv_lo), big(5)),
                      merge_job("hgrn_out", ACTS, big(6), big(5))])
            split_phase([(big(5), act_hi, act_lo)])
            products([resjob("out3", ACTS, alpha=ALPHA)])
            normalize(X, KT, True, LN_EPS, column("ln1_g_3", 0), column("ln1_b_3", 0), dst=X, split=(act_hi, act_lo))
            ffn_phase("ffn4", "convgelu", taps=conv_taps("w_ffn_dw_3", 0, 22), tap_bias=column("b_ffn_dw_3", 0),
                      alpha=ALPHA)
            normalize(X, KT, True, LN_EPS, column("ln2_g_3", 0), column("ln2_b_3", 0), dst=X)

        start()
        if 1 in blocks:
            block1()
        if 2 in blocks:
            block2()
        if 3 in blocks:
            block3()
        finish()


_INS = ["x", "c", "w_ada", "b_ada", "w_in", "w_sb_up", "ssm_a_re", "ssm_a_im", "ssm_log_dt", "ssm_b_re", "ssm_b_im",
        "ssm_c_re", "ssm_c_im", "ssm_d", "w_glu", "b_glu", "w_ssm_up", "w_out", "ln1_g", "ln1_b", "w_ffn_in",
        "w_ffn_out", "ln2_g", "ln2_b", "attn_norm_2", "attn_w_in_2", "gla_w_a2_2", "gla_b_a_2", "gla_head_g_2",
        "attn_w_o_2", "sgu_norm_2", "sgu_w_uv_2", "sgu_ln_g_2", "sgu_ln_b_2", "sgu_w_s_2", "sgu_b_s_2", "sgu_w_out_2",
        "ffn_norm_2", "ffn_w_up_2", "ffn_conv_w_2", "ffn_conv_b_2", "ffn_w_down_2", "final_norm_2", "w_in_3",
        "w_conv_dw_3", "b_conv_dw_3", "conv_ln_g_3", "conv_ln_b_3", "w_conv_out_3", "hgrn_lb_logits_3",
        "hgrn_norm_g_3", "w_hgrn_out_3", "w_out_3", "ln1_g_3", "ln1_b_3", "w_ffn_in_3", "w_ffn_dw_3", "b_ffn_dw_3",
        "w_ffn_out_3", "ln2_g_3", "ln2_b_3"]


def kernel(**inputs):
    import numpy as _np
    import concourse.bacc as _bacc
    from concourse import mybir as _mybir
    from concourse.bass_utils import run_bass_kernel_spmd as _run

    nc = _bacc.Bacc("TRN2", target_bir_lowering=False, num_devices=1)
    arrays, args = {"constants": constants()}, {}
    for name in _INS:
        arrays[name] = _np.ascontiguousarray(inputs[name])
    for name, v in arrays.items():
        args[name] = nc.dram_tensor(name, v.shape, _mybir.dt.from_np(v.dtype), kind="ExternalInput").ap()
    out = nc.dram_tensor("out", (1, T, D), F32, kind="ExternalOutput").ap()
    build_program(nc, args, out)
    r = _run(nc, [arrays], core_ids=[0])
    return r.results[0]["out"]
```

```python
import math
from contextlib import ExitStack

import numpy as np
import concourse.bass as bass
from concourse import mybir

F32 = mybir.dt.float32
F32R = mybir.dt.float32r
I32 = mybir.dt.int32
ALU = mybir.AluOpType
ACT = mybir.ActivationFunctionType
AXX = mybir.AxisListType.X

P = 128
T = 512
D = 1024
KT = D // P
TT = T // P
HID = 2816
HT = HID // P
SLOTS = 2
SLOT = 2048
BANKS = 4
LN_EPS, RMS_EPS = 1e-5, 1e-6
ALPHA = 2.0 ** 0.25
NEG = -3.0e38
TOPK = min(256, T // 4)

VECTORS = [
    ("b_ada", 48), ("ssm_a_re", 16), ("ssm_a_im", 16), ("ssm_d", 4), ("b_glu", 4), ("c", 8),
    ("ln1_g", 8), ("ln1_b", 8), ("ln2_g", 8), ("ln2_b", 8), ("attn_norm_2", 8),
    ("gla_b_a_2", 2), ("gla_head_g_2", 1), ("sgu_norm_2", 8), ("ffn_norm_2", 16),
    ("ffn_conv_w_2", 264), ("ffn_conv_b_2", 88), ("final_norm_2", 8),
    ("w_conv_dw_3", 124), ("b_conv_dw_3", 4), ("conv_ln_g_3", 4), ("conv_ln_b_3", 4),
    ("hgrn_lb_logits_3", 16), ("hgrn_norm_g_3", 8), ("ln1_g_3", 8), ("ln1_b_3", 8),
    ("w_ffn_dw_3", 66), ("b_ffn_dw_3", 22), ("ln2_g_3", 8), ("ln2_b_3", 8),
]
COLUMN, _at = {}, 0
for _name, _rows in VECTORS:
    COLUMN[_name] = _at
    _at += _rows
VROWS = _at
VTILES = -(-VROWS // P)

CONST_AT = {}


def constants():
    r, c = np.arange(P)[:, None], np.arange(P)[None, :]
    parts, at = [], 0

    def put(name, a):
        nonlocal at
        CONST_AT[name] = at
        a = np.broadcast_to(np.asarray(a, np.float32), (P, a.shape[-1]))
        parts.append(a)
        at += a.shape[1]

    put("ident", (r == c).astype(np.float32))
    put("ones", np.ones((P, P)))
    put("later", (r > c).astype(np.float32))
    put("before", (r < c).astype(np.float32))
    put("upto", (r <= c).astype(np.float32))
    put("chunk64", ((r <= c) & (r // 64 == c // 64)).astype(np.float32))
    put("notyet", np.where(c <= r, 0.0, NEG))
    perm = np.zeros((P, P))
    for h in range(2):
        for i in range(8):
            perm[64 * h + 8 + i, 64 * h + i] = -1.0
            perm[64 * h + i, 64 * h + 8 + i] = 1.0
    put("turn", perm)
    for lv in range(7):
        h = 64 >> lv
        put(f"level{lv}", ((r // (2 * h) == c // (2 * h)) & (r % (2 * h) < h) & (c % (2 * h) >= h)).astype(np.float32))
    put("group0", ((r // 16) % 2 == 0).astype(np.float32))
    put("group1", ((r // 16) % 2 == 1).astype(np.float32))
    inv = np.power(np.float32(500000.0), -(np.arange(8, dtype=np.float32) * 2.0 / 16)).astype(np.float32)
    ang = (np.arange(T, dtype=np.float32)[None, :] * inv[:, None]).astype(np.float32)
    cos, sin = np.ones((P, T)), np.zeros((P, T))
    for h in range(2):
        for k in range(2):
            cos[64 * h + 8 * k:64 * h + 8 * k + 8] = np.cos(ang)
            sin[64 * h + 8 * k:64 * h + 8 * k + 8] = np.sin(ang)
    CONST_AT["tables"] = at
    put("cos", cos)
    put("sin", sin)
    put("keep64", (np.arange(T)[None, :] % 64 != 0).astype(np.float32))
    put("keep128", (np.arange(T)[None, :] % 128 != 0).astype(np.float32))
    return np.ascontiguousarray(np.concatenate(parts, axis=1), np.float32)


class Signal:

    def __init__(self, handle):
        self.handle, self.base, self.total = handle, 0, 0

    def up(self):
        self.total += 1
        return self.handle, 1

    def at(self, k):
        return self.handle, self.base + k


class Gemm:

    def __init__(self, name, n, panels, tiles, kt, evac, ppt=1):
        self.name, self.n, self.panels, self.tiles, self.kt = name, n, panels, tiles, kt
        self.evac, self.ppt = evac, ppt
        self.ppu = len(panels)


def build_program(nc, a, out, debug=None, blocks=(1, 2, 3)):
    ctx = ExitStack()
    with ctx:
        def sbuf(name, shape, dt=F32):
            return ctx.enter_context(nc.sbuf_tensor(name, shape, dt))

        signals = {}

        def sig(name):
            if name not in signals:
                signals[name] = Signal(ctx.enter_context(nc.semaphore(name)))
            return signals[name]

        base_at = [nc.sbuf_base + (-nc.sbuf_base) % 64]

        def place(name, shape, dt=F32, at=None):
            size = -(-4 * int(np.prod(shape[1:])) // 64) * 64
            if at is None:
                at = base_at[0]
                base_at[0] += size
            return nc.alloc_sbuf_tensor_at(name, shape, dt, offset=at)

        TILE = T * 4
        arena_at = base_at[0]
        arena_t = place("arena", [P, 68, T])
        act_hi = place("act_hi", [P, KT, T], F32R, arena_at + 8 * TILE)
        act_lo = place("act_lo", [P, KT, T], F32R, arena_at + 16 * TILE)
        hid_hi = place("hid_hi", [P, HT, T], F32R, arena_at + 24 * TILE)
        hid_lo = place("hid_lo", [P, HT, T], F32R, arena_at + 46 * TILE)
        conv_hi = place("conv_hi", [P, 4, T], F32R, arena_at + 24 * TILE)
        conv_lo = place("conv_lo", [P, 4, T], F32R, arena_at + 28 * TILE)
        weights = place("weights", [P, SLOTS, SLOT])
        w_hi = place("w_hi", [P, SLOTS, SLOT], F32R)
        w_lo = place("w_lo", [P, SLOTS, SLOT], F32R)
        constants()
        ncst = CONST_AT["tables"]
        cst = place("cst", [P, ncst])
        cols = place("cols", [P, VTILES * P])
        rows = place("rows", [P, 5, T])
        mod = place("mod", [P, 48])
        small = place("small", [P, 512])
        ps = ctx.enter_context(nc.psum_tensor("ps", [P, 8, 512], F32))

        def big(i):
            return arena_t[:, 8 * i:8 * i + 8, :]

        def part_of(i, lo, hi):
            return arena_t[:, 8 * i + lo:8 * i + hi, :]

        def const(name, n=P):
            return cst[:, CONST_AT[name]:CONST_AT[name] + n]

        def col(name, i=0):
            at = COLUMN[name] + i
            return cols[:, at:at + 1] if isinstance(i, int) else cols[:, bass.ds(at, 1)]

        X = big(0)

        def big_words(i, at, n):
            return arena_t[:, :, :].rearrange("p k t -> p (k t)")[:, 4096 * i + at:4096 * i + at + n]

        def parts(hi, lo, first=0):
            return lambda k: (hi[:, first + k, :], lo[:, first + k, :])
        ACTS = parts(act_hi, act_lo)
        ident = const("ident")

        def kview(w):
            return w.rearrange("(k p) n -> p k n", p=P)

        def slot_view(s, kt, n, of=None):
            return (weights if of is None else of)[:, s, 0:kt * n].rearrange("p (k n) -> p k n", k=kt)

        def cols_panel(w, kt, c0, width):
            def dmas(u, s):
                return [(slot_view(s, kt, width), kview(w)[:, :, bass.ds(c0 + u * width, width)])]
            return dmas

        def pair_panel(w):
            v = kview(w).rearrange("p k (h n) -> p k h n", h=2)
            return lambda u, s: [(slot_view(s, KT, 256)[:, :, h * P:h * P + P], v[:, :, h, bass.ds(u * P, P)])
                                 for h in range(2)]

        def half_panel(w, half):
            v = w.rearrange("(h k p) n -> p h k n", p=P, h=2)[:, half]
            return lambda u, s: [(slot_view(s, HT // 2, P), v[:, :, bass.ds(u * P, P)])]

        plan, order = {}, []

        def gemm(name, *args, **kw):
            plan[name] = Gemm(name, *args, **kw)
            order.append(plan[name])

        def feat(name, w, kt, n, evac, c0=0):
            width = 256 if kt == 8 else 512
            tiles = [("w", i * P, P, 0) for i in range(width // P)]
            gemm(name, n, [cols_panel(w, kt, c0, width)], tiles, kt, evac)

        def tok(name, w, kt, n, evac, c0=0):
            gemm(name, n, [cols_panel(w, kt, c0, 256)], [("x", 0, 256, i) for i in range(TT)], kt, evac)

        def ffn(tag, w_in, w_out, evac):
            gemm(tag + "_in", HT, [pair_panel(w_in)], [("w", 0, P, 0), ("w", P, P, 0)], KT, evac)
            gemm(tag + "_out", KT, [half_panel(w_out, 0), half_panel(w_out, 1)], [("w", 0, P, 0)], HT, "dve")

        if 1 in blocks:
            w = a["w_in"][0]
            feat("qk", w, KT, 4, "act")
            tok("v", w, KT, 2, "act", c0=1024)
            feat("u", w, KT, 2, "act", c0=1536)
            feat("gates", w, KT, 8, "act", c0=2048)
            feat("sb_up", a["w_sb_up"][0], 4, 2, "dve")
            feat("glu", a["w_glu"][0], 4, 1, "act")
            feat("ssm_up", a["w_ssm_up"][0], 4, 2, "dve")
            feat("out1", a["w_out"][0], KT, 4, "dve")
            ffn("ffn1", a["w_ffn_in"][0], a["w_ffn_out"][0], "swiglu")
        if 2 in blocks:
            w = a["attn_w_in_2"][0]
            feat("bq", w, KT, 2, "act", c0=1552)
            feat("iq", w, KT, 1, "act", c0=2192)
            wk = kview(w)
            gemm("shared", 1, [lambda u, s: [
                (slot_view(s, KT, 256)[:, :, 64 * i:64 * i + 64], wk[:, :, c0:c0 + 64])
                for i, c0 in enumerate((2064, 2064, 2448, 2448))]],
                [("w", 0, P, 0), ("w", P, P, 0)], KT, "act")
            gemm("narrow", 1, [lambda u, s: [
                (slot_view(s, KT, 256)[:, :, o:o + n], wk[:, :, c0:c0 + n])
                for o, n, c0 in ((0, 16, 1536), (16, 64, 2128), (80, 4, 2512))]],
                [("w", 0, P, 0)] + [("x", 16, 68, i) for i in range(TT)], KT, "act")
            feat("aqk", w, KT, 2, "act")
            tok("av", w, KT, 2, "act", c0=512)
            feat("ar", w, KT, 2, "act", c0=1024)
            feat("w_o", a["attn_w_o_2"][0], KT, 4, "dve")
            ffn("ffn2", a["ffn_w_up_2"][0], a["ffn_w_down_2"][0], "conv")
            feat("sgu_u", a["sgu_w_uv_2"][0], KT, 4, "act")
            tok("sgu_v", a["sgu_w_uv_2"][0], KT, 4, "act", c0=1024)
            feat("sgu_out", a["sgu_w_out_2"][0], KT, 4, "dve")
            ffn("ffn3", a["ffn_w_up_2"][1], a["ffn_w_down_2"][1], "conv")
        if 3 in blocks:
            w = a["w_in_3"][0]
            feat("cval", w, KT, 2, "act")
            feat("cgate", w, KT, 2, "act", c0=512)
            feat("qz", w, KT, 4, "act", c0=1024)
            feat("fz", w, KT, 4, "act", c0=2048)
            tok("iv", w, KT, 4, "act", c0=3072)
            feat("gz", w, KT, 4, "act", c0=4096)
            feat("mz", w, KT, 8, "act", c0=5120)
            feat("conv_out", a["w_conv_out_3"][0], 4, 2, "dve")
            feat("hgrn_out", a["w_hgrn_out_3"][0], KT, 4, "dve")
            feat("out3", a["w_out_3"][0], KT, 4, "dve")
            ffn("ffn4", a["w_ffn_in_3"][0], a["w_ffn_out_3"][0], "convgelu")

        RATES = {"act": {"tile_act": "t"}, "dve": {"tile_dve": "t"},
                 "swiglu": {"tile_act": 1, "tile_dve": 1, "hid_hi": 1, "hidden_done": 1},
                 "conv": {"tap_act": 2, "tap_step": 2, "tile_dve": 2, "gate_act": 1, "hidden_mul": 1, "hid_hi": 1,
                          "hidden_done": 1},
                 "convgelu": {"tap_act": 1, "tap_step": 1, "tile_dve": 2, "gate_act": 1, "hid_hi": 1,
                              "hidden_done": 1}}
        running = dict.fromkeys(["marks", "bank", "tile_act", "tile_dve", "tap_act", "tap_step", "gate_act",
                                 "hidden_mul", "hid_hi"], 0)
        running["hidden_done"] = 2
        panel_list, slot_count = [], [0] * SLOTS
        for g in order:
            g.base, g.first_panel, g.dmas = dict(running), len(panel_list), len(g.panels[0](0, 0))
            g.marks = len(g.tiles) * g.ppu
            for u in range(g.n):
                for j, dmas in enumerate(g.panels):
                    s = len(panel_list) % SLOTS
                    slot_count[s] += 16 * len(dmas(0, s))
                    panel_list.append(dict(g=g, u=u, j=j, slot=s, filled=slot_count[s]))
            running["marks"] += g.n * g.marks
            running["bank"] += g.n * len(g.tiles)
            for k, v in RATES[g.evac].items():
                running[k] += g.n * (len(g.tiles) if v == "t" else v)
            g.end = dict(running)
        marks = sig("marks")
        panel_in = [sig(f"panel_in{s}") for s in range(SLOTS)]
        hi_ready, lo_ready = sig("hi_ready"), sig("lo_ready")
        fed = [0]

        def one_panel(sp, p, p_value, u):
            info = panel_list[p]
            if p >= SLOTS:
                sp.wait_ge(lo_ready.handle, p_value - (SLOTS - 1))
            for dst, src in info["g"].panels[info["j"]](u, info["slot"]):
                sp.dma_start(dst, src).then_inc(panel_in[info["slot"]].handle, 16)

        def feed(sp, last):
            g = plan[last] if last else None
            end = min((g.first_panel + g.n * g.ppu if g else 0) + SLOTS, len(panel_list))
            while fed[0] < end:
                p = fed[0]
                g, ppu = panel_list[p]["g"], panel_list[p]["g"].ppu
                per = SLOTS // ppu
                stop = min(end, g.first_panel + g.n * ppu)
                turns = (stop - p) // SLOTS
                if p >= SLOTS and (p - g.first_panel) % ppu == 0 and turns >= 3:
                    u0 = panel_list[p]["u"]
                    with sp.Fori(0, turns) as i:
                        for j in range(SLOTS):
                            one_panel(sp, p + j, i * SLOTS + (p + j), i * per + (u0 + j // ppu))
                    fed[0] += turns * SLOTS
                else:
                    one_panel(sp, p, p, panel_list[p]["u"])
                    fed[0] += 1

        def units(eng, g, emit, loop=True):
            turns = (g.n - (g is order[-1])) // 4 if loop else 0
            done = 0
            if turns >= 2:
                with eng.Fori(0, turns) as i:
                    for j in range(4):
                        emit(i * 4 + j, j)
                done = turns * 4
            for u in range(done, g.n):
                emit(u, u)

        def units_from(eng, g, emit):
            turns = (g.n - (g is order[-1])) // 4
            looped = turns >= 3
            for u in range(1, 4 if looped else g.n):
                emit(u, u)
            if looped:
                with eng.Fori(1, turns) as i:
                    for j in range(4):
                        emit(i * 4 + j, j)
                for u in range(turns * 4, g.n):
                    emit(u, u)

        def split_hi(act, g, u, j):
            for jj in range(g.ppu):
                p = g.first_panel + j * g.ppu + jj + 1
                if p >= len(panel_list):
                    continue
                s = p % SLOTS
                act.wait_ge(panel_in[s].handle, (u - j) * (g.dmas * g.ppu * 16 // SLOTS) + panel_list[p]["filled"])
                read = u * g.marks + (g.base["marks"] + jj)
                if not isinstance(read, int) or read > 0:
                    act.wait_ge(marks.handle, read)
                nc.scalar.activation(w_hi[:, s, :], weights[:, s, :], ACT.Copy).then_inc(hi_ready.handle, 1)

        def split_lo(dve, g, u, j):
            for jj in range(g.ppu):
                p = g.first_panel + j * g.ppu + jj + 1
                if p >= len(panel_list):
                    continue
                s = p % SLOTS
                dve.wait_ge(hi_ready.handle, (u - j) * g.ppu + (p + 1))
                nc.vector.tensor_tensor(w_lo[:, s, :], weights[:, s, :], w_hi[:, s, :].bitcast(F32), ALU.subtract)\
                  .then_inc(lo_ready.handle, 1)

        def bank_of(g, j, t):
            return (g.base["bank"] + j * len(g.tiles) + t) % BANKS

        def width_of(g):
            return P if g.kt == HT else 256 if g.kt == KT else 512

        def mm_gemm(pe, name, x, ready=None, beside=None):
            g = plan[name]
            nt = len(g.tiles)
            for k in ("tile_act", "tile_dve"):
                if g.base[k]:
                    pe.wait_ge(sig(k).handle, g.base[k])
            pairs = {"swiglu": [("tile_act", 0, 1), ("tile_dve", 0, 1)],
                     "conv": [("tile_dve", 0, 2), ("tile_dve", 1, 2)],
                     "convgelu": [("tile_dve", 0, 2), ("tile_dve", 1, 2)]}

            def operands(tile, wh, wl, xh, xl, k, bank):
                kind, c0, width, tt = tile
                c, r = slice(c0, c0 + width), slice(tt * P, tt * P + P)
                if kind == "w":
                    return ps[:, bank, :], ((wh[:, k, c], xh), (wh[:, k, c], xl), (wl[:, k, c], xh))
                return ps[:, bank, 0:width], ((xh[:, r], wh[:, k, c]), (xh[:, r], wl[:, k, c]), (xl[:, r], wh[:, k, c]))

            def emit(u, j):
                kt = g.kt // g.ppu
                if ready is not None and j == 0 and isinstance(u, int):
                    s = g.first_panel % SLOTS
                    pe.wait_ge(lo_ready.handle, g.first_panel + 1)
                    wh, wl = (slot_view(s, kt, width_of(g), of) for of in (w_hi, w_lo))
                    for k in range(kt):
                        pe.wait_ge(*sig(ready).at(k + 1))
                        xh, xl = x(k)
                        for t, tile in enumerate(g.tiles):
                            o, ops = operands(tile, wh, wl, xh, xl, k, bank_of(g, j, t))
                            for n, (lhs, rhs) in enumerate(ops):
                                last = nc.tensor.matmul(o, lhs, rhs, start=k == 0 and n == 0,
                                                        stop=k == kt - 1 and n == 2)
                            if k == kt - 1:
                                last.then_inc(marks.handle, 1)
                    if beside is not None:
                        for t in range(nt):
                            beside(t)
                    return
                for t, tile in enumerate(g.tiles):
                    bank = bank_of(g, j, t)
                    if j * nt + t >= BANKS or not isinstance(u, int):
                        back = j * nt + t - BANKS
                        bu, bt = back // nt, back % nt
                        k, idx, rate = pairs[g.evac][bt] if g.evac in pairs else ("tile_" + g.evac, bt, nt)
                        assert isinstance(u, int) or g.base[k] >= BANKS
                        pe.wait_ge(sig(k).handle, (u + (bu - j)) * rate + (g.base[k] + idx + 1))
                    kk = 0
                    for i in range(g.ppu):
                        p = g.first_panel + j * g.ppu + i
                        s = p % SLOTS
                        if t == 0:
                            pe.wait_ge(lo_ready.handle, (u - j) * g.ppu + (p + 1))
                        wh, wl = (slot_view(s, kt, width_of(g), of) for of in (w_hi, w_lo))
                        for k in range(kt):
                            xh, xl = x(kk)
                            o, ops = operands(tile, wh, wl, xh, xl, k, bank)
                            for n, (lhs, rhs) in enumerate(ops):
                                last = nc.tensor.matmul(o, lhs, rhs, start=kk == 0 and n == 0,
                                                        stop=kk == g.kt - 1 and n == 2)
                            kk += 1
                        if i < g.ppu - 1:
                            last.then_inc(marks.handle, 1)
                    last.then_inc(marks.handle, 1)
                    if beside is not None:
                        beside(u * nt + t)

            if ready is not None:
                emit(0, 0)
                units_from(pe, g, emit)
            else:
                units(pe, g, emit, loop=beside is None)

        def take(eng, name, signal, tiles, fn, split, extra=None, begun=False, beside=None):
            g = plan[name]

            def emit(u, j):
                if not (begun and isinstance(u, int) and u == 0):
                    split(eng, g, u, j)
                if extra is not None and isinstance(u, int):
                    extra(name, u)
                for t in range(len(g.tiles)):
                    if t in tiles:
                        eng.wait_ge(marks.handle, u * g.marks + (g.base["marks"] + (t + 1) * g.ppu))
                        fn(u, t, bank_of(g, j, t)).then_inc(sig(signal).handle, 1)
                    if beside is not None:
                        beside(u * len(g.tiles) + t)
            if begun:
                emit(0, 0)
                units_from(eng, g, emit)
            else:
                units(eng, g, emit, loop=beside is None)

        def at_tile(view, i):
            if isinstance(i, int):
                return view[:, i, :]
            return view[:, bass.ds(i, 1), :].rearrange("p a t -> p (a t)")

        def phase(last=None):
            for s in signals.values():
                s.base = s.total
            block = nc.Block()
            return block

        def stepper(eng, name):
            s = sig(name)

            def step(ins):
                ins.then_inc(*s.up())
                eng.wait_ge(s.handle, s.total)
                return ins
            return step

        def bc(row, n):
            return row.rearrange("p (a t) -> p a t", a=1).broadcast_to([row.shape[0], n, row.shape[1]])

        def bl(c, n):
            return c.rearrange("p (a b) -> p a b", b=1).broadcast_to([c.shape[0], c.shape[1], n])

        def small_row(i):
            return rows[:, i, :]

        class Norm:

            def __init__(self, src, kt, center, eps, gain, bias=None, func=ACT.Identity, dst=None, split=None,
                         cen=24, sq=32, stats=False):
                self.src, self.kt, self.center, self.eps, self.n = src, kt, center, eps, kt * P
                self.gain, self.bias, self.func, self.dst, self.split, self.stats = gain, bias, func, dst, split, stats
                self.CEN, self.SQ = arena_t[:, cen:cen + kt, :], arena_t[:, sq:sq + kt, :]
                self.part, self.squares, self.mean, self.var, self.shift = (rows[:, i, :] for i in range(5))

            def tensor(self, pe):
                if self.stats:
                    if self.center:
                        nc.tensor.matmul(ps[:, 4, :], const("ones"), self.part, start=True, stop=True)
                    nc.tensor.matmul(ps[:, 5, :], const("ones"), self.squares, start=True, stop=True)\
                      .then_inc(*sig("squares_summed").up())
                    return
                if self.center:
                    pe.wait_ge(*sig("part_sum").at(1))
                    nc.tensor.matmul(ps[:, 4, :], const("ones"), self.part, start=True, stop=True)\
                      .then_inc(*sig("summed").up())
                for k in range(self.kt):
                    pe.wait_ge(*sig("squared").at(k + 1))
                    last = nc.tensor.matmul(ps[:, 5, :], const("ones"), self.SQ[:, k, :], start=k == 0,
                                            stop=k == self.kt - 1)
                last.then_inc(*sig("squares_summed").up())

            def vector_stats(self, dve, beside=None):
                step = stepper(dve, "norm_step")
                n, mean, var = self.n, self.mean, self.var

                def centre():
                    for k in range(self.kt):
                        nc.vector.tensor_tensor(self.CEN[:, k, :], self.src[:, k, :], mean, ALU.subtract)\
                          .then_inc(*sig("centered").up())
                if self.stats and self.center:
                    dve.wait_ge(*sig("squares_summed").at(1))
                    step(nc.vector.scalar_tensor_tensor(mean, ps[:, 4, :], 1.0 / n, self.shift, ALU.mult, ALU.subtract))
                    step(nc.vector.tensor_tensor(var, mean, mean, ALU.mult))
                    step(nc.vector.scalar_tensor_tensor(var, ps[:, 5, :], 1.0 / n, var, ALU.mult, ALU.subtract))
                    nc.vector.tensor_scalar(var, var, 0.0, self.eps, ALU.max, ALU.add).then_inc(*sig("variance").up())
                    step(nc.vector.tensor_tensor(mean, mean, self.shift, ALU.add))
                    centre()
                else:
                    if self.center:
                        nc.vector.tensor_reduce(self.part, self.src.rearrange("p k t -> p t k"), AXX, ALU.add)\
                          .then_inc(*sig("part_sum").up())
                        dve.wait_ge(*sig("summed").at(1))
                        step(nc.vector.tensor_scalar(mean, ps[:, 4, :], 1.0 / n, None, ALU.mult))
                        centre()
                    dve.wait_ge(*sig("squares_summed").at(1))
                    nc.vector.tensor_scalar(var, ps[:, 5, :], 1.0 / n, self.eps, ALU.mult, ALU.add)\
                      .then_inc(*sig("variance").up())
                if beside:
                    beside()
                dve.wait_ge(*sig("deviation").at(1))
                step(nc.vector.reciprocal(var, var))

            def direct(self):
                return self.split and self.dst is None and self.func == ACT.Identity

            def vector_tiles(self, dve):
                Y = self.dst if self.dst is not None else self.CEN
                cur = self.CEN if self.center else self.src

                def lower(k):
                    dve.wait_ge(*sig("upper_ready").at(k + 1))
                    hi, lo = self.split[0][:, k, :].bitcast(F32), self.split[1][:, k, :]
                    if self.direct() and self.bias:
                        last = nc.vector.scalar_tensor_tensor(lo, self.CEN[:, k, :], self.bias(k), hi, ALU.add, ALU.subtract)
                    else:
                        last = nc.vector.tensor_tensor(lo, Y[:, k, :], hi, ALU.subtract)
                    last.then_inc(*sig("lower_ready").up())
                for k in range(self.kt):
                    if self.direct():
                        last = nc.vector.scalar_tensor_tensor(self.CEN[:, k, :], cur[:, k, :], self.gain(k), self.var,
                                                              ALU.mult, ALU.mult)
                    else:
                        last = nc.vector.tensor_tensor(self.CEN[:, k, :], cur[:, k, :], self.var, ALU.mult)
                    last.then_inc(*sig("normed").up())
                    if self.split and k >= 2:
                        lower(k - 2)
                if self.split:
                    lower(self.kt - 2)
                    lower(self.kt - 1)

            def scalar_stats(self, act, beside=None):
                if not self.stats:
                    cur = self.CEN if self.center else self.src
                    for k in range(self.kt):
                        if self.center:
                            act.wait_ge(*sig("centered").at(k + 1))
                        nc.scalar.activation(self.SQ[:, k, :], cur[:, k, :], ACT.Square).then_inc(*sig("squared").up())
                if beside:
                    beside()
                act.wait_ge(*sig("variance").at(1))
                nc.scalar.activation(self.var, self.var, ACT.Sqrt).then_inc(*sig("deviation").up())

            def scalar_tiles(self, act):
                Y = self.dst if self.dst is not None else self.CEN
                if self.direct():
                    for k in range(self.kt):
                        act.wait_ge(*sig("normed").at(k + 1))
                        if self.bias:
                            last = nc.scalar.activation(self.split[0][:, k, :], self.CEN[:, k, :], ACT.Identity,
                                                        bias=self.bias(k))
                        else:
                            last = nc.scalar.activation(self.split[0][:, k, :], self.CEN[:, k, :], ACT.Copy)
                        last.then_inc(*sig("upper_ready").up())
                    return

                def upper(k):
                    act.wait_ge(*sig("affine_ready").at(k + 1))
                    nc.scalar.activation(self.split[0][:, k, :], Y[:, k, :], ACT.Copy).then_inc(*sig("upper_ready").up())
                for k in range(self.kt):
                    act.wait_ge(*sig("normed").at(k + 1))
                    nc.scalar.activation(Y[:, k, :], self.CEN[:, k, :], self.func, scale=self.gain(k),
                                         bias=self.bias(k) if self.bias else 0.0).then_inc(*sig("affine_ready").up())
                    if self.split and k:
                        upper(k - 1)
                if self.split:
                    upper(self.kt - 1)

        def normalize(*args, **kw):
            norm = Norm(*args, **kw)
            with phase() as block:
                @block.vector
                def _(dve):
                    norm.vector_stats(dve)
                    norm.vector_tiles(dve)

                @block.tensor
                def _(pe):
                    norm.tensor(pe)

                @block.scalar
                def _(act):
                    norm.scalar_stats(act)
                    norm.scalar_tiles(act)

        class Stats:

            def __init__(self, name, center, scratch):
                self.g, self.center, self.tiles = plan[name], center, KT
                self.DEV = [arena_t[:, scratch + i, :] for i in range(2)]
                self.SQ = [arena_t[:, scratch + 2 + i, :] for i in range(2)]
                self.part, self.squares, self.shift = rows[:, 0, :], rows[:, 1, :], rows[:, 4, :]

            def tensor(self, pe, m):
                if self.center and m == 1:
                    pe.wait_ge(sig("tile_dve").handle, self.g.base["tile_dve"] + 1)
                    nc.tensor.matmul(ps[:, 4, :], const("ones"), X[:, 0, :], start=True, stop=True)\
                      .then_inc(*sig("shift_summed").up())

            def vector(self, dve, m):
                for k in [m - 1] + [m] * (m == self.tiles - 1):
                    if k < 0 or not self.center:
                        continue
                    dve.wait_ge(sig("tile_dve").handle, self.g.base["tile_dve"] + k + 1)
                    if k == 0:
                        dve.wait_ge(*sig("shift_summed").at(1))
                        nc.vector.tensor_scalar(self.shift, ps[:, 4, :], 1.0 / P, None, ALU.mult)\
                          .then_inc(*sig("shift_ready").up())
                        dve.wait_ge(*sig("shift_ready").at(1))
                    else:
                        if k > 1:
                            dve.wait_ge(*sig("part_step").at(k - 1))
                        nc.vector.tensor_tensor(self.part, X[:, 0, :] if k == 1 else self.part, X[:, k, :], ALU.add)\
                          .then_inc(*sig("part_step").up())
                    if k >= 2:
                        dve.wait_ge(*sig("tile_squared").at(k - 1))
                    nc.vector.tensor_tensor(self.DEV[k % 2], X[:, k, :], self.shift, ALU.subtract)\
                      .then_inc(*sig("deviated").up())

            def scalar(self, act, m):
                for k in [m - 1] + [m] * (m == self.tiles - 1):
                    if k < 0:
                        continue
                    if self.center:
                        act.wait_ge(*sig("deviated").at(k + 1))
                    else:
                        act.wait_ge(sig("tile_dve").handle, self.g.base["tile_dve"] + k + 1)
                    if k >= 3:
                        act.wait_ge(*sig("square_added").at(k - 2))
                    nc.scalar.activation(self.SQ[k % 2] if k else self.squares,
                                         self.DEV[k % 2] if self.center else X[:, k, :], ACT.Square)\
                      .then_inc(*sig("tile_squared").up())

            def gpsimd(self, pool):
                pool.wait_ge(*sig("tile_squared").at(1))
                for k in range(1, self.tiles):
                    pool.wait_ge(*sig("tile_squared").at(k + 1))
                    if k > 1:
                        pool.wait_ge(*sig("square_added").at(k - 1))
                    nc.gpsimd.tensor_tensor(self.squares, self.squares, self.SQ[k % 2], ALU.add)\
                      .then_inc(*sig("square_added").up())

        class Split:

            def __init__(self, tiles, last=None):
                self.tiles, self.last = tiles, last

            def tensor(self, pe):
                pass

            def scalar_stats(self, act, beside=None):
                self.scalar_beside = beside

            def scalar_tiles(self, act):
                made = 0
                for src, hi, _, make, func in self.tiles:
                    if make:
                        made += 1
                        act.wait_ge(*sig("source_made").at(made))
                    if func:
                        nc.scalar.activation(src, src, func).then_inc(*sig("source_func").up())
                        act.wait_ge(sig("source_func").handle, sig("source_func").total)
                    nc.scalar.activation(hi, src, ACT.Copy).then_inc(*sig("upper_ready").up())
                self.scalar_beside()

            def vector_stats(self, dve, beside=None):
                self.vector_beside = beside

            def vector_tiles(self, dve):
                def source(k):
                    if k < len(self.tiles) and self.tiles[k][3]:
                        self.tiles[k][3]().then_inc(*sig("source_made").up())
                source(0)
                source(1)
                for k, (src, hi, lo, _, _) in enumerate(self.tiles):
                    source(k + 2)
                    dve.wait_ge(*sig("upper_ready").at(k + 1))
                    nc.vector.tensor_tensor(lo, src, hi.bitcast(F32), ALU.subtract).then_inc(*sig("lower_ready").up())
                self.vector_beside()
                if self.last:
                    self.last(dve)

        def split_tiles(src, hi, lo, make=None, func=None):
            return [(src[:, k, :], hi[:, k, :], lo[:, k, :], make and (lambda k=k: make(k)), func)
                    for k in range(src.shape[1])]

        def start():
            xtok = big(2).rearrange("p k t -> p (k t)").rearrange("p (a n) -> p a n", a=TT)
            stage = big(3).rearrange("p k t -> p (k t)")[:, 0:VTILES * P].rearrange("p (a n) -> p a n", a=VTILES)
            with phase() as block:
                pieces = []
                for name, rows_ in VECTORS:
                    src = a[name]
                    flat = src.rearrange(" ".join("abcd"[:len(src.shape)]) + " -> (" + " ".join("abcd"[:len(src.shape)]) + ")")
                    v = flat.rearrange("(r p) -> r p", p=P)
                    at, left, r0 = COLUMN[name], rows_, 0
                    while left:
                        m = min(left, P - at % P)
                        pieces.append((at // P, at % P, m, v[r0:r0 + m, :]))
                        at, left, r0 = at + m, left - m, r0 + m

                @block.gpsimd
                def _(pool):
                    nc.gpsimd.memset(stage, 0.0).then_inc(*sig("stage_zero").up())

                @block.sync
                def _(sp):
                    sp.dma_start(cst[:, :], a["constants"][:, 0:ncst]).then_inc(sig("loaded").handle, 16)
                    sp.dma_start(xtok, a["x"][0].rearrange("(a p) n -> p a n", p=P)).then_inc(sig("loaded").handle, 16)
                    feed(sp, None)
                    if 1 in blocks:
                        sp.wait_ge(sig("vectors").handle, 16 * len(pieces))
                        for k in range(KT):
                            sp.dma_start(big_words(4, 2048 * k, 2048), a["w_ada"][0, k * P:k * P + P, 0:2048])\
                              .then_inc(sig(f"ada_in{k}").handle, 16)

                @block.scalar
                def _(act):
                    act.wait_ge(*sig("stage_zero").at(1))
                    for tile, p0, m, src in pieces:
                        act.dma_start(stage[p0:p0 + m, tile, :], src).then_inc(sig("vectors").handle, 16)
                    act.wait_ge(panel_in[0].handle, panel_list[0]["filled"])
                    nc.scalar.activation(w_hi[:, 0, :], weights[:, 0, :], ACT.Copy).then_inc(hi_ready.handle, 1)

                @block.tensor
                def _(pe):
                    pe.wait_ge(sig("loaded").handle, 32)
                    for k in range(KT):
                        for i in range(TT):
                            last = nc.tensor.transpose(ps[:, k % 4, i * P:(i + 1) * P], xtok[:, i, k * P:(k + 1) * P], ident)
                        last.then_inc(*sig("turned").up())
                        if k >= 3:
                            pe.wait_ge(sig("turned_out").handle, k - 2)
                    pe.wait_ge(sig("vectors").handle, 16 * len(pieces))
                    for i in range(VTILES):
                        last = nc.tensor.transpose(ps[:, 4 + i // 4, (i % 4) * P:(i % 4 + 1) * P], stage[:, i, :], ident)
                    last.then_inc(*sig("turned").up())

                @block.vector
                def _(dve):
                    for k in range(KT):
                        dve.wait_ge(*sig("turned").at(k + 1))
                        nc.vector.tensor_copy(X[:, k, :], ps[:, k % 4, :]).then_inc(*sig("turned_out").up())
                    dve.wait_ge(*sig("turned").at(KT + 1))
                    nc.vector.tensor_copy(cols[:, :], ps[:, 4:6, :].rearrange("p a n -> p (a n)")[:, 0:VTILES * P])
                    for i in range(2):
                        nc.vector.memset(small[:, i:i + 1], 0.0).then_inc(sig("hidden_done").handle, 1)
                    dve.wait_ge(hi_ready.handle, 1)
                    nc.vector.tensor_tensor(w_lo[:, 0, :], weights[:, 0, :], w_hi[:, 0, :].bitcast(F32), ALU.subtract)\
                      .then_inc(lo_ready.handle, 1)

        def finish():
            otok = big(2).rearrange("p k t -> p (k t)").rearrange("p (a n) -> p a n", a=TT)
            with phase() as block:
                @block.tensor
                def _(pe):
                    for n in range(8):
                        i, half = n // 2, n % 2
                        if n >= 4:
                            pe.wait_ge(*sig("turned_out").at(n - 3))
                        for k in range(4):
                            last = nc.tensor.transpose(ps[:, n % 4, k * P:(k + 1) * P],
                                                       X[:, half * 4 + k, i * P:(i + 1) * P], ident)
                        last.then_inc(*sig("turned").up())

                @block.vector
                def _(dve):
                    for n in range(8):
                        dve.wait_ge(*sig("turned").at(n + 1))
                        nc.vector.tensor_copy(otok[:, n // 2, (n % 2) * 512:(n % 2) * 512 + 512], ps[:, n % 4, :])\
                          .then_inc(*sig("turned_out").up())

                @block.sync
                def _(sp):
                    for i in range(TT):
                        sp.wait_ge(*sig("turned_out").at(2 * i + 2))
                        sp.dma_start(out[0, i * P:(i + 1) * P, :], otok[:, i, :]).then_inc(sig("stored").handle, 16)
                    sp.wait_ge(sig("stored").handle, 16 * TT)

        def products(jobs, extra=None, after=None, norm=None, center=None):
            first = plan[jobs[0][0]]
            stats = Stats(jobs[-1][0], center, 24) if center is not None else None

            def beside(name, what, eng):
                if stats is None or name != jobs[-1][0]:
                    return None
                return lambda m: what(eng, m)
            with phase() as block:
                @block.sync
                def _(sp):
                    feed(sp, jobs[-1][0])

                @block.tensor
                def _(pe):
                    if norm:
                        norm.tensor(pe)
                    for n, (name, x, _, _) in enumerate(jobs):
                        if norm and n == 1:
                            pe.wait_ge(sig("lower_ready").handle, sig("lower_ready").total)
                        mm_gemm(pe, name, x, "lower_ready" if norm and n == 0 else None,
                                beside(name, stats and stats.tensor, pe))
                        if after:
                            after("tensor", pe, name)

                @block.scalar
                def _(act):
                    if norm:
                        norm.scalar_stats(act, lambda: split_hi(act, first, 0, 0))
                        norm.scalar_tiles(act)
                    for n, (name, _, who, fn) in enumerate(jobs):
                        take(act, name, "tile_act", range(len(plan[name].tiles)) if who == "act" else [], fn, split_hi,
                             begun=bool(norm) and n == 0, beside=beside(name, stats and stats.scalar, act))

                @block.vector
                def _(dve):
                    if norm:
                        norm.vector_stats(dve, lambda: split_lo(dve, first, 0, 0))
                        norm.vector_tiles(dve)
                    for n, (name, _, who, fn) in enumerate(jobs):
                        take(dve, name, "tile_dve", range(len(plan[name].tiles)) if who == "dve" else [], fn, split_lo,
                             extra and (lambda nm, u: extra(dve, nm, u)), begun=bool(norm) and n == 0,
                             beside=beside(name, stats and stats.vector, dve))
                    if after:
                        after("vector", dve, None)

                @block.gpsimd
                def _(pool):
                    if after:
                        after("gpsimd", pool, None)
                    if stats:
                        stats.gpsimd(pool)

        def to(view, func=ACT.Identity, first=0, bias=None, scale=1.0):
            def fn(u, t, bank, nt=None):
                m = u * fn.nt + (first + t)
                b = bias(m) if bias else 0.0
                return nc.scalar.activation(at_tile(view, m), ps[:, bank, :], func, bias=b, scale=scale)
            return fn

        def nt_of(name, fn):
            fn.nt = len(plan[name].tiles)
            return fn

        def fjob(name, x, view, func=ACT.Identity, bias=None):
            return name, x, "act", nt_of(name, to(view, func, bias=bias))

        def tjob(name, x, view, func=ACT.Identity):
            def fn(u, t, bank):
                return nc.scalar.activation(view[:, t, bass.ds(u * 256, 256)] if not isinstance(u, int)
                                            else view[:, t, u * 256:u * 256 + 256], ps[:, bank, 0:256], func)
            return name, x, "act", fn

        def resjob(name, x, gain=None, alpha=1.0):
            nt = len(plan[name].tiles)

            def fn(u, t, bank):
                m = u * nt + t
                xt = at_tile(X, m)
                if gain is None:
                    return nc.vector.scalar_tensor_tensor(xt, xt, alpha, ps[:, bank, :], ALU.mult, ALU.add)
                return nc.vector.scalar_tensor_tensor(xt, ps[:, bank, :], gain(m), xt, ALU.mult, ALU.add)
            return name, x, "dve", fn

        def scale_residual(dve):
            for k in range(KT):
                nc.vector.tensor_scalar(X[:, k, :], X[:, k, :], ALPHA, None, ALU.mult).then_inc(*sig("scaled").up())
            dve.wait_ge(*sig("scaled").at(KT))

        def ffn_phase(tag, kind, norm, taps=None, tap_bias=None, gain=None, alpha=1.0, center=True):
            g, go = plan[tag + "_in"], plan[tag + "_out"]
            b = g.base
            rj = resjob(tag + "_out", None, gain, alpha)
            mul = "hidden_mul" if kind == "conv" else "tile_dve"
            mul_rate = {"conv": 1, "swiglu": 1, "convgelu": 2}[kind]

            stats = Stats(tag + "_out", center, 8)

            def run(eng, emit):
                emit(0, 0)
                units_from(eng, g, emit)

            def buf(j, t):
                return rows[:, 2 * (j % 2) + t, :]
            with phase() as block:
                @block.sync
                def _(sp):
                    feed(sp, tag + "_out")

                @block.tensor
                def _(pe):
                    norm.tensor(pe)
                    mm_gemm(pe, tag + "_in", ACTS, "lower_ready")
                    pe.wait_ge(sig("hidden_done").handle, g.end["hidden_done"])
                    mm_gemm(pe, tag + "_out", parts(hid_hi, hid_lo), beside=lambda m: stats.tensor(pe, m))

                @block.scalar
                def _(act):
                    norm.scalar_stats(act, lambda: split_hi(act, g, 0, 0))
                    norm.scalar_tiles(act)

                    def emit(u, j):
                        if not isinstance(u, int) or u:
                            split_hi(act, g, u, j)
                        gate, up = bank_of(g, j, 0), bank_of(g, j, 1)
                        act.wait_ge(sig("hidden_done").handle, u + (b["hidden_done"] - 1))
                        res = buf(j, 1 if kind != "convgelu" else 0)
                        if kind == "swiglu":
                            act.wait_ge(marks.handle, u * 2 + (b["marks"] + 1))
                            nc.scalar.activation(buf(j, 0), ps[:, gate, :], ACT.Silu).then_inc(sig("tile_act").handle, 1)
                        else:
                            nt = 2 if kind == "conv" else 1
                            for t in range(nt):
                                act.wait_ge(marks.handle, u * 2 + (b["marks"] + t + 1))
                                m = u + HT * t
                                nc.scalar.activation(buf(j, t), ps[:, bank_of(g, j, t), :], ACT.Identity,
                                                     scale=taps(2, m), bias=tap_bias(m)).then_inc(sig("tap_act").handle, 1)
                            act.wait_ge(sig("tile_dve").handle, u * 2 + (b["tile_dve"] + 1))
                            nc.scalar.activation(buf(j, 0), buf(j, 0), ACT.Silu if kind == "conv" else GELU)\
                              .then_inc(sig("gate_act").handle, 1)
                        act.wait_ge(sig(mul).handle, u * mul_rate + (b[mul] + mul_rate))
                        nc.scalar.activation(at_tile(hid_hi, u), res, ACT.Copy).then_inc(sig("hid_hi").handle, 1)
                    run(act, emit)
                    take(act, tag + "_out", None, [], None, split_hi, beside=lambda m: stats.scalar(act, m))

                @block.vector
                def _(dve):
                    norm.vector_stats(dve, lambda: split_lo(dve, g, 0, 0))
                    norm.vector_tiles(dve)
                    if gain is not None:
                        scale_residual(dve)

                    def emit(u, j):
                        if not isinstance(u, int) or u:
                            split_lo(dve, g, u, j)
                        gate, up = bank_of(g, j, 0), bank_of(g, j, 1)
                        res = buf(j, 1 if kind != "convgelu" else 0)
                        if kind == "swiglu":
                            dve.wait_ge(sig("tile_act").handle, u + (b["tile_act"] + 1))
                            dve.wait_ge(marks.handle, u * 2 + (b["marks"] + 2))
                            nc.vector.tensor_tensor(res, buf(j, 0), ps[:, up, :], ALU.mult).then_inc(sig(mul).handle, 1)
                        else:
                            nt = 2 if kind == "conv" else 1
                            for t in range(nt):
                                m = u + HT * t
                                c = buf(j, t)
                                bank = bank_of(g, j, t)
                                dve.wait_ge(sig("tap_act").handle, u * nt + (b["tap_act"] + t + 1))
                                nc.vector.scalar_tensor_tensor(c[:, 1:T], ps[:, bank, 0:T - 1], taps(1, m), c[:, 1:T],
                                                               ALU.mult, ALU.add).then_inc(sig("tap_step").handle, 1)
                                dve.wait_ge(sig("tap_step").handle, u * nt + (b["tap_step"] + t + 1))
                                nc.vector.scalar_tensor_tensor(c[:, 2:T], ps[:, bank, 0:T - 2], taps(0, m), c[:, 2:T],
                                                               ALU.mult, ALU.add).then_inc(sig("tile_dve").handle, 1)
                            dve.wait_ge(sig("gate_act").handle, u + (b["gate_act"] + 1))
                            if kind == "conv":
                                dve.wait_ge(sig("tile_dve").handle, u * 2 + (b["tile_dve"] + 2))
                                other = buf(j, 1)
                            else:
                                dve.wait_ge(marks.handle, u * 2 + (b["marks"] + 2))
                                other = ps[:, up, :]
                            nc.vector.tensor_tensor(res, buf(j, 0), other, ALU.mult).then_inc(sig(mul).handle, 1)
                        dve.wait_ge(sig("hid_hi").handle, u + (b["hid_hi"] + 1))
                        nc.vector.tensor_tensor(at_tile(hid_lo, u), res, at_tile(hid_hi, u).bitcast(F32), ALU.subtract)\
                          .then_inc(sig("hidden_done").handle, 1)
                    run(dve, emit)
                    take(dve, tag + "_out", "tile_dve", [0], rj[3], split_lo, beside=lambda m: stats.vector(dve, m))

                @block.gpsimd
                def _(pool):
                    stats.gpsimd(pool)

        GELU = ACT.Gelu_apprx_tanh
        def flat(view):
            return view.rearrange("p k t -> p (k t)")

        def merge_job(name, x, gate, total=None):
            nt = len(plan[name].tiles)

            def fn(u, t, bank):
                m = u * nt + t
                first = nc.vector.tensor_tensor(gate[:, m, :], gate[:, m, :], ps[:, bank, :], ALU.mult)
                if total is None:
                    return first
                first.then_inc(*sig("merge_step").up())
                nc.vector.wait_ge(sig("merge_step").handle, sig("merge_step").total)
                return nc.vector.tensor_tensor(total[:, m, :], total[:, m, :], gate[:, m, :], ALU.add)
            return name, x, "dve", fn

        PACK = [0, 512, 1024, 896]
        WIDE = [T - P * j for j in range(TT)]
        CAUSAL = sum(WIDE)

        class FirstNorm(Norm):

            def tensor(self, pe):
                Norm.tensor(self, pe)
                pe.wait_ge(*sig("ada_summed").at(1))
                ada_columns(pe, ADA[0], 0)

            def scalar_stats(self, act, beside=None):
                nc.scalar.activation(small[:, 0:8], cols[:, COLUMN["c"]:COLUMN["c"] + KT], ACT.Silu)\
                  .then_inc(*sig("c_ready").up())
                Norm.scalar_stats(self, act, beside)

            def vector_stats(self, dve, beside=None):
                Norm.vector_stats(self, dve, beside)
                dve.wait_ge(*sig("c_ready").at(1))
                step = stepper(dve, "mod_step")
                for k in range(KT):
                    dve.wait_ge(sig(f"ada_in{k}").handle, 16)
                    last = ada_add(ADA[0], big_words(4, 2048 * k, 2048), k)
                    if k < KT - 1:
                        step(last)
                last.then_inc(*sig("ada_summed").up())
                dve.wait_ge(*sig("ada_columns").at(1))
                mod_bias(step, 0, 2)

        ADA = [big_words(8, 0, 2048), rows[:, 0:4, :].rearrange("p k t -> p (k t)")]

        def ada_add(acc, w, k):
            c = small[:, k:k + 1]
            if k == 0:
                return nc.vector.tensor_scalar(acc, w, c, None, ALU.mult)
            return nc.vector.scalar_tensor_tensor(acc, w, c, acc, ALU.mult, ALU.add)

        def ada_columns(pe, acc, part):
            for m in range(16):
                last = nc.tensor.matmul(ps[:, 7, 16 * part + m:16 * part + m + 1], acc[:, m * P:m * P + P],
                                        const("ones")[:, 0:1], start=True, stop=True)
            last.then_inc(*sig("ada_columns").up())

        def mod_bias(step, lo, hi):
            c = slice(lo * KT, hi * KT)
            b = COLUMN["b_ada"]
            step(nc.vector.tensor_tensor(mod[:, c], ps[:, 7, c], cols[:, b + lo * KT:b + hi * KT], ALU.add))
            for part in (1, 2, 4, 5):
                if lo <= part < hi:
                    v = mod[:, part * KT:part * KT + KT]
                    step(nc.vector.tensor_scalar(v, v, 1.0, None, ALU.add))

        def ada_rest_add(dve, name, u):
            first = {"qk": 0, "v": 4, "u": 6}.get(name)
            if first is None:
                return
            for n in (2 * (first + u), 2 * (first + u) + 1):
                half, k = n // KT, n % KT
                dve.wait_ge(sig(f"ada_slot{n % 2}").handle, 16 * (n // 2 + 1))
                if k:
                    dve.wait_ge(*sig("ada_step").at(n))
                ada_add(ADA[half], big_words(3, 2048 * (n % 2), 2048), k).then_inc(*sig("ada_step").up())

        def ada_rest(engine, eng, name):
            if engine == "gpsimd":
                eng.wait_ge(*sig("lower_ready").at(KT))
                for n in range(16):
                    half, k = n // KT, n % KT
                    if n >= 2:
                        eng.wait_ge(*sig("ada_step").at(n - 1))
                    eng.dma_start(big_words(3, 2048 * (n % 2), 2048),
                                  a["w_ada"][0, k * P:k * P + P, 2048 * (half + 1):2048 * (half + 2)])\
                       .then_inc(sig(f"ada_slot{n % 2}").handle, 16)
            elif engine == "tensor" and name in ("v", "gates"):
                half = int(name == "gates")
                eng.wait_ge(*sig("ada_step").at(8 * (half + 1)))
                ada_columns(eng, ADA[half], half + 1)
            elif engine == "vector":
                eng.wait_ge(*sig("ada_columns").at(3))
                mod_bias(stepper(eng, "mod_step"), 2, 6)

        def mod_col(part):
            def at(k):
                i = part * KT + k
                return mod[:, i:i + 1] if isinstance(i, int) else mod[:, bass.ds(i, 1)]
            return at

        def stick_breaking(QK, V, out_view):
            scale = 64 ** -0.5
            f7, f8 = flat(big(1)), flat(big(2))
            LB = [f7[:, 0:CAUSAL], f7[:, CAUSAL:2 * CAUSAL]]
            OM = [f7[:, 2 * CAUSAL:3 * CAUSAL], f8[:, 0:CAUSAL], flat(big(3))[:, CAUSAL:2 * CAUSAL]]
            EX = [f8[:, CAUSAL:2 * CAUSAL], f8[:, 2 * CAUSAL:3 * CAUSAL], flat(big(3))[:, 0:CAUSAL]]
            Z = ps[:, 0:3, :].rearrange("p b n -> p (b n)")
            AFTER = ps[:, 3:6, :].rearrange("p b n -> p (b n)")
            with phase() as block:
                @block.tensor
                def _(pe):
                    def scores(h):
                        r = 64 * (h % 2)
                        if h:
                            pe.wait_ge(*sig("scores_taken").at(h))
                        for j in range(TT):
                            last = nc.tensor.matmul(Z[:, PACK[j]:PACK[j] + WIDE[j]],
                                                    QK[r:r + 64, 4 + h // 2, j * P:(j + 1) * P],
                                                    QK[r:r + 64, h // 2, j * P:T], start=True, stop=True)
                        last.then_inc(*sig("scores_ready").up())
                    def after(h):
                        pe.wait_ge(*sig("stick_ready").at(h + 1))
                        if h:
                            pe.wait_ge(*sig("log_weight").at(h))
                        om = OM[h % 3]
                        for i in range(TT):
                            for j in range(i, TT):
                                last = nc.tensor.matmul(
                                    AFTER[:, PACK[i] + P * (j - i):PACK[i] + WIDE[i]],
                                    const("later" if i == j else "ones"),
                                    om[:, PACK[j]:PACK[j] + WIDE[j]], start=j == i, stop=j == TT - 1)
                        last.then_inc(*sig("after_ready").up())

                    def values(h):
                        r = 64 * (h % 2)
                        pe.wait_ge(*sig("weight_masked").at(h + 1))
                        if h >= 2:
                            pe.wait_ge(*sig("head_out").at(h - 1))
                        for j in range(TT):
                            last = nc.tensor.matmul(ps[r:r + 64, 6 + h % 2, j * P:T], V[:, j, 64 * h:64 * h + 64],
                                                    EX[h % 3][:, PACK[j]:PACK[j] + WIDE[j]],
                                                    start=j == 0, stop=j == TT - 1)
                        last.then_inc(*sig("values_ready").up())
                    scores(0)
                    scores(1)
                    for h in range(8):
                        if h + 2 < 8:
                            scores(h + 2)
                        after(h)
                        if h:
                            values(h - 1)
                    values(7)

                @block.scalar
                def _(act):
                    step = stepper(act, "act_step")

                    def soft(h):
                        ex = EX[h % 3]
                        act.wait_ge(*sig("scores_taken").at(h + 1))
                        if h >= 3:
                            act.wait_ge(*sig("values_ready").at(h - 2))
                        step(nc.scalar.activation(ex, OM[h % 3], ACT.Abs))
                        step(nc.scalar.activation(ex, ex, ACT.Exp, scale=-1.0))
                        nc.scalar.activation(ex, ex, ACT.Ln, bias=1.0).then_inc(*sig("soft_ready").up())
                    soft(0)
                    for h in range(8):
                        if h + 1 < 8:
                            soft(h + 1)
                        act.wait_ge(*sig("log_weight").at(h + 1))
                        nc.scalar.activation(EX[h % 3], LB[h % 2], ACT.Exp).then_inc(*sig("weight_ready").up())

                @block.vector
                def _(dve):
                    step = stepper(dve, "dve_step")

                    def scaled(h):
                        dve.wait_ge(*sig("scores_ready").at(h + 1))
                        if h >= 3:
                            dve.wait_ge(*sig("after_ready").at(h - 2))
                        nc.vector.tensor_scalar(OM[h % 3], Z[:, 0:CAUSAL], scale, None, ALU.mult)\
                          .then_inc(*sig("scores_taken").up())

                    def diagonal(view, signal):
                        for j in range(TT):
                            d = view[:, PACK[j]:PACK[j] + P]
                            last = nc.vector.tensor_tensor(d, d, const("before"), ALU.mult)
                        last.then_inc(*sig(signal).up())

                    def weights_masked(h):
                        dve.wait_ge(*sig("weight_ready").at(h + 1))
                        diagonal(EX[h % 3], "weight_masked")

                    def head_out(h):
                        r = 64 * (h % 2)
                        dve.wait_ge(*sig("values_ready").at(h + 1))
                        nc.vector.tensor_copy(out_view[r:r + 64, h // 2, :], ps[r:r + 64, 6 + h % 2, :])\
                          .then_inc(*sig("head_out").up())
                    scaled(0)
                    scaled(1)
                    for h in range(8):
                        lb, om = LB[h % 2], OM[h % 3]
                        dve.wait_ge(*sig("soft_ready").at(h + 1))
                        step(nc.vector.scalar_tensor_tensor(lb, om, 0.0, EX[h % 3], ALU.min, ALU.subtract))
                        step(nc.vector.tensor_tensor(om, lb, om, ALU.subtract))
                        diagonal(om, "stick_ready")
                        if h + 2 < 8:
                            scaled(h + 2)
                        if h:
                            weights_masked(h - 1)
                        if h >= 2:
                            head_out(h - 2)
                        dve.wait_ge(*sig("after_ready").at(h + 1))
                        nc.vector.tensor_tensor(lb, lb, AFTER[:, 0:CAUSAL], ALU.add).then_inc(*sig("log_weight").up())
                    weights_masked(7)
                    head_out(6)
                    head_out(7)

        def block1():
            c1 = lambda n: (lambda k: col(n, k))
            QK, V, U = big(4), part_of(5, 0, 4), part_of(5, 4, 8)
            G2 = arena_t[:, 48:64, :]
            YSB, YS = part_of(8, 0, 4), part_of(4, 4, 8)
            products([fjob("qk", ACTS, QK), tjob("v", ACTS, V), fjob("u", ACTS, U),
                      fjob("gates", ACTS, G2, ACT.Sigmoid)], ada_rest_add, ada_rest,
                     FirstNorm(X, KT, True, LN_EPS, mod_col(1), mod_col(0), split=(act_hi, act_lo), cen=24, sq=8))
            stick_breaking(QK, V, YSB)
            s5(U, YS)
            YG, GL = part_of(3, 4, 8), part_of(3, 0, 4)

            def skip(k):
                return nc.vector.scalar_tensor_tensor(YG[:, k, :], U[:, k, :], col("ssm_d", k), YS[:, k, :],
                                                      ALU.mult, ALU.add)
            products([merge_job("sb_up", ACTS, big(6)),
                      fjob("glu", parts(act_hi, act_lo, 4), GL, ACT.Sigmoid, bias=c1("b_glu"))],
                     norm=Split(split_tiles(YSB, act_hi[:, 0:4], act_lo[:, 0:4])
                                + split_tiles(YG, act_hi[:, 4:8], act_lo[:, 4:8], skip, GELU)))

            def gated(k):
                return nc.vector.tensor_tensor(YG[:, k, :], YG[:, k, :], GL[:, k, :], ALU.mult)
            products([merge_job("ssm_up", ACTS, big(7), big(6))],
                     norm=Split(split_tiles(YG, act_hi[:, 0:4], act_lo[:, 0:4], gated)))
            products([resjob("out1", ACTS, mod_col(2))], center=True,
                     norm=Split(split_tiles(big(6), act_hi, act_lo), scale_residual))
            normalize(X, KT, True, LN_EPS, c1("ln1_g"), c1("ln1_b"), dst=X, stats=True)
            ffn_phase("ffn1", "swiglu", Norm(X, KT, True, LN_EPS, mod_col(4), mod_col(3), split=(act_hi, act_lo)),
                      gain=mod_col(5))
            normalize(X, KT, True, LN_EPS, c1("ln2_g"), c1("ln2_b"), dst=X, stats=True)

        def s5(U, YS):
            L, NCH, NP = 8, T // 8, 16

            def words(i, at, n):
                return big_words(i, at, n)

            def v16(i):
                return small[:, 16 + 16 * i:32 + 16 * i]
            (dt, lr, li, kq, red, mag, sn, sh, Lr, Li, den, xr, fr, fi, t0, t1, s2) = (v16(i) for i in range(17))
            cs, wr, wi, decay8, l2r, l2i, l4r, l4i = (v16(i) for i in range(17, 25))
            nat = words(3, 0, 1024)
            Bnat = nat[:, 0:512].rearrange("p (r j c) -> p r j c", r=2, j=NP)
            Cnat = nat[:, 512:1024].rearrange("p (r m s) -> p r m s", r=2, m=4)
            rowsf = rows[:, 0:4, :].rearrange("p a n -> p (a n)")
            Cpad = rowsf[:, 0:1024].rearrange("p (r m g s) -> p r m g s", r=2, m=4, g=2)
            tA = rowsf[:, 1024:1536].rearrange("p (j c) -> p j c", j=NP)
            tB = rowsf[:, 1536:2048].rearrange("p (j c) -> p j c", j=NP)
            R = words(1, 0, 8192).rearrange("p (r j d c) -> p r j d c", r=2, j=NP, d=L)
            BB = words(3, 4608, 1024).rearrange("p (r j c) -> p r j c", r=2, j=NP)
            RT = words(3, 0, 8192).rearrange("p (r h j s) -> p r h j s", r=2, h=2, j=NP)
            US = words(5, 0, 2048).rearrange("p (h j n) -> p h j n", h=2, j=NP)
            KB = words(5, 0, 2048).rearrange("p (b d c) -> p b d c", b=2, d=L)
            HS = words(1, 0, 2048).rearrange("p (r j n) -> p r j n", r=2, j=NP)
            Gn = words(1, 2048, 4608).rearrange("p (d j c) -> p d j c", d=9, j=NP)
            Gr = words(3, 0, 4608).rearrange("p (d j c) -> p d j c", d=9, j=NP)
            DECAY = words(1, 6656, 1024).rearrange("p (j n) -> p j n", j=NP)
            poolA, poolB = (w.rearrange("p (j c) -> p j c", j=NP) for w in (words(3, 5632, 512), words(1, 7680, 512)))
            TEMP = [words(3, 6144 + 1024 * i, 1024).rearrange("p (j n) -> p j n", j=NP) for i in range(2)]
            lateA, lateB = (words(3, 6144 + 512 * i, 512).rearrange("p (j c) -> p j c", j=NP) for i in range(2))
            TURN32 = rowsf[:, 1024:2048].rearrange("p (r j n) -> p r j n", r=2, j=NP)
            TURN = words(5, 0, 2048).rearrange("p (r j n) -> p r j n", r=2, j=NP)
            m0, m1 = (rows[:, 4, 256 * i:256 * i + 256] for i in range(2))
            ldt = rowsf[0:16, 0:2]
            ldtw = rowsf[0:16, 128:256]
            ab = (COLUMN["ssm_a_re"], COLUMN["ssm_a_im"])
            ar, ai = cols[:, ab[0]:ab[0] + 16], cols[:, ab[1]:ab[1] + 16]
            PI2 = 2 * math.pi
            C1 = 6.28125
            C2 = float(np.float32(PI2 - C1) - np.float32(PI2 - C1) % np.float32(2.0 ** -21))
            C3 = float(np.float32(PI2 - C1 - C2))
            MAGIC = 1.5 * 2.0 ** 23
            UV = U.rearrange("p m (n l) -> p m n l", l=L)
            with phase() as block:
                @block.sync
                def _(sp):
                    sp.dma_start(ldt, a["ssm_log_dt"][0].rearrange("(j g) -> j g", g=2)).then_inc(sig("ssm_loaded").handle, 16)
                    for r, (b, c) in enumerate((("ssm_b_re", "ssm_c_re"), ("ssm_b_im", "ssm_c_im"))):
                        sp.dma_start(Bnat[:, r], a[b][0].rearrange("(j g) s c -> (g s) j c", g=2))\
                          .then_inc(sig("ssm_loaded").handle, 16)
                        sp.dma_start(Cnat[:, r], a[c][0].rearrange("g c s -> (g c) s")
                                     .rearrange("(m q) s -> q m s", q=P)).then_inc(sig("ssm_loaded").handle, 16)

                @block.vector
                def _(dve):
                    step = stepper(dve, "dve_step")
                    dve.wait_ge(sig("ssm_loaded").handle, 80)
                    step(nc.vector.tensor_copy(ldtw.rearrange("p (g s) -> p g s", g=2),
                                               ldt.rearrange("p (g s) -> p g s", s=1).broadcast_to([16, 2, 64])))
                    nc.vector.tensor_copy(ldtw, ldtw).then_inc(*sig("dt_rows").up())
                    dve.wait_ge(*sig("dt_ready").at(1))
                    TS, TTT, STT = nc.vector.tensor_scalar, nc.vector.tensor_tensor, nc.vector.scalar_tensor_tensor
                    TTT(lr, ar, dt, ALU.mult)
                    step(TTT(li, ai, dt, ALU.mult))
                    step(TS(kq, li, 1.0 / PI2, MAGIC, ALU.mult, ALU.add))
                    step(TS(kq, kq, MAGIC, None, ALU.subtract))
                    for c in (C1, C2, C3):
                        step(STT(red if c != C1 else red, kq, -c, li if c == C1 else red, ALU.mult, ALU.add))
                    TS(red, red, 3.1415925, -3.1415925, ALU.min, ALU.max).then_inc(*sig("angle_ready").up())
                    dve.wait_ge(*sig("polar_ready").at(1))
                    step(TTT(t0, sh, sh, ALU.mult))
                    step(TS(cs, t0, -2.0, 1.0, ALU.mult, ALU.add))
                    step(TTT(Lr, mag, cs, ALU.mult))
                    step(TTT(Li, mag, sn, ALU.mult))
                    step(TTT(t0, ar, ar, ALU.mult))
                    step(TTT(t1, ai, ai, ALU.mult))
                    step(TTT(den, t0, t1, ALU.add))
                    step(nc.vector.reciprocal(den, den))
                    step(TS(xr, Lr, 1.0, None, ALU.subtract))
                    step(TTT(t0, xr, ar, ALU.mult))
                    step(TTT(t1, Li, ai, ALU.mult))
                    step(TTT(t0, t0, t1, ALU.add))
                    step(TTT(fr, t0, den, ALU.mult))
                    step(TTT(t0, Li, ar, ALU.mult))
                    step(TTT(t1, xr, ai, ALU.mult))
                    step(TTT(t0, t0, t1, ALU.subtract))
                    step(TTT(fi, t0, den, ALU.mult))
                    for r in range(2):
                        for g in range(2):
                            step(TS(Cpad[:, r, :, g, :], Cnat[:, r], const(f"group{g}", 1), None, ALU.mult))
                    nc.vector.tensor_copy(s2, fr).then_inc(*sig("c_padded").up())
                    step(nc.vector.memset(R[:, :, :, 0, :], 0.0))
                    for g in range(2):
                        q = slice(64 * g, 64 * g + 64)
                        c = slice(16 * g, 16 * g + 16)
                        br, bi = Bnat[q, 0], Bnat[q, 1]
                        FR, FI = bl(fr[q], 16), bl(fi[q], 16)
                        step(TTT(tA[q, :, 0:16], br, FR, ALU.mult))
                        step(TTT(tB[q, :, 0:16], bi, FI, ALU.mult))
                        step(TTT(R[q, 0, :, 0, c], tA[q, :, 0:16], tB[q, :, 0:16], ALU.subtract))
                        step(TTT(tA[q, :, 0:16], br, FI, ALU.mult))
                        step(TTT(tB[q, :, 0:16], bi, FR, ALU.mult))
                        step(TTT(R[q, 1, :, 0, c], tA[q, :, 0:16], tB[q, :, 0:16], ALU.add))
                    LR, LI = bl(Lr, 32), bl(Li, 32)
                    for d in range(1, L):
                        pr, pi = R[:, 0, :, d - 1, :], R[:, 1, :, d - 1, :]
                        step(TTT(tA, pr, LR, ALU.mult))
                        step(TTT(tB, pi, LI, ALU.mult))
                        step(TTT(R[:, 0, :, d, :], tA, tB, ALU.subtract))
                        step(TTT(tA, pr, LI, ALU.mult))
                        step(TTT(tB, pi, LR, ALU.mult))
                        step(TTT(R[:, 1, :, d, :], tA, tB, ALU.add))
                    nc.vector.tensor_copy(s2, fr).then_inc(*sig("powers_ready").up())

                    def square(dr, di, sr, si):
                        step(TTT(t0, sr, sr, ALU.mult))
                        step(TTT(t1, si, si, ALU.mult))
                        step(TTT(s2, sr, si, ALU.mult))
                        step(TTT(dr, t0, t1, ALU.subtract))
                        step(TS(di, s2, 2.0, None, ALU.mult))

                    def turned(dst, src, a, b):
                        n = src.shape[-1]
                        WR, WI = bl(wr, n), bl(wi, n)
                        step(TTT(a, src[:, 0], WR, ALU.mult))
                        step(TTT(b, src[:, 1], WI, ALU.mult))
                        step(TTT(dst[:, 0], a, b, ALU.subtract))
                        step(TTT(a, src[:, 0], WI, ALU.mult))
                        step(TTT(b, src[:, 1], WR, ALU.mult))
                        step(TTT(dst[:, 1], a, b, ALU.add))
                    square(l2r, l2i, Lr, Li)
                    square(l4r, l4i, l2r, l2i)
                    square(wr, wi, cs, sn)
                    for _ in range(2):
                        square(wr, wi, wr, wi)
                    step(nc.vector.memset(TURN32[:, 0, :, 0:1], 1.0))
                    step(nc.vector.memset(TURN32[:, 1, :, 0:1], 0.0))
                    n = 1
                    while n < 32:
                        turned(TURN32[:, :, :, n:2 * n], TURN32[:, :, :, 0:n],
                               *(m[:, 0:16 * n].rearrange("p (j n) -> p j n", j=NP) for m in (m0, m1)))
                        square(wr, wi, wr, wi)
                        n *= 2
                    dve.wait_ge(*sig("chunks_in").at(1))
                    nc.vector.tensor_copy(BB, R[:, :, :, 0, :]).then_inc(*sig("input_kept").up())
                    dve.wait_ge(*sig("input_kept").at(1))
                    step(nc.vector.tensor_copy(DECAY, bl(decay8, 64)))
                    step(nc.vector.memset(DECAY[:, :, 0:1], 0.0))
                    step(nc.vector.memset(HS[:, :, :, 0:1], 0.0))
                    turned(TURN[:, :, :, 32:64], TURN32, TEMP[0][:, :, 0:32], TEMP[1][:, :, 0:32])
                    dve.wait_ge(*sig("table_copied").at(1))
                    ur, ui = (ps[:, 4 + 2 * r:6 + 2 * r, :].rearrange("p b (j n) -> p (b j) n", n=64)[:, :, 0:63]
                              for r in range(2))
                    c1, s1 = TURN[:, 0, :, 1:64], TURN[:, 1, :, 1:64]
                    hr, hi = HS[:, 0, :, 1:64], HS[:, 1, :, 1:64]
                    a, b = TEMP[0][:, :, 1:64], TEMP[1][:, :, 1:64]
                    TTT(a, s1, ui, ALU.mult)
                    TTT(b, s1, ur, ALU.mult)
                    TTT(hr, c1, ur, ALU.mult)
                    step(TTT(hi, c1, ui, ALU.mult))
                    TTT(hr, hr, a, ALU.add)
                    step(TTT(hi, hi, b, ALU.subtract))
                    for r in range(2):
                        flat_state = HS[:, r].rearrange("p j n -> p (j n)")
                        last = nc.vector.tensor_tensor_scan(TEMP[r].rearrange("p j n -> p (j n)"),
                                                            DECAY.rearrange("p j n -> p (j n)"), flat_state, 0.0,
                                                            ALU.mult, ALU.add)
                    step(last)
                    gr, gi = TEMP
                    step(TTT(DECAY, TURN[:, 1], gi, ALU.mult))
                    step(TTT(HS[:, 0], TURN[:, 0], gr, ALU.mult))
                    step(TTT(HS[:, 0], HS[:, 0], DECAY, ALU.subtract))
                    step(TTT(DECAY, TURN[:, 1], gr, ALU.mult))
                    step(TTT(HS[:, 1], TURN[:, 0], gi, ALU.mult))
                    step(TTT(HS[:, 1], HS[:, 1], DECAY, ALU.add))
                    nc.vector.memset(KB, 0.0).then_inc(*sig("scanned").up())
                    dve.wait_ge(*sig("g_first").at(1))
                    for d in range(4, L + 1):
                        base, (pr, pi) = (0, (l4r, l4i)) if d == 4 else (d - 1, (Lr, Li))
                        PR, PI = bl(pr, 32), bl(pi, 32)
                        step(TTT(lateA, Gr[:, base], PR, ALU.mult))
                        step(TTT(lateB, Gn[:, base], PI, ALU.mult))
                        step(TTT(Gr[:, d], lateA, lateB, ALU.add))
                        step(TTT(lateA, Gn[:, base], PR, ALU.mult))
                        step(TTT(lateB, Gr[:, base], PI, ALU.mult))
                        step(TTT(Gn[:, d], lateA, lateB, ALU.subtract))
                    nc.vector.tensor_copy(s2, fr).then_inc(*sig("g_late").up())
                    for m in range(4):
                        dve.wait_ge(*sig("kernel_ready").at(m + 1))
                        if m >= 2:
                            dve.wait_ge(*sig("inside_done").at(m - 1))
                        for q in range(4):
                            w = slice(32 * q, 32 * q + 32)
                            last = nc.vector.tensor_copy(KB[w, m % 2, :, w],
                                                         ps[w, m % 2, 0:256].rearrange("p (d c) -> p d c", d=L))
                        last.then_inc(*sig("kernel_out").up())

                @block.scalar
                def _(act):
                    act.wait_ge(*sig("dt_turned").at(1))
                    nc.scalar.activation(dt, ps[:, 0, 0:16], ACT.Exp).then_inc(*sig("dt_ready").up())
                    act.wait_ge(*sig("angle_ready").at(1))
                    nc.scalar.activation(mag, lr, ACT.Exp)
                    nc.scalar.activation(decay8, lr, ACT.Exp, scale=float(L))
                    nc.scalar.activation(sn, red, ACT.Sin)
                    nc.scalar.activation(sh, red, ACT.Sin, scale=0.5).then_inc(*sig("polar_ready").up())
                    for d in range(L):
                        for q in range(4):
                            last = nc.scalar.activation(
                                US[32 * (d % 4):32 * (d % 4) + 32, d // 4].rearrange("p (m r) n -> p r m n", r=4)[:, q],
                                UV[32 * q:32 * q + 32, :, :, L - 1 - d], ACT.Copy)
                    last.then_inc(*sig("steps_stacked").up())
                    for n in range(16):
                        r, h, j = n // 8, n // 4 % 2, 4 * (n % 4)
                        act.wait_ge(*sig("power_turned").at(n + 1))
                        nc.scalar.activation(RT[:, r, h, j:j + 4, :].rearrange("p j s -> p (j s)"), ps[:, n % 4, :],
                                             ACT.Copy).then_inc(*sig("power_out").up())
                    act.wait_ge(*sig("input_kept").at(1))
                    nc.scalar.activation(TURN[:, :, :, 0:32], TURN32, ACT.Copy).then_inc(*sig("table_copied").up())
                    act.wait_ge(*sig("c_turned").at(1))
                    nc.scalar.activation(Gr[:, 0].rearrange("p j c -> p (j c)"), ps[:, 0, :], ACT.Copy)
                    nc.scalar.activation(Gn[:, 0].rearrange("p j c -> p (j c)"), ps[:, 1, :], ACT.Copy, scale=-1.0)\
                      .then_inc(*sig("g_first").up())
                    for m in range(4):
                        act.wait_ge(*sig("y_ready").at(m + 1))
                        nc.scalar.activation(YS[:, m, :], ps[:, 4 + m, :], ACT.Copy)

                @block.gpsimd
                def _(pool):
                    step = stepper(pool, "pool_step")
                    pool.wait_ge(*sig("g_first").at(1))
                    pool.wait_ge(*sig("powers_ready").at(1))
                    LR, LI = bl(Lr, 32), bl(Li, 32)
                    TTT = nc.gpsimd.tensor_tensor
                    for d in range(1, 4):
                        step(TTT(poolA, Gr[:, d - 1], LR, ALU.mult))
                        step(TTT(poolB, Gn[:, d - 1], LI, ALU.mult))
                        step(TTT(Gr[:, d], poolA, poolB, ALU.add))
                        step(TTT(poolA, Gn[:, d - 1], LR, ALU.mult))
                        step(TTT(poolB, Gr[:, d - 1], LI, ALU.mult))
                        last = TTT(Gn[:, d], poolA, poolB, ALU.subtract)
                        if d < 3:
                            step(last)
                    last.then_inc(*sig("g_ready").up())

                @block.tensor
                def _(pe):
                    pe.wait_ge(*sig("dt_rows").at(1))
                    nc.tensor.transpose(ps[:, 0, 0:16], ldtw, ident[0:16, 0:16]).then_inc(*sig("dt_turned").up())
                    pe.wait_ge(*sig("powers_ready").at(1))
                    for n in range(16):
                        r, h, j = n // 8, n // 4 % 2, 4 * (n % 4)
                        if n >= 4:
                            pe.wait_ge(*sig("power_out").at(n - 3))
                        for q in range(4):
                            last = nc.tensor.transpose(ps[:, n % 4, q * P:(q + 1) * P],
                                                       R[:, r, j + q, 4 * h:4 * h + 4, :].rearrange("p d c -> p (d c)"), ident)
                        last.then_inc(*sig("power_turned").up())
                    pe.wait_ge(*sig("steps_stacked").at(1))
                    pe.wait_ge(*sig("power_out").at(16))
                    for r in range(2):
                        for j in range(NP):
                            for h in range(2):
                                last = nc.tensor.matmul(ps[:, 4 + 2 * r + j // 8, 64 * (j % 8):64 * (j % 8) + 64],
                                                        RT[:, r, h, j, :], US[:, h, j, :], start=h == 0, stop=h == 1)
                    last.then_inc(*sig("chunks_in").up())
                    pe.wait_ge(*sig("chunks_in").at(1))
                    for r in range(2):
                        for m in range(4):
                            last = nc.tensor.transpose(ps[:, r, m * P:(m + 1) * P],
                                                       Cpad[:, r, m].rearrange("p g s -> p (g s)"), ident)
                    last.then_inc(*sig("c_turned").up())
                    pe.wait_ge(*sig("g_ready").at(1))
                    pe.wait_ge(*sig("g_late").at(1))

                    def kernels(m):
                        if m >= 2:
                            pe.wait_ge(*sig("kernel_out").at(m - 1))
                        for q in range(4):
                            o = ps[32 * q:32 * q + 32, m % 2, 0:256]
                            nc.tensor.matmul(o, BB[:, 0, 4 * m + q, :], Gr[:, 0:L, 4 * m + q, :], start=True, stop=False)
                            last = nc.tensor.matmul(o, BB[:, 1, 4 * m + q, :], Gn[:, 0:L, 4 * m + q, :], start=False, stop=True)
                        last.then_inc(*sig("kernel_ready").up())
                    kernels(0)
                    for m in range(4):
                        if m < 3:
                            kernels(m + 1)
                        y = ps[:, 4 + m, :].rearrange("p (n l) -> p n l", l=L)
                        pe.wait_ge(*sig("kernel_out").at(m + 1))
                        pe.wait_ge(*sig("scanned").at(1))
                        for d in range(L):
                            last = nc.tensor.matmul(y[:, :, d:L], KB[:, m % 2, d, :], UV[:, m, :, 0:L - d],
                                                    start=d == 0, stop=False, skip_group_check=True)
                        last.then_inc(*sig("inside_done").up())
                        for q in range(4):
                            for t in range(L):
                                for G, r in ((Gr, 0), (Gn, 1)):
                                    last = nc.tensor.matmul(y[32 * q:32 * q + 32, :, t], G[:, t + 1, 4 * m + q, :],
                                                            HS[:, r, 4 * m + q, :], start=False, stop=True,
                                                            skip_group_check=True)
                        last.then_inc(*sig("y_ready").up())
        def gla(AQ, AK, V, ALR, W2, AR, OUT):
            NC = T // 64
            B, DM, DL = part_of(1, 0, 2), part_of(1, 2, 4), part_of(1, 4, 6)
            E1, E2, E3, E4 = (part_of(2, 2 * i, 2 * i + 2) for i in range(4))
            QD, KD, KE, QE = (part_of(6, 2 * i, 2 * i + 2) for i in range(4))
            KTOK = flat(part_of(7, 4, 6)).rearrange("p (m i c) -> p m i c", m=2, i=TT)
            ATT = part_of(1, 4, 8)
            S = flat(part_of(7, 0, 4)).rearrange("p (m n v) -> p m n v", m=2, n=NC)
            O, SQ = part_of(2, 0, 4), part_of(2, 4, 8)
            VAR = part_of(6, 0, 4)
            KEEP = flat(part_of(5, 7, 8))

            def ch(v):
                return v.rearrange("p m (n l) -> p (m n) l", l=64)

            def point(v, k):
                return ch(v)[:, :, k:k + 1].broadcast_to([P, 2 * NC, 64])
            with phase() as block:
                @block.sync
                def _(sp):
                    sp.dma_start(W2, a["gla_w_a2_2"][0]).then_inc(sig("gate_w").handle, 16)
                    at = CONST_AT["keep64"]
                    sp.dma_start(KEEP, a["constants"][:, at:at + T]).then_inc(sig("keep_in").handle, 16)

                @block.tensor
                def _(pe):
                    pe.wait_ge(sig("gate_w").handle, 16)
                    for m in range(2):
                        last = nc.tensor.matmul(ps[:, m, :], W2[:, m * P:m * P + P], ALR, start=True, stop=True)
                    last.then_inc(*sig("decay_in").up())
                    pe.wait_ge(*sig("gla_factors").at(1))
                    for m in range(2):
                        for i in range(TT):
                            last = nc.tensor.transpose(ps[:, 2 + m, i * P:i * P + P], KE[:, m, i * P:i * P + P], ident)
                    last.then_inc(*sig("k_turned").up())
                    for h in range(4):
                        r = 64 * (h % 2)
                        for i in range(TT):
                            w = slice(i * P, i * P + P)
                            last = nc.tensor.matmul(ps[:, 4 + h, w], KD[r:r + 64, h // 2, w], QD[r:r + 64, h // 2, w],
                                                    start=True, stop=True)
                    last.then_inc(*sig("gla_scores").up())
                    pe.wait_ge(*sig("k_tok").at(1))
                    for m in range(2):
                        for n in range(NC - 1):
                            q = slice(64 * (n % 2), 64 * (n % 2) + 64)
                            for g in range(2):
                                h = 2 * m + g
                                last = nc.tensor.matmul(ps[64 * g:64 * g + 64, 2 * m + n % 2, P * (n // 2):P * (n // 2) + P],
                                                        KTOK[q, m, n // 2, 64 * g:64 * g + 64],
                                                        V[q, n // 2, h * P:h * P + P], start=True, stop=True)
                    last.then_inc(*sig("state_adds").up())
                    pe.wait_ge(*sig("att_masked").at(1))
                    pe.wait_ge(*sig("states_ready").at(1))
                    for h in range(4):
                        r = 64 * (h % 2)
                        for i in range(TT):
                            nc.tensor.matmul(ps[:, 4 + h, i * P:i * P + P], V[:, i, h * P:h * P + P],
                                             ATT[:, h, i * P:i * P + P], start=True, stop=False, skip_group_check=True)
                            for n in (2 * i, 2 * i + 1):
                                last = nc.tensor.matmul(ps[:, 4 + h, 64 * n:64 * n + 64], S[r:r + 64, h // 2, n, :],
                                                        QE[r:r + 64, h // 2, 64 * n:64 * n + 64],
                                                        start=False, stop=True, skip_group_check=True)
                        last.then_inc(*sig("heads_ready").up())
                    HeadNorm(4, SQ, VAR).tensor(pe)

                @block.scalar
                def _(act):
                    step = stepper(act, "act_step")
                    act.wait_ge(*sig("decay_in").at(1))
                    for m in range(2):
                        last = nc.scalar.activation(DM[:, m, :], ps[:, m, :], ACT.Identity, bias=col("gla_b_a_2", m))
                    step(last)
                    step(nc.scalar.activation(DL, DM, ACT.Abs))
                    step(nc.scalar.activation(DL, DL, ACT.Exp, scale=-1.0))
                    nc.scalar.activation(DL, DL, ACT.Ln, bias=1.0).then_inc(*sig("soft_ready").up())
                    act.wait_ge(*sig("decays_ready").at(1))
                    nc.scalar.activation(E1, DM, ACT.Exp)
                    nc.scalar.activation(E2, DM, ACT.Exp, scale=-1.0)
                    nc.scalar.activation(E3, DL, ACT.Exp, scale=-1.0)
                    nc.scalar.activation(E4, B, ACT.Exp).then_inc(*sig("exps_ready").up())
                    act.wait_ge(*sig("k_turned").at(1))
                    nc.scalar.activation(KTOK.rearrange("p m i c -> p (m i c)"),
                                         ps[:, 2:4, :].rearrange("p b n -> p (b n)"), ACT.Copy).then_inc(*sig("k_tok").up())
                    HeadNorm(4, SQ, VAR).scalar(act)

                @block.vector
                def _(dve):
                    step = stepper(dve, "dve_step")
                    dve.wait_ge(*sig("soft_ready").at(1))
                    step(nc.vector.tensor_scalar(DM, DM, 0.0, None, ALU.min))
                    step(nc.vector.tensor_tensor(DM, DM, DL, ALU.subtract))
                    step(nc.vector.tensor_scalar(DM, DM, 1.0 / 16.0, None, ALU.mult))
                    dve.wait_ge(sig("keep_in").handle, 16)
                    for m in range(2):
                        step(nc.vector.tensor_tensor_scan(B[:, m, :], KEEP, DM[:, m, :], 0.0, ALU.mult, ALU.add))
                    step(nc.vector.tensor_tensor(ch(DM), ch(B), point(B, 32), ALU.subtract))
                    nc.vector.tensor_tensor(ch(DL), ch(B), point(B, 63), ALU.subtract).then_inc(*sig("decays_ready").up())
                    dve.wait_ge(*sig("exps_ready").at(1))
                    nc.vector.scalar_tensor_tensor(QD, AQ, 0.125, E1, ALU.mult, ALU.mult)
                    nc.vector.tensor_tensor(KD, AK, E2, ALU.mult)
                    nc.vector.tensor_tensor(KE, AK, E3, ALU.mult)
                    nc.vector.scalar_tensor_tensor(QE, AQ, 0.125, E4, ALU.mult, ALU.mult).then_inc(*sig("gla_factors").up())
                    dve.wait_ge(*sig("gla_scores").at(1))
                    m64 = const("chunk64").rearrange("p (a c) -> p a c", a=1).broadcast_to([P, 16, P])
                    nc.vector.tensor_tensor(ATT.rearrange("p h (i c) -> p (h i) c", c=P),
                                            ps[:, 4:8, :].rearrange("p h (i c) -> p (h i) c", c=P), m64, ALU.mult)\
                      .then_inc(*sig("att_masked").up())
                    step(nc.vector.memset(S[:, :, 0, :], 0.0))
                    dve.wait_ge(*sig("state_adds").at(1))
                    for n in range(NC - 1):
                        for m in range(2):
                            last = nc.vector.scalar_tensor_tensor(
                                S[:, m, n + 1, :], S[:, m, n, :], E4[:, m, 64 * n + 63:64 * n + 64],
                                ps[:, 2 * m + n % 2, P * (n // 2):P * (n // 2) + P], ALU.mult, ALU.add)
                        if n < NC - 2:
                            step(last)
                    last.then_inc(*sig("states_ready").up())

                    def take_head(h, head, inverse):
                        nc.vector.scalar_tensor_tensor(O[:, h, :], AR[:, h, :], col("gla_head_g_2", 0), head,
                                                       ALU.mult, ALU.mult).then_inc(*sig("head_gated").up())
                        dve.wait_ge(*sig("head_gated").at(h + 1))
                        nc.vector.tensor_tensor(OUT[:, h, :], O[:, h, :], inverse, ALU.mult)
                    HeadNorm(4, SQ, VAR).vector(dve, take_head)

        def rotate(XS):
            TMP = big(7)
            COS, SIN = flat(part_of(8, 0, 1)), flat(part_of(8, 1, 2))
            with phase() as block:
                @block.sync
                def _(sp):
                    for dst, name in ((COS, "cos"), (SIN, "sin")):
                        sp.dma_start(dst, a["constants"][:, CONST_AT[name]:CONST_AT[name] + T])\
                          .then_inc(sig("tables_in").handle, 16)

                @block.tensor
                def _(pe):
                    for t in range(8):
                        last = nc.tensor.matmul(ps[:, t, :], const("turn"), XS[t // 4][:, t % 4, :], start=True, stop=True)
                    last.then_inc(*sig("turned").up())

                @block.vector
                def _(dve):
                    step = stepper(dve, "dve_step")
                    dve.wait_ge(*sig("turned").at(1))
                    dve.wait_ge(sig("tables_in").handle, 32)
                    step(nc.vector.tensor_tensor(TMP, ps[:, :, :], bc(SIN, 8), ALU.mult))
                    for v in XS:
                        step(nc.vector.tensor_tensor(v, v, bc(COS, 4), ALU.mult))
                    for i, v in enumerate(XS):
                        last = nc.vector.tensor_tensor(v, v, TMP[:, 4 * i:4 * i + 4, :], ALU.add)

        MOFF = [0, 128, 384, 768]

        class SelectKeys:
            NB3 = TT - 1
            NS = [P * (b + 2) for b in range(TT - 1)]
            ROUNDS = TOPK // 8 - 1

            def __init__(self, IQ, IK, NB, MASK):
                self.IQ, self.IK, self.NB, self.MASK = IQ, IK, NB, MASK
                f6, f7 = flat(big(6)), flat(big(7))
                self.SC = [f6[:, 512 * b:512 * b + 512] for b in range(self.NB3)]
                self.WK = [f6[:, 1536 + 512 * b:2048 + 512 * b] for b in range(self.NB3)]
                self.RL = [f6[:, 3072:3584], f6[:, 3584:4096]]
                self.ONE, self.EQ, self.CUM = (f7[:, 512 * i:512 * i + 512] for i in range(3))
                self.top, self.cnt = small[:, 0:24], small[:, 24:27]
                self.iw = small[:, 32:48].rearrange("p (i h) -> p i h", i=TT)

            def scores(self):
                IQ, IK, NB3, NS, SC, WK, RL, iw = (self.IQ, self.IK, self.NB3, self.NS, self.SC, self.WK, self.RL,
                                                   self.iw)
                with phase() as block:
                    @block.tensor
                    def _(pe):
                        for b in range(NB3):
                            i, ns = 1 + b, NS[b]
                            for h in range(4):
                                r = 64 * (h % 2)
                                if b == 2:
                                    pe.wait_ge(*sig("index_relu").at(h + 1))
                                nc.tensor.matmul(ps[:, (4 * b + h) % 8, 0:ns], IQ[r:r + 64, h // 2, i * P:i * P + P],
                                                 IK[r:r + 64, 0:ns], start=True, stop=True)\
                                  .then_inc(*sig("index_ready").up())

                    @block.scalar
                    def _(act):
                        for n in range(4 * NB3):
                            b = n // 4
                            act.wait_ge(*sig("index_ready").at(n + 1))
                            if n >= 2:
                                act.wait_ge(*sig("index_added").at(n - 1))
                            nc.scalar.activation(RL[n % 2][:, 0:NS[b]], ps[:, n % 8, 0:NS[b]], ACT.Relu, scale=0.125)\
                              .then_inc(*sig("index_relu").up())

                    @block.vector
                    def _(dve):
                        step = stepper(dve, "dve_step")
                        step(nc.vector.tensor_scalar(iw, self.NB[:, :, 64:68], 0.5, None, ALU.mult))
                        nc.vector.memset(self.ONE, 1.0)
                        nc.vector.tensor_copy(self.MASK[:, 0:P], const("notyet"))
                        for n in range(4 * NB3):
                            b, h = n // 4, n % 4
                            s, rl = SC[b][:, 0:NS[b]], RL[n % 2][:, 0:NS[b]]
                            w = iw[:, 1 + b, h:h + 1]
                            dve.wait_ge(*sig("index_relu").at(n + 1))
                            if h == 0:
                                last = nc.vector.tensor_scalar(s, rl, w, None, ALU.mult)
                            else:
                                last = nc.vector.scalar_tensor_tensor(s, rl, w, s, ALU.mult, ALU.add)
                            last.then_inc(*sig("index_added").up())
                            dve.wait_ge(*sig("index_added").at(n + 1))
                        for b in range(NB3):
                            d = SC[b][:, NS[b] - P:NS[b]]
                            step(nc.vector.tensor_tensor(d, d, const("notyet"), ALU.add))
                            nc.vector.tensor_copy(WK[b][:, 0:NS[b]], SC[b][:, 0:NS[b]])

            def best_eight(self, dve):
                h = sig("top_step")
                for b in range(self.NB3):
                    nc.vector.max(self.top[:, 8 * b:8 * b + 8], self.WK[b][:, 0:self.NS[b]]).then_inc(*h.up())
                dve.wait_ge(h.handle, h.total)
                nc.vector.memset(self.cnt, 0.0)
                for b in range(self.NB3):
                    w = self.WK[b][:, 0:self.NS[b]]
                    nc.vector.match_replace(w, self.top[:, 8 * b:8 * b + 8], w, NEG).then_inc(*h.up())
                dve.wait_ge(h.handle, h.total)

            def beside(self, dve, name, u):
                n = 2 * {"aqk": 0, "av": 1, "ar": 2}[name] + u
                for _ in range(self.ROUNDS * n // 6, self.ROUNDS * (n + 1) // 6):
                    self.best_eight(dve)

            def finish(self, engine, eng, name):
                if engine != "vector":
                    return
                step = stepper(eng, "dve_step")
                top, cnt = self.top, self.cnt
                for b in range(self.NB3):
                    ns = self.NS[b]
                    s, gt, eq, cum = self.SC[b][:, 0:ns], self.WK[b][:, 0:ns], self.EQ[:, 0:ns], self.CUM[:, 0:ns]
                    m = self.MASK[:, MOFF[1 + b]:MOFF[1 + b] + ns]
                    step(nc.vector.max(top[:, 8 * b:8 * b + 8], self.WK[b][:, 0:ns]))
                    th = top[:, 8 * b + 7:8 * b + 8]
                    step(nc.vector.tensor_scalar(gt, s, th, None, ALU.is_gt))
                    step(nc.vector.tensor_scalar(eq, s, th, None, ALU.is_equal))
                    step(nc.vector.tensor_reduce(cnt[:, b:b + 1], gt, AXX, ALU.add))
                    step(nc.vector.tensor_scalar(cnt[:, b:b + 1], cnt[:, b:b + 1], -1.0, float(TOPK), ALU.mult, ALU.add))
                    step(nc.vector.tensor_tensor_scan(cum, self.ONE[:, 0:ns], eq, 0.0, ALU.mult, ALU.add))
                    step(nc.vector.scalar_tensor_tensor(eq, cum, cnt[:, b:b + 1], eq, ALU.is_le, ALU.mult))
                    step(nc.vector.tensor_tensor(gt, gt, eq, ALU.add))
                    step(nc.vector.tensor_scalar(m, gt, 1.0, -NEG, ALU.subtract, ALU.mult))

        def sparse_attention(BQ, BK, NB, MASK, OUT):
            SOFF = [0, 128, 512, 1024]
            f6, f7, f8 = flat(big(1)), flat(big(2)), flat(big(6))
            SM = [f6[:, 0:CAUSAL], f6[:, CAUSAL:2 * CAUSAL]]
            EX = [f7[:, 0:CAUSAL], f7[:, CAUSAL:2 * CAUSAL]]
            PT = [f8[:, 0:CAUSAL], f8[:, CAUSAL:2 * CAUSAL]]
            S = ps[:, 0:3, :].rearrange("p b n -> p (b n)")
            TP = ps[:, 3:6, :].rearrange("p b n -> p (b n)")
            mx = [small[:, 64 + 4 * i:68 + 4 * i] for i in range(2)]
            nm = [small[:, 72 + 4 * i:76 + 4 * i] for i in range(2)]
            sm = [small[:, 80 + 4 * i:84 + 4 * i] for i in range(2)]
            with phase() as block:
                @block.tensor
                def _(pe):
                    def scores(h):
                        r = 64 * (h % 2)
                        if h:
                            pe.wait_ge(*sig("masked").at(h))
                        for i in range(TT):
                            n = P * (i + 1)
                            last = nc.tensor.matmul(S[:, SOFF[i]:SOFF[i] + n], BQ[r:r + 64, h // 2, i * P:i * P + P],
                                                    BK[r:r + 64, 0:n], start=True, stop=True)
                        last.then_inc(*sig("scores_ready").up())
                    scores(0)
                    scores(1)

                    def turn(h):
                        pe.wait_ge(*sig("probs_ready").at(h + 1))
                        if h:
                            pe.wait_ge(*sig("probs_out").at(h))
                        for j in range(TT):
                            for i in range(j, TT):
                                last = nc.tensor.transpose(TP[:, PACK[j] + P * (i - j):PACK[j] + P * (i - j) + P],
                                                           EX[h % 2][:, MOFF[i] + j * P:MOFF[i] + j * P + P], ident)
                        last.then_inc(*sig("probs_turned").up())

                    def values(h):
                        r = 64 * (h % 2)
                        pe.wait_ge(*sig("probs_out").at(h + 1))
                        if h >= 2:
                            pe.wait_ge(*sig("head_out").at(h - 1))
                        for j in range(TT):
                            last = nc.tensor.matmul(ps[r:r + 64, 6 + h % 2, j * P:T], NB[:, j, 0:64],
                                                    PT[h % 2][:, PACK[j]:PACK[j] + WIDE[j]], start=j == 0, stop=j == TT - 1)
                        last.then_inc(*sig("values_ready").up())
                    for h in range(8):
                        if h < 6:
                            scores(h + 2)
                        turn(h)
                        if h:
                            values(h - 1)
                    values(7)

                @block.scalar
                def _(act):
                    def turn_out(h):
                        act.wait_ge(*sig("probs_turned").at(h + 1))
                        if h >= 2:
                            act.wait_ge(*sig("values_ready").at(h - 1))
                        nc.scalar.activation(PT[h % 2], TP[:, 0:CAUSAL], ACT.Copy).then_inc(*sig("probs_out").up())

                    def head_out(h):
                        r = 64 * (h % 2)
                        act.wait_ge(*sig("values_ready").at(h + 1))
                        nc.scalar.activation(OUT[r:r + 64, h // 2, :], ps[r:r + 64, 6 + h % 2, :], ACT.Copy)\
                          .then_inc(*sig("head_out").up())
                    for h in range(8):
                        act.wait_ge(*sig("maximum").at(h + 1))
                        if h >= 2:
                            act.wait_ge(*sig("probs_turned").at(h - 1))
                        for i in range(TT):
                            w = slice(MOFF[i], MOFF[i] + P * (i + 1))
                            last = nc.scalar.activation(EX[h % 2][:, w], SM[h % 2][:, w], ACT.Exp, scale=0.125,
                                                        bias=nm[h % 2][:, i:i + 1], accum_out=sm[h % 2][:, i:i + 1])
                        last.then_inc(*sig("exps_ready").up())
                        if h:
                            turn_out(h - 1)
                        if h >= 2:
                            head_out(h - 2)
                    turn_out(7)
                    head_out(6)
                    head_out(7)

                @block.gpsimd
                def _(pool):
                    for h in range(8):
                        pool.wait_ge(*sig("sums_inverted").at(h + 1))
                        for i in range(TT):
                            w = slice(MOFF[i], MOFF[i] + P * (i + 1))
                            last = nc.gpsimd.tensor_tensor(
                                EX[h % 2][:, w], EX[h % 2][:, w],
                                sm[h % 2][:, i:i + 1].broadcast_to([P, P * (i + 1)]), ALU.mult)
                        last.then_inc(*sig("probs_ready").up())

                @block.vector
                def _(dve):
                    def masked(h):
                        dve.wait_ge(*sig("scores_ready").at(h + 1))
                        if h >= 2:
                            dve.wait_ge(*sig("exps_ready").at(h - 1))
                        for i in range(TT):
                            n = P * (i + 1)
                            w = slice(MOFF[i], MOFF[i] + n)
                            last = nc.vector.tensor_tensor_reduce(
                                out=SM[h % 2][:, w], in0=S[:, SOFF[i]:SOFF[i] + n], in1=MASK[:, w], scale=1.0,
                                scalar=NEG, op0=ALU.add, op1=ALU.max, accum_out=mx[h % 2][:, i:i + 1])
                        last.then_inc(*sig("masked").up())
                        dve.wait_ge(*sig("masked").at(h + 1))
                        nc.vector.tensor_scalar(nm[h % 2], mx[h % 2], -0.125, None, ALU.mult).then_inc(*sig("maximum").up())
                    masked(0)
                    for h in range(8):
                        dve.wait_ge(*sig("exps_ready").at(h + 1))
                        nc.vector.reciprocal(sm[h % 2], sm[h % 2]).then_inc(*sig("sums_inverted").up())
                        if h < 7:
                            masked(h + 1)

        def sgu(U, V):
            f4, f5 = flat(big(5)), flat(big(6))
            GB, BB, BS = f4[:, 0:1024], f4[:, 1024:2048], f4[:, 2048:3072].rearrange("p (g t) -> p g t", g=8)
            WS, WT = (f5[:, 1024 * i:1024 * i + 1024].rearrange("p (g s) -> p g s", g=8) for i in range(2))
            st = small[:, 0:48].rearrange("p (i h s) -> p i h s", i=TT, h=2)
            mv = small[:, 48:56].rearrange("p (i s) -> p i s", i=TT)
            sd = small[:, 56:60]
            TMP = [f5[:, 2048:2560], f5[:, 2560:3072]]
            with phase() as block:
                @block.sync
                def _(sp):
                    for dst, name in ((GB, "sgu_ln_g_2"), (BB, "sgu_ln_b_2")):
                        sp.dma_start(dst, a[name].broadcast_to([P, 1024])).then_inc(sig("sgu_rows").handle, 16)
                    sp.dma_start(f4[:, 2048:3072], a["sgu_b_s_2"].rearrange("a g t -> a (g t)").broadcast_to([P, 1024]))\
                      .then_inc(sig("sgu_rows").handle, 16)
                    sp.dma_start(WS, a["sgu_w_s_2"][0].rearrange("g t s -> t g s")).then_inc(sig("sgu_w").handle, 16)

                @block.tensor
                def _(pe):
                    pe.wait_ge(sig("sgu_w").handle, 16)
                    for g in range(8):
                        last = nc.tensor.transpose(ps[:, g // 4, P * (g % 4):P * (g % 4) + P], WS[:, g, :], ident)
                    last.then_inc(*sig("w_turned").up())
                    pe.wait_ge(*sig("v_normed").at(1))
                    for g in range(8):
                        if g >= 4:
                            pe.wait_ge(*sig("mixed_out").at(g - 3))
                        for i in range(TT):
                            last = nc.tensor.matmul(ps[:, 4 + g % 4, i * P:i * P + P], V[:, i, g * P:g * P + P], WT[:, g, :],
                                                    start=True, stop=True)
                        last.then_inc(*sig("mixed").up())

                @block.scalar
                def _(act):
                    act.wait_ge(*sig("variance").at(1))
                    nc.scalar.activation(sd, sd, ACT.Sqrt).then_inc(*sig("deviation").up())

                @block.vector
                def _(dve):
                    step = stepper(dve, "dve_step")
                    for i in range(TT):
                        for h in range(2):
                            last = nc.vector.bn_stats(st[:, i, h, :], V[:, i, 512 * h:512 * h + 512])
                    step(last)
                    for i in range(TT):
                        last = nc.vector.bn_aggr(mv[:, i, :], st[:, i].rearrange("p h s -> p (h s)"))
                    step(last)
                    nc.vector.tensor_scalar(sd, mv[:, :, 1], LN_EPS, None, ALU.add).then_inc(*sig("variance").up())
                    dve.wait_ge(*sig("w_turned").at(1))
                    nc.vector.tensor_tensor(WT, ps[:, 0:2, :].rearrange("p b (g t) -> p (b g) t", t=P),
                                            bc(const("upto"), 8), ALU.mult)
                    dve.wait_ge(*sig("deviation").at(1))
                    step(nc.vector.reciprocal(sd, sd))
                    for i in range(TT):
                        last = nc.vector.tensor_scalar(V[:, i, :], V[:, i, :], mv[:, i, 0:1], sd[:, i:i + 1],
                                                       ALU.subtract, ALU.mult)
                    step(last)
                    dve.wait_ge(sig("sgu_rows").handle, 48)
                    step(nc.vector.tensor_tensor(V, V, bc(GB, TT), ALU.mult))
                    nc.vector.tensor_tensor(V, V, bc(BB, TT), ALU.add).then_inc(*sig("v_normed").up())
                    for g in range(8):
                        dve.wait_ge(*sig("mixed").at(g + 1))
                        t = TMP[g % 2]
                        nc.vector.tensor_tensor(t.rearrange("p (i c) -> p i c", c=P),
                                                ps[:, 4 + g % 4, :].rearrange("p (i c) -> p i c", c=P),
                                                BS[:, g:g + 1, :].broadcast_to([P, TT, P]), ALU.add)\
                          .then_inc(*sig("mixed_out").up())
                        dve.wait_ge(*sig("mixed_out").at(g + 1))
                        nc.vector.tensor_tensor(U[:, g, :], U[:, g, :], t, ALU.mult)

        class HeadNorm:

            def __init__(self, heads, SQ, DIAG):
                self.heads, self.other, self.SQ, self.DIAG = heads, 4 - heads, SQ, DIAG
                self.inv = small[:, 96:112]

            def scalar(self, act):
                for h in range(4):
                    act.wait_ge(*sig("heads_ready").at(h + 1))
                    nc.scalar.activation(self.SQ[:, h, :], ps[:, self.heads + h, :], ACT.Square)\
                      .then_inc(*sig("heads_squared").up())
                act.wait_ge(*sig("variance").at(1))
                nc.scalar.activation(self.inv, self.inv, ACT.Sqrt).then_inc(*sig("deviation").up())

            def tensor(self, pe):
                for h in range(4):
                    pe.wait_ge(*sig("heads_squared").at(h + 1))
                    for i in range(TT):
                        last = nc.tensor.matmul(ps[:, self.other, 4 * h + i:4 * h + i + 1],
                                                self.SQ[:, h, i * P:i * P + P], const("ones")[:, 0:1],
                                                start=True, stop=True)
                last.then_inc(*sig("heads_summed").up())
                for h in range(4):
                    pe.wait_ge(*sig("diagonals").at(h + 1))
                    nc.tensor.matmul(ps[:, self.other + h, :], const("ones"), self.DIAG[:, h, :], start=True, stop=True)\
                      .then_inc(*sig("inverse_spread").up())

            def vector(self, dve, take_head):
                step = stepper(dve, "dve_step")
                dve.wait_ge(*sig("heads_summed").at(1))
                nc.vector.tensor_scalar(self.inv, ps[:, self.other, 0:16], 1.0 / P, RMS_EPS, ALU.mult, ALU.add)\
                  .then_inc(*sig("variance").up())
                dve.wait_ge(*sig("deviation").at(1))
                step(nc.vector.reciprocal(self.inv, self.inv))
                for h in range(4):
                    nc.vector.tensor_tensor(self.DIAG[:, h, :].rearrange("p (i c) -> p i c", c=P), bc(ident, TT),
                                            bl(self.inv[:, 4 * h:4 * h + 4], P), ALU.mult).then_inc(*sig("diagonals").up())
                for h in range(4):
                    dve.wait_ge(*sig("inverse_spread").at(h + 1))
                    take_head(h, ps[:, self.heads + h, :], ps[:, self.other + h, :])

        def column(name, first):
            return lambda k: col(name, k + first)

        def conv_taps(name, first, tiles):
            return lambda j, m: col(name, m + (first + tiles * j))

        def block2():
            AQK, AR = part_of(3, 0, 4), part_of(3, 4, 8)
            V, BQ, IQK = part_of(4, 0, 4), part_of(4, 4, 8), part_of(5, 0, 4)
            ALR = part_of(5, 4, 5)[0:16, 0, :]
            NB = part_of(5, 5, 6)[:, 0, 0:272].rearrange("p (i c) -> p i c", i=TT)
            W2 = part_of(5, 6, 7)[0:16, 0, 0:256]
            OA, OB = part_of(8, 0, 4), part_of(7, 0, 4)

            def narrow(u, t, bank):
                if t == 0:
                    return nc.scalar.activation(ALR, ps[0:16, bank, :], ACT.Copy)
                return nc.scalar.activation(NB[:, t - 1, :], ps[:, bank, 0:68], ACT.Copy)
            products([fjob("bq", ACTS, BQ), fjob("iq", ACTS, IQK[:, 0:2]), fjob("shared", ACTS, IQK[:, 2:4]),
                      ("narrow", ACTS, "act", narrow)],
                     norm=Norm(X, KT, False, RMS_EPS, column("attn_norm_2", 0), split=(act_hi, act_lo)))
            rotate([BQ, IQK])
            MASK = rows[:, 0:3, :].rearrange("p a n -> p (a n)")[:, 0:CAUSAL]
            select = SelectKeys(IQK[:, 0:2], IQK[:, 3, :], NB, MASK)
            select.scores()
            products([fjob("aqk", ACTS, AQK), tjob("av", ACTS, V), fjob("ar", ACTS, AR, ACT.Silu)],
                     select.beside, select.finish)
            gla(AQK[:, 0:2], AQK[:, 2:4], V, ALR, W2, AR, OA)
            sparse_attention(BQ, IQK[:, 2, :], NB, MASK, OB)
            products([resjob("w_o", ACTS)], center=False,
                     norm=Split(split_tiles(OA, act_hi[:, 0:4], act_lo[:, 0:4])
                                + split_tiles(OB, act_hi[:, 4:8], act_lo[:, 4:8])))

            def ffn_layer(tag, l):
                norm = Norm(X, KT, False, RMS_EPS, column("ffn_norm_2", 8 * l), split=(act_hi, act_lo), stats=True)
                ffn_phase(tag, "conv", norm, center=False, taps=conv_taps("ffn_conv_w_2", 132 * l, 44),
                          tap_bias=column("ffn_conv_b_2", 44 * l))
            ffn_layer("ffn2", 0)
            V2 = big(4).rearrange("p k t -> p (k t)").rearrange("p (i n) -> p i n", i=TT)
            products([fjob("sgu_u", ACTS, big(3), GELU), tjob("sgu_v", ACTS, V2, GELU)],
                     norm=Norm(X, KT, False, RMS_EPS, column("sgu_norm_2", 0), split=(act_hi, act_lo), stats=True))
            sgu(big(3), V2)
            products([resjob("sgu_out", ACTS)], center=False, norm=Split(split_tiles(big(3), act_hi, act_lo)))
            ffn_layer("ffn3", 1)
            return Norm(X, KT, False, RMS_EPS, column("final_norm_2", 0), dst=X, split=(act_hi, act_lo), stats=True)

        def hgrn(Q, Fz, V, K):
            lb, om = small[:, 0:8], small[:, 8:16]
            e0, e1, mm = small[:, 16:24], small[:, 24:32], small[:, 32:40]
            lg = COLUMN["hgrn_lb_logits_3"]
            l0, l1 = cols[:, lg:lg + 8], cols[:, lg + 8:lg + 16]
            LOGS, KEEP = big(1), flat(part_of(2, 0, 1))
            with phase() as block:
                @block.sync
                def _(sp):
                    at = CONST_AT["keep128"]
                    sp.dma_start(KEEP, a["constants"][:, at:at + T]).then_inc(sig("keep3_in").handle, 16)

                @block.vector
                def _(dve):
                    step = stepper(dve, "dve_step")
                    step(nc.vector.tensor_tensor(mm, l0, l1, ALU.max))
                    step(nc.vector.tensor_tensor(e0, l0, mm, ALU.subtract))
                    nc.vector.tensor_tensor(e1, l1, mm, ALU.subtract).then_inc(*sig("logits_ready").up())
                    dve.wait_ge(*sig("logit_exps").at(1))
                    step(nc.vector.tensor_tensor(mm, e0, e1, ALU.add))
                    step(nc.vector.reciprocal(mm, mm))
                    step(nc.vector.tensor_tensor(lb, e0, mm, ALU.mult))
                    step(nc.vector.tensor_scalar(om, lb, -1.0, 1.0, ALU.mult, ALU.add))
                    for k in range(KT):
                        dve.wait_ge(*sig("sigmoids").at(k + 1))
                        nc.vector.tensor_scalar(K[:, k, :], K[:, k, :], om[:, k:k + 1], None, ALU.mult)
                        nc.vector.tensor_scalar(Fz[:, k, :], Fz[:, k, :], om[:, k:k + 1], lb[:, k:k + 1],
                                                ALU.mult, ALU.add).then_inc(*sig("forget_ready").up())
                    dve.wait_ge(sig("keep3_in").handle, 16)
                    for k in range(KT):
                        dve.wait_ge(*sig("log_ready").at(k + 1))
                        nc.vector.tensor_tensor_scan(Fz[:, k, :], KEEP, LOGS[:, k, :], 0.0,
                                                     ALU.mult, ALU.add)

                @block.scalar
                def _(act):
                    act.wait_ge(*sig("logits_ready").at(1))
                    nc.scalar.activation(small[:, 16:32], small[:, 16:32], ACT.Exp).then_inc(*sig("logit_exps").up())
                    for k in range(KT):
                        nc.scalar.activation(K[:, k, :], Fz[:, k, :], ACT.Sigmoid, scale=-1.0).then_inc(*sig("act_step").up())
                        act.wait_ge(sig("act_step").handle, sig("act_step").total)
                        nc.scalar.activation(Fz[:, k, :], Fz[:, k, :], ACT.Sigmoid).then_inc(*sig("sigmoids").up())
                    for k in range(KT):
                        act.wait_ge(*sig("forget_ready").at(k + 1))
                        nc.scalar.activation(LOGS[:, k, :], Fz[:, k, :], ACT.Ln).then_inc(*sig("log_ready").up())
            for half in range(2):
                hgrn_heads(Q[:, 4 * half:4 * half + 4], K[:, 4 * half:4 * half + 4], Fz[:, 4 * half:4 * half + 4], V, 4 * half)

        def hgrn_heads(Q, K, B, V, h0):
            QE, KE, KTOK = part_of(7, 0, 4), part_of(7, 4, 8), part_of(1, 0, 4)
            S = flat(part_of(1, 4, 8)).rearrange("p (h n v) -> p h n v", h=4, n=4)
            ATT = KE
            dec = small[:, 64:80].rearrange("p (h n) -> p h n", h=4)
            C = P
            LEVELS = 7

            def ch(v, l=C):
                return v.rearrange("p h (n l) -> p (h n) l", l=l)

            def halves(v, lv):
                h = 64 >> lv
                return v.rearrange("p h (n s l) -> p (h n) s l", s=2, l=h)
            LEVEL = [part_of(2, 4, 8), part_of(2, 0, 4), KTOK]
            norm = HeadNorm(0, LEVEL[0], LEVEL[1])

            def scores_bank(lv):
                return 4 * ((lv + 1) % 2)
            with phase() as block:
                @block.scalar
                def _(act):
                    act.wait_ge(*sig("tail_diff").at(1))
                    nc.scalar.activation(KE, KE, ACT.Exp)
                    nc.scalar.activation(QE, B, ACT.Exp)
                    nc.scalar.activation(dec, B.rearrange("p h (n l) -> p h n l", l=C)[:, :, :, C - 1], ACT.Exp)\
                      .then_inc(*sig("exps_ready").up())
                    for lv in range(2):
                        act.wait_ge(*sig("level_diff").at(lv + 1))
                        nc.scalar.activation(LEVEL[lv], LEVEL[lv], ACT.Exp).then_inc(*sig("level_exp").up())
                    for m in range(4):
                        act.wait_ge(*sig("k_turned").at(m + 1))
                        nc.scalar.activation(KTOK[:, m, :], ps[:, m, :], ACT.Copy).then_inc(*sig("k_tok").up())
                    for lv in range(2, LEVELS):
                        act.wait_ge(*sig("level_diff").at(lv + 1))
                        nc.scalar.activation(LEVEL[lv % 3], LEVEL[lv % 3], ACT.Exp).then_inc(*sig("level_exp").up())
                    norm.scalar(act)

                @block.gpsimd
                def _(pool):
                    for lv in range(LEVELS):
                        b, d = halves(B, lv), halves(LEVEL[lv % 3], lv)
                        hh = 64 >> lv
                        ref = b[:, :, 0, hh - 1:hh].broadcast_to([P, b.shape[1], hh])
                        if lv == 2:
                            pool.wait_ge(*sig("state_adds").at(1))
                        elif lv > 2:
                            pool.wait_ge(*sig("level_scores").at(lv - 1))
                        nc.gpsimd.tensor_tensor(d[:, :, 0, :], ref, b[:, :, 0, :], ALU.subtract)
                        nc.gpsimd.tensor_tensor(d[:, :, 1, :], b[:, :, 1, :], ref, ALU.subtract)\
                          .then_inc(*sig("level_diff").up())

                @block.vector
                def _(dve):
                    step = stepper(dve, "dve_step")
                    nc.vector.tensor_tensor(ch(KE), ch(B)[:, :, C - 1:C].broadcast_to([P, 16, C]), ch(B), ALU.subtract)\
                      .then_inc(*sig("tail_diff").up())
                    dve.wait_ge(*sig("exps_ready").at(1))
                    step(nc.vector.tensor_tensor(QE, QE, Q, ALU.mult))
                    nc.vector.tensor_tensor(KE, KE, K, ALU.mult).then_inc(*sig("tail_ready").up())

                    def level_times(lv):
                        dve.wait_ge(*sig("level_exp").at(lv + 1))
                        x = halves(LEVEL[lv % 3], lv)
                        nc.vector.tensor_tensor(x[:, :, 0, :], halves(K, lv)[:, :, 0, :], x[:, :, 0, :], ALU.mult)
                        nc.vector.tensor_tensor(x[:, :, 1, :], halves(Q, lv)[:, :, 1, :], x[:, :, 1, :], ALU.mult)\
                          .then_inc(*sig("level_ready").up())
                    level_times(0)
                    dve.wait_ge(*sig("state_adds").at(1))
                    step(nc.vector.tensor_copy(S[:, :, 1, :], ps[:, 4:7, :].rearrange("p n (h v) -> p h n v", h=4)[:, :, 0]))
                    for n in (1, 2):
                        for h in range(4):
                            last = nc.vector.scalar_tensor_tensor(S[:, h, n + 1, :], S[:, h, n, :], dec[:, h, n:n + 1],
                                                                  ps[:, 4 + n, h * P:h * P + P], ALU.mult, ALU.add)
                        step(last)
                    nc.vector.memset(ATT, 0.0).then_inc(*sig("states_taken").up())
                    dve.wait_ge(*sig("states_taken").at(1))
                    att = ATT.rearrange("p h (i c) -> p (h i) c", c=P)
                    for lv in range(-1, LEVELS):
                        if 1 <= lv + 2 < LEVELS:
                            level_times(lv + 2)
                        dve.wait_ge(*sig("level_scores").at(lv + 2))
                        bank = scores_bank(lv)
                        if lv >= 0:
                            dve.wait_ge(*sig("level_taken").at(lv + 1))
                        mask = const("ident" if lv < 0 else f"level{lv}").bitcast(I32)
                        nc.vector.copy_predicated(att, bc(mask, 16), ps[:, bank:bank + 4, :].rearrange("p h (i c) -> p (h i) c", c=P))\
                          .then_inc(*sig("level_taken").up())

                    def take_head(h, head, inverse):
                        nc.vector.tensor_scalar(Q[:, h, :], head, col("hgrn_norm_g_3", h0 + h), None, ALU.mult)\
                          .then_inc(*sig("head_gated").up())
                        dve.wait_ge(*sig("head_gated").at(h + 1))
                        nc.vector.tensor_tensor(Q[:, h, :], Q[:, h, :], inverse, ALU.mult)
                    norm.vector(dve, take_head)

                @block.tensor
                def _(pe):
                    pe.wait_ge(*sig("tail_ready").at(1))
                    for h in range(4):
                        for i in range(TT):
                            last = nc.tensor.transpose(ps[:, h, i * P:i * P + P], KE[:, h, i * P:i * P + P], ident)
                        last.then_inc(*sig("k_turned").up())
                    for h in range(4):
                        pe.wait_ge(*sig("k_tok").at(h + 1))
                        for n in range(3):
                            last = nc.tensor.matmul(ps[:, 4 + n, h * P:h * P + P], KTOK[:, h, n * P:n * P + P],
                                                    V[:, n, (h0 + h) * P:(h0 + h) * P + P], start=True, stop=True)
                    last.then_inc(*sig("state_adds").up())
                    for lv in range(-1, LEVELS):
                        bank = scores_bank(lv)
                        if lv >= 0:
                            pe.wait_ge(*sig("level_ready").at(lv + 1))
                        if lv == 0:
                            pe.wait_ge(*sig("states_taken").at(1))
                        if lv >= 1:
                            pe.wait_ge(*sig("level_taken").at(lv))
                        X_ = LEVEL[lv % 3]
                        for h in range(4):
                            for i in range(TT):
                                w = slice(i * P, i * P + P)
                                lhs, rhs = (K[:, h, w], Q[:, h, w]) if lv < 0 else (X_[:, h, w], X_[:, h, w])
                                last = nc.tensor.matmul(ps[:, bank + h, w], lhs, rhs, start=True, stop=True)
                        last.then_inc(*sig("level_scores").up())
                    pe.wait_ge(*sig("level_taken").at(LEVELS + 1))
                    for h in range(4):
                        for i in range(TT):
                            w = slice(i * P, i * P + P)
                            last = nc.tensor.matmul(ps[:, h, w], V[:, i, (h0 + h) * P:(h0 + h) * P + P], ATT[:, h, w],
                                                    start=True, stop=i == 0)
                            if i:
                                last = nc.tensor.matmul(ps[:, h, w], S[:, h, i, :], QE[:, h, w], start=False, stop=True)
                        last.then_inc(*sig("heads_ready").up())
                    norm.tensor(pe)

        def block3(norm):
            CV, CG, CACC, CN = part_of(3, 0, 4), part_of(3, 4, 8), part_of(7, 0, 4), part_of(8, 0, 4)
            V = flat(big(6)).rearrange("p (i n) -> p i n", i=TT)
            if norm is None:
                norm = Split(split_tiles(X, act_hi, act_lo))
            products([fjob("cval", ACTS, CV), fjob("cgate", ACTS, CG, ACT.Sigmoid)], norm=norm)
            NTAP = 31

            def convolve(dve, name, u):
                unit = {"qz": 0, "fz": 4, "iv": 8}[name] + u
                if unit == 0:
                    nc.vector.tensor_tensor(CV, CV, CG, ALU.mult).then_inc(*sig("conv_step").up())
                per = -(-4 * NTAP // 12)
                for n in range(per * unit, min(per * unit + per, 4 * NTAP)):
                    t, k = n // 4, n % 4
                    w = col("w_conv_dw_3", 4 * (NTAP - 1 - t) + k)
                    dve.wait_ge(*sig("conv_step").at(max(1, n - 2)))
                    if t == 0:
                        last = nc.vector.tensor_scalar(CACC[:, k, :], CV[:, k, :], w, col("b_conv_dw_3", k),
                                                       ALU.mult, ALU.add)
                    else:
                        last = nc.vector.scalar_tensor_tensor(CACC[:, k, t:T], CV[:, k, 0:T - t], w,
                                                              CACC[:, k, t:T], ALU.mult, ALU.add)
                    last.then_inc(*sig("conv_step").up())
            products([fjob("qz", ACTS, big(4), ACT.Silu), fjob("fz", ACTS, big(5)), tjob("iv", ACTS, V)], convolve)
            normalize(CACC, 4, True, LN_EPS, column("conv_ln_g_3", 0), column("conv_ln_b_3", 0),
                      func=ACT.Silu, dst=CN, cen=24, sq=28)
            hgrn(big(4), big(5), V, big(3))
            M2 = arena_t[:, 40:56, :]
            products([fjob("gz", ACTS, big(7), ACT.Silu), fjob("mz", ACTS, M2, ACT.Sigmoid)],
                     norm=Split(split_tiles(X, act_hi, act_lo)))

            def gated(k):
                return nc.vector.tensor_tensor(big(4)[:, k, :], big(4)[:, k, :], big(7)[:, k, :], ALU.mult)
            products([merge_job("conv_out", parts(conv_hi, conv_lo), big(5)),
                      merge_job("hgrn_out", ACTS, big(6), big(5))],
                     norm=Split(split_tiles(CN, conv_hi, conv_lo) + split_tiles(big(4), act_hi, act_lo, gated)))
            products([resjob("out3", ACTS, alpha=ALPHA)], center=True, norm=Split(split_tiles(big(5), act_hi, act_lo)))
            norm = Norm(X, KT, True, LN_EPS, column("ln1_g_3", 0), column("ln1_b_3", 0), dst=X, split=(act_hi, act_lo),
                        stats=True)
            ffn_phase("ffn4", "convgelu", norm, taps=conv_taps("w_ffn_dw_3", 0, 22), tap_bias=column("b_ffn_dw_3", 0),
                      alpha=ALPHA)
            normalize(X, KT, True, LN_EPS, column("ln2_g_3", 0), column("ln2_b_3", 0), dst=X, stats=True)

        start()
        if 1 in blocks:
            block1()
        norm = None
        if 2 in blocks:
            norm = block2()
        if 3 in blocks:
            block3(norm)
        elif norm:
            with phase() as block:
                @block.vector
                def _(dve):
                    norm.vector_stats(dve)
                    norm.vector_tiles(dve)

                @block.tensor
                def _(pe):
                    norm.tensor(pe)

                @block.scalar
                def _(act):
                    norm.scalar_stats(act)
                    norm.scalar_tiles(act)
        finish()


_INS = ["x", "c", "w_ada", "b_ada", "w_in", "w_sb_up", "ssm_a_re", "ssm_a_im", "ssm_log_dt", "ssm_b_re", "ssm_b_im",
        "ssm_c_re", "ssm_c_im", "ssm_d", "w_glu", "b_glu", "w_ssm_up", "w_out", "ln1_g", "ln1_b", "w_ffn_in",
        "w_ffn_out", "ln2_g", "ln2_b", "attn_norm_2", "attn_w_in_2", "gla_w_a2_2", "gla_b_a_2", "gla_head_g_2",
        "attn_w_o_2", "sgu_norm_2", "sgu_w_uv_2", "sgu_ln_g_2", "sgu_ln_b_2", "sgu_w_s_2", "sgu_b_s_2", "sgu_w_out_2",
        "ffn_norm_2", "ffn_w_up_2", "ffn_conv_w_2", "ffn_conv_b_2", "ffn_w_down_2", "final_norm_2", "w_in_3",
        "w_conv_dw_3", "b_conv_dw_3", "conv_ln_g_3", "conv_ln_b_3", "w_conv_out_3", "hgrn_lb_logits_3",
        "hgrn_norm_g_3", "w_hgrn_out_3", "w_out_3", "ln1_g_3", "ln1_b_3", "w_ffn_in_3", "w_ffn_dw_3", "b_ffn_dw_3",
        "w_ffn_out_3", "ln2_g_3", "ln2_b_3"]


def kernel(**inputs):
    import numpy as _np
    import concourse.bacc as _bacc
    from concourse import mybir as _mybir
    from concourse.bass_utils import run_bass_kernel_spmd as _run

    nc = _bacc.Bacc("TRN2", target_bir_lowering=False, num_devices=1)
    arrays, args = {"constants": constants()}, {}
    for name in _INS:
        arrays[name] = _np.ascontiguousarray(inputs[name])
    for name, v in arrays.items():
        args[name] = nc.dram_tensor(name, v.shape, _mybir.dt.from_np(v.dtype), kind="ExternalInput").ap()
    out = nc.dram_tensor("out", (1, T, D), F32, kind="ExternalOutput").ap()
    build_program(nc, args, out)
    r = _run(nc, [arrays], core_ids=[0])
    return r.results[0]["out"]
```
